# Optimizing a Trainium2 kernel written in Bass

```python
import jax, jax.numpy as jnp
from jax import lax
import numpy as np

D_MODEL = 1024
BATCH = 1
SEQ = 1024
DEPTH = 2
DEC_BATCH = 8
DEC_SEQ = 4
PAST_LEN = 2048
PAGE_SIZE = 128

N_A = DEPTH // 2
N_B = DEPTH - N_A
POOL_WINDOWS = (2, 4, 8, 16)
N_POOL_GROUPS = len(POOL_WINDOWS)
W_A = 2 * D_MODEL
GW = W_A // N_POOL_GROUPS
POOL_BUF = max(POOL_WINDOWS) - 1
HEAD_DIM = 64
N_HEADS = D_MODEL // HEAD_DIM
W_B = N_HEADS * HEAD_DIM
Q_BLOCK = 128
EPS = 1e-6
NEG = -1e30
F_BIAS_CENTER = 3.0

kernel_name = 'yoco_pool_forgetting_attention_step'

def rmsnorm(x, g):
    x32 = x.astype(jnp.float32)
    y = x32 * lax.rsqrt(jnp.mean(x32 * x32, axis=-1, keepdims=True) + EPS)
    return (y * g.astype(jnp.float32)).astype(x.dtype)

def adaln(c, w, b):
    m = jnp.einsum('bd,de->be', jax.nn.silu(c), w) + b
    shift, scale, gate = jnp.split(m[:, None, :], 3, axis=-1)
    return shift, scale, gate

def pool_mixer(h, hist, start_pos, in_w, grp_w, scale, out_w):
    uz = h @ in_w
    u, z = jnp.split(uz, 2, axis=-1)
    full = jnp.concatenate([hist.astype(u.dtype), u], axis=1)
    p = hist.shape[1]
    n = u.shape[1]
    cs = jnp.cumsum(full.astype(jnp.float32), axis=1)
    cs = jnp.pad(cs, ((0, 0), (1, 0), (0, 0)))
    rows = p + jnp.arange(n)
    avail = start_pos + jnp.arange(n) + 1
    u32 = u.astype(jnp.float32)
    groups = []
    for g, w in enumerate(POOL_WINDOWS):
        sl = slice(g * GW, (g + 1) * GW)
        hi = cs[:, p + 1:, sl]
        lo = jnp.take(cs[:, :, sl], jnp.maximum(rows + 1 - w, 0), axis=1)
        cnt = jnp.minimum(avail, w).astype(jnp.float32)[None, :, None]
        groups.append((hi - lo) / cnt - u32[:, :, sl])
    pooled = jnp.stack(groups, axis=2).astype(u.dtype)
    mixed = jnp.einsum('bngc,gcd->bngd', pooled, grp_w).reshape(u.shape) * scale
    y = (mixed * jax.nn.silu(z)) @ out_w
    return y, full[:, -POOL_BUF:]

def shared_kv(x, kv_g, kv_w, f_b):
    b, n, _ = x.shape
    kvf = rmsnorm(x, kv_g) @ kv_w
    k = kvf[..., :W_B].reshape(b, n, N_HEADS, HEAD_DIM)
    v = kvf[..., W_B:2 * W_B].reshape(b, n, N_HEADS, HEAD_DIM)
    logf = jax.nn.log_sigmoid((kvf[..., 2 * W_B:] + f_b).astype(jnp.float32))
    return k, v, logf

def forget_attend(q, q_idx, k, v, fk, fq):
    s = jnp.einsum('bqhd,bkhd->bhqk', q, k, preferred_element_type=jnp.float32) * (HEAD_DIM ** -0.5)
    s = s + (jnp.transpose(fq, (0, 2, 1))[..., :, None] - jnp.transpose(fk, (0, 2, 1))[..., None, :])
    mask = jnp.arange(k.shape[1])[None, :] <= q_idx[:, None]
    s = jnp.where(mask, s, NEG)
    p = jax.nn.softmax(s, axis=-1)
    return jnp.einsum('bhqk,bkhd->bqhd', p.astype(v.dtype), v)

def prompt_attend(q, k, v, F):
    b, s = q.shape[:2]

    def one(i):
        start = i * Q_BLOCK
        qb = lax.dynamic_slice_in_dim(q, start, Q_BLOCK, axis=1)
        fqb = lax.dynamic_slice_in_dim(F, start, Q_BLOCK, axis=1)
        return forget_attend(qb, start + jnp.arange(Q_BLOCK), k, v, F, fqb)

    out = lax.map(one, jnp.arange(s // Q_BLOCK))
    return jnp.moveaxis(out, 0, 1).reshape(b, s, N_HEADS, HEAD_DIM)

def gather_pages(cache, page_table):
    g = cache[page_table]
    return g.reshape((g.shape[0], g.shape[1] * g.shape[2]) + g.shape[3:])

def trunk(x, c, pool_hist, start_pos, past, ada_w, ada_b, pre_g, post_g,
          a_in_w, a_grp_w, a_scale, a_out_w, kv_g, kv_w, f_b, b_in_w, b_out_w):
    new_pool = []
    k_new = v_new = logf_new = None
    for l in range(DEPTH):
        shift, scale, gate = adaln(c, ada_w[l], ada_b[l])
        h = rmsnorm(x, pre_g[l]) * (1 + scale) + shift
        if l < N_A:
            out, hist = pool_mixer(h, pool_hist[l], start_pos, a_in_w[l], a_grp_w[l], a_scale[l], a_out_w[l])
            new_pool.append(hist)
        else:
            if l == N_A:
                k_new, v_new, logf_new = shared_kv(x, kv_g, kv_w, f_b)
                if past is None:
                    k_all, v_all, lf_all = k_new, v_new, logf_new
                else:
                    k_all = jnp.concatenate([past[0].astype(k_new.dtype), k_new], axis=1)
                    v_all = jnp.concatenate([past[1].astype(v_new.dtype), v_new], axis=1)
                    lf_all = jnp.concatenate([past[2].astype(jnp.float32), logf_new], axis=1)
                F_all = jnp.cumsum(lf_all, axis=1)
                n_past = k_all.shape[1] - x.shape[1]
            j = l - N_A
            bsz, n, _ = h.shape
            qz = h @ b_in_w[j]
            q = qz[..., :W_B].reshape(bsz, n, N_HEADS, HEAD_DIM)
            zg = qz[..., W_B:]
            if past is None:
                o = prompt_attend(q, k_all, v_all, F_all)
            else:
                o = forget_attend(q, n_past + jnp.arange(n), k_all, v_all, F_all, F_all[:, n_past:])
            o = o.reshape(bsz, n, W_B).astype(h.dtype)
            out = (o * jax.nn.silu(zg)) @ b_out_w[j]
        x = x + gate * rmsnorm(out, post_g[l])
    return x, jnp.stack(new_pool, axis=0), k_new, v_new, logf_new

def setup_inputs(seed: int = 0) -> dict:
    key = jax.random.key(seed)
    ks = jax.random.split(key, 24)
    f32 = jnp.float32
    n_pages = PAST_LEN // PAGE_SIZE
    n_used = DEC_BATCH * n_pages
    n_phys = n_used + n_used // 4
    nrm = lambda k, s, sc: jax.random.normal(k, s, f32) * sc
    page_table = jax.random.permutation(ks[0], n_phys)[:n_used].reshape(DEC_BATCH, n_pages).astype(jnp.int32)
    kv_w = jnp.concatenate([
        nrm(ks[1], (D_MODEL, 2 * W_B), D_MODEL ** -0.5),
        nrm(ks[2], (D_MODEL, N_HEADS), 0.1 * D_MODEL ** -0.5)], axis=1)
    return {
        'x_prompt': nrm(ks[3], (BATCH, SEQ, D_MODEL), 1.0),
        'x_sample': nrm(ks[4], (DEC_BATCH, DEC_SEQ, D_MODEL), 1.0),
        'state_pool': nrm(ks[5], (N_A, DEC_BATCH, POOL_BUF, W_A), 1.0),
        'cache_k': nrm(ks[6], (n_phys, PAGE_SIZE, N_HEADS, HEAD_DIM), 1.0),
        'cache_v': nrm(ks[7], (n_phys, PAGE_SIZE, N_HEADS, HEAD_DIM), 1.0),
        'cache_logf': jax.nn.log_sigmoid(F_BIAS_CENTER + nrm(ks[8], (n_phys, PAGE_SIZE, N_HEADS), 0.5)),
        'page_table': page_table,
        'c_prompt': nrm(ks[9], (BATCH, D_MODEL), 1.0),
        'c_sample': nrm(ks[10], (DEC_BATCH, D_MODEL), 1.0),
        'ada_w': nrm(ks[11], (DEPTH, D_MODEL, 3 * D_MODEL), 0.5 * D_MODEL ** -0.5),
        'ada_b': nrm(ks[12], (DEPTH, 3 * D_MODEL), 0.02),
        'pre_g': 1.0 + nrm(ks[13], (DEPTH, D_MODEL), 0.05),
        'post_g': 1.0 + nrm(ks[14], (DEPTH, D_MODEL), 0.05),
        'a_in_w': nrm(ks[15], (N_A, D_MODEL, 2 * W_A), D_MODEL ** -0.5),
        'a_grp_w': nrm(ks[16], (N_A, N_POOL_GROUPS, GW, GW), GW ** -0.5),
        'a_scale': 1.0 + nrm(ks[17], (N_A, W_A), 0.1),
        'a_out_w': nrm(ks[18], (N_A, W_A, D_MODEL), W_A ** -0.5),
        'kv_g': 1.0 + nrm(ks[19], (D_MODEL,), 0.05),
        'kv_w': kv_w,
        'f_b': F_BIAS_CENTER + nrm(ks[20], (N_HEADS,), 0.5),
        'b_in_w': nrm(ks[21], (N_B, D_MODEL, 2 * W_B), D_MODEL ** -0.5),
        'b_out_w': nrm(ks[22], (N_B, W_B, D_MODEL), W_B ** -0.5),
    }

def reference(x_prompt, x_sample, state_pool, cache_k, cache_v, cache_logf, page_table,
              c_prompt, c_sample, ada_w, ada_b, pre_g, post_g, a_in_w, a_grp_w, a_scale,
              a_out_w, kv_g, kv_w, f_b, b_in_w, b_out_w):
    weights = (ada_w, ada_b, pre_g, post_g, a_in_w, a_grp_w, a_scale, a_out_w, kv_g, kv_w, f_b, b_in_w, b_out_w)
    empty_hist = [jnp.zeros((x_prompt.shape[0], 0, W_A), x_prompt.dtype)] * N_A
    y_prompt, pool_prompt, k_prompt, v_prompt, logf_prompt = trunk(
        x_prompt, c_prompt, empty_hist, 0, None, *weights)
    n_past = page_table.shape[1] * cache_k.shape[1]
    past = (gather_pages(cache_k, page_table), gather_pages(cache_v, page_table),
            gather_pages(cache_logf, page_table))
    y_sample, pool_sample, k_sample, v_sample, logf_sample = trunk(
        x_sample, c_sample, state_pool, n_past, past, *weights)
    return (y_prompt, y_sample, pool_prompt, pool_sample, k_prompt, v_prompt, logf_prompt,
            k_sample, v_sample, logf_sample)


_drawn_inputs = setup_inputs


def setup_inputs(seed=0):
    import zlib

    import numpy as np

    out = dict(_drawn_inputs(seed))
    spreads = {}
    factors = {'cache_logf': 3.233, 'post_g': 2.787}
    for name, (base, spread) in spreads.items():
        noise = np.random.default_rng([zlib.crc32(name.encode()), seed]).standard_normal(out[name].shape)
        drawn = base * np.exp(spread * noise) if base else spread * noise
        out[name] = __import__('jax').numpy.asarray(drawn.astype(out[name].dtype))
    for name, factor in factors.items():
        out[name] = (out[name] * factor).astype(out[name].dtype)
    return out
```

```python
from contextlib import ExitStack

import concourse.bass as bass
from concourse import mybir

ALU = mybir.AluOpType
ACT = mybir.ActivationFunctionType
AX_X = mybir.AxisListType.X
F32 = mybir.dt.float32
F32R = mybir.dt.float32r
I32 = mybir.dt.int32

P = 128
D = 1024
KD = D // P
SEQ = 1024
QB = SEQ // P
NB = 8
NT = 4
NS = NB * NT
T = SEQ + NS
TT = QB + 1
NCH = 3
CH = T // NCH
W_A = 2 * D
KA = W_A // P
WINDOWS = (2, 4, 8, 16)
NG = len(WINDOWS)
GT = KA // NG
HIST = max(WINDOWS) - 1
SEG = HIST + NT
UW = HIST + SEQ + NB * SEG
NCOND = 1 + NB
NH = 16
HD = 64
NP = NH // 2
PAGE = 128
NPG = 16
PAST = NPG * PAGE
NR = NH * NT
EPS = 1e-6
NEG = -1e30
BANK = 512
RAW = 2
SPL = 2


def rows_of(i):
    return P if i < QB else NS


def stream_weights(sp, w, jobs):
    for j, src in enumerate(jobs):
        if j >= RAW:
            sp.wait_ge(w["split"], j - RAW + 1)
        sp.dma_start(w["raw"][:, j % RAW, 0:src.shape[1], 0:src.shape[2]], src).then_inc(
            w["landed"][j % RAW], 16)


def split_weights(pool, w, jobs):
    for j, src in enumerate(jobs):
        kt = src.shape[1]
        raw, hi, lo = (w[n][:, j % r, 0:kt, :] for n, r in (("raw", RAW), ("hi", SPL), ("lo", SPL)))
        pool.wait_ge(w["landed"][j % RAW], 16 * (j // RAW + 1))
        if j >= SPL:
            pool.wait_ge(w["used"], j - SPL + 1)
        pool.tensor_copy(hi, raw).then_inc(w["hi_ready"], 1)
        pool.wait_ge(w["hi_ready"], j + 1)
        pool.tensor_tensor(lo, raw, hi.bitcast(F32), ALU.subtract).then_inc(w["split"], 1)


def product(pe, w, j, kt, acc, act_hi, act_lo, k0, first=True, last=True):
    pe.wait_ge(w["split"], j + 1)
    hi, lo = w["hi"], w["lo"]
    for k in range(kt):
        for s, (wt, act) in enumerate(((hi, act_hi), (hi, act_lo), (lo, act_hi))):
            for c in range(NCH):
                mm = pe.matmul(acc[:, c, 0:CH], wt[:, j % SPL, k, :], act[:, k0 + k, c * CH:(c + 1) * CH],
                               start=first and k == 0 and s == 0, stop=last and k == kt - 1 and s == 2)
    mm.then_inc(w["used"], 1)


def thirds(acc):
    return acc[:, :, 0:CH]


def as_thirds(ap):
    return ap.rearrange("p (c t) -> p c t", c=NCH)


def build(nc, x_prompt, x_sample, state_pool, cache_k, cache_v, cache_logf, page_table, c_prompt,
          c_sample, ada_w, ada_b, pre_g, post_g, a_in_w, a_grp_w, a_scale, a_out_w, kv_g, kv_w,
          f_b, b_in_w, b_out_w, y_prompt, y_sample, pool_prompt, pool_sample, k_prompt, v_prompt,
          logf_prompt, k_sample, v_sample, logf_sample):
    ctx = ExitStack()
    n_phys = cache_k.shape[0]
    base = (nc.sbuf_base + 31) // 32 * 32
    top = nc.sbuf_usable_end
    size = {F32: 4, F32R: 4, I32: 4}

    class Arena:

        def __init__(self, at):
            self.at = at

        def take(self, name, shape, dt=F32):
            n = size[dt]
            for d in shape[1:]:
                n *= d
            t = nc.alloc_sbuf_tensor_at(name, shape, dt, offset=self.at)
            self.at = (self.at + n + 31) // 32 * 32
            assert self.at <= top, (name, self.at - top)
            return t

    stage_sems = []

    def sem(name):
        stage_sems.append(nc.alloc_semaphore(name))
        return stage_sems[-1]

    s_pout = [nc.alloc_semaphore(f"s_pout{i}") for i in range(2)]
    s_tout = [nc.alloc_semaphore(f"s_tout{i}") for i in range(2)]
    s_lout = nc.alloc_semaphore("s_lout")
    s_xout = [nc.alloc_semaphore(f"s_xout{i}") for i in range(2)]

    def end_stage():
        nc.clear_and_free_semaphores(list(stage_sems))
        stage_sems.clear()
        nc.all_engine_barrier()

    def scratch(name, shape):
        return nc.dram_tensor(name, shape, F32, kind="Internal").ap()

    gate_d = scratch("gate_d", (2, NCOND, D))
    g_d = scratch("g_d", (KA, P, T))
    x1_d = scratch("x1_d", (TT, P, D))
    qT_d = scratch("qT_d", (NP, P, T))
    kT_d = scratch("kT_d", (NP, P, T))
    zT_d = scratch("zT_d", (NP, P, T))
    negF_d = scratch("negF_d", (NH, SEQ))

    x_p = x_prompt.rearrange("a (t p) d -> p (a t) d", p=P)
    x_s = x_sample.rearrange("b t d -> (b t) d")
    yp = y_prompt.rearrange("a (t p) d -> p (a t) d", p=P)
    ys = y_sample.rearrange("b t d -> (b t) d")
    kp = k_prompt.rearrange("a (t p) h d -> p (a t) (h d)", p=P)
    vp = v_prompt.rearrange("a (t p) h d -> p (a t) (h d)", p=P)
    ks = k_sample.rearrange("b t h d -> (b t) (h d)")
    vs = v_sample.rearrange("b t h d -> (b t) (h d)")
    lfp = logf_prompt.rearrange("a (t p) h -> p (a t) h", p=P)
    lfs = logf_sample.rearrange("b t h -> (b t) h")

    def w_tiles(mat, k0, kt, n0, n):
        return mat[k0 * P:(k0 + kt) * P, n0:n0 + n].rearrange("(k p) n -> p k n", p=P)

    keep = Arena(base)
    ident = keep.take("ident", [P, P])
    modA = keep.take("modA", [P, 2, KD, NCOND])
    modB = keep.take("modB", [P, 2, KD, NCOND])
    kvg = keep.take("kvg", [P, KD])
    asc = keep.take("asc", [P, KA])
    sel_p = keep.take("sel_p", [NCOND, P])
    sel_s = keep.take("sel_s", [NCOND, NS])
    Ftok = keep.take("Ftok", [P, QB, NH])
    lf_s = keep.take("lf_s", [NS, NH])
    act_at = keep.at
    actH = keep.take("actH", [P, KA, T], F32R)
    actL_at = keep.at
    actL = keep.take("actL", [P, KA, T], F32R)
    free = keep.at

    ps = ctx.enter_context(nc.psum_tensor("ps", [P, 8, BANK], F32))
    acc = [ps[:, 0:3, :], ps[:, 3:6, :]]

    def weight_ring(tag, arena):
        return {
            "raw": arena.take(f"w_raw_{tag}", [P, RAW, KD, P]),
            "hi": arena.take(f"w_hi_{tag}", [P, SPL, KD, P], F32R),
            "lo": arena.take(f"w_lo_{tag}", [P, SPL, KD, P], F32R),
            "landed": [sem(f"w_landed_{tag}{i}") for i in range(RAW)],
            "hi_ready": sem(f"w_hi_ready_{tag}"),
            "split": sem(f"w_split_{tag}"),
            "used": sem(f"w_used_{tag}"),
        }

    def chainer(name):
        s, n = sem(name), [0]

        def link(eng, ins):
            n[0] += 1
            ins.then_inc(s, 1)
            eng.wait_ge(s, n[0])
        return link

    def b_t(ap):
        return ap[:, :, 1:NCOND].unsqueeze(3).broadcast_to([P, KD, NB, NT])

    class NormedTranspose:

        BANKS = 4
        TMP = 4

        def __init__(self, tag, targets, tmp):
            self.targets, self.tmp = targets, tmp
            self.turned = sem(f"turned_{tag}")
            self.high = sem(f"high_{tag}")
            self.low = sem(f"low_{tag}")
            self.full = sem(f"full_{tag}")
            self.rounds = [(g, k) for g in range(QB // 4) for k in range(KD)]

        def pe(self, pe, x_tok, x_ready, x_count):
            nt = len(self.targets)
            for n, (g, k) in enumerate(self.rounds):
                pe.wait_ge(x_ready, x_count(4 * g + 3))
                if n >= self.BANKS:
                    pe.wait_ge(self.full, nt * (n - self.BANKS + 1))
                for i in range(4):
                    mm = pe.transpose(ps[:, n % self.BANKS, i * P:(i + 1) * P],
                                      x_tok[:, 4 * g + i, k * P:(k + 1) * P], ident[:, :])
                mm.then_inc(self.turned, 1)
            n = len(self.rounds)
            pe.wait_ge(x_ready, x_count(QB))
            pe.wait_ge(self.full, nt * (n - self.BANKS + 1))
            for k in range(KD):
                mm = pe.transpose(ps[:, n % self.BANKS, k * NS:(k + 1) * NS],
                                  x_tok[0:NS, QB, k * P:(k + 1) * P], ident[0:NS, 0:NS])
            mm.then_inc(self.turned, 1)

        def act(self, act):
            m = 0
            for g, k in self.rounds:
                for k0, A, B in self.targets:
                    act.wait_ge(self.full, m + 1)
                    act.copy(actH[:, k0 + k, g * BANK:(g + 1) * BANK], self.tmp[:, m % self.TMP, :]).then_inc(self.high, 1)
                    m += 1

        def dve(self, dve, link):
            tmp, m = self.tmp, 0

            def low(m, k0, g, k):
                cols = slice(g * BANK, (g + 1) * BANK)
                dve.wait_ge(self.high, m + 1)
                dve.tensor_tensor(actL[:, k0 + k, cols], tmp[:, m % self.TMP, :],
                                  actH[:, k0 + k, cols].bitcast(F32), ALU.subtract).then_inc(self.low, 1)

            behind = []
            for n, (g, k) in enumerate(self.rounds):
                dve.wait_ge(self.turned, n + 1)
                for k0, A, B in self.targets:
                    src, t = ps[:, n % self.BANKS, :], tmp[:, m % self.TMP, :]
                    if m >= self.TMP:
                        dve.wait_ge(self.low, m - self.TMP + 1)
                    if B is not None:
                        ins = dve.tensor_scalar(t, src, A[:, k, 0:1], B[:, k, 0:1], ALU.mult, ALU.add)
                    else:
                        ins = dve.tensor_scalar(t, src, A[:, k:k + 1], None, ALU.mult)
                    ins.then_inc(self.full, 1)
                    behind.append((m, k0, g, k))
                    m += 1
                    if len(behind) > 2:
                        low(*behind.pop(0))
            for b in behind:
                low(*b)
            dve.wait_ge(self.low, m)
            n = len(self.rounds)
            dve.wait_ge(self.turned, n + 1)
            src = ps[:, n % self.BANKS, 0:KD * NS]
            t = tmp[:, 0, 0:KD * NS]
            for k0, A, B in self.targets:
                hi, lo = (x[:, k0:k0 + KD, SEQ:T] for x in (actH, actL))
                v = t.rearrange("p (k b t) -> p k b t", k=KD, b=NB)
                s4 = src.rearrange("p (k b t) -> p k b t", k=KD, b=NB)
                for k in range(KD):
                    if B is not None:
                        bc = A[:, k, 1:NCOND].unsqueeze(2).broadcast_to([P, NB, NT])
                        link(dve, dve.tensor_tensor(v[:, k], s4[:, k], bc, ALU.mult))
                        bc = B[:, k, 1:NCOND].unsqueeze(2).broadcast_to([P, NB, NT])
                        link(dve, dve.tensor_tensor(v[:, k], v[:, k], bc, ALU.add))
                    else:
                        link(dve, dve.tensor_scalar(v[:, k], s4[:, k], A[:, k:k + 1], None, ALU.mult))
                t3 = t.rearrange("p (k n) -> p k n", k=KD)
                link(dve, dve.tensor_copy(hi, t3))
                link(dve, dve.tensor_tensor(lo, t3, hi.bitcast(F32), ALU.subtract))

    def stage_conditioning():
        a = Arena(free)
        crow = a.take("crow", [NCOND, D])
        srow = a.take("srow", [NCOND, D])
        scT = a.take("scT", [P, KD, NCOND])
        adab = a.take("adab", [NCOND, 2, BANK])
        mrow = a.take("mrow", [NCOND, 2, BANK])
        preg = a.take("preg", [P, 2, KD])
        x_tok = a.take("x_tok1", [P, TT, D])
        junk = a.take("junk1", [P, D])
        ss = a.take("ss1", [P, TT])
        rstd = a.take("rstd1", [P, TT])
        tmp = a.take("tmp1", [P, 4, BANK])
        adaw = Arena(actL_at + KD * T * 4).take("adaw", [P, 2, KD, BANK])

        chunks = [(l, n) for l in range(2) for n in range(3 * D // BANK)]
        s_c, s_small, s_x = sem("s_c"), sem("s_small"), sem("s_x")
        s_aw = [sem(f"s_aw{i}") for i in range(2)]
        s_ab = [sem(f"s_ab{i}") for i in range(2)]
        s_gate = [sem(f"s_gate{i}") for i in range(2)]
        s_const, s_id = sem("s_const"), sem("s_id")
        s_silu, s_cT, s_scT = sem("s_silu"), sem("s_cT"), sem("s_scT")
        s_m, s_mrow, s_mT, s_mod = sem("s_m"), sem("s_mrow"), sem("s_mT"), sem("s_mod")
        s_ss_init = sem("s_ss_init")
        s_ss, s_var, s_std, s_xn = sem("s_ss"), sem("s_var"), sem("s_std"), sem("s_xn")
        link = chainer("dve_chain1")
        alink = chainer("act_chain1")
        normed = NormedTranspose("l0", [(0, modA[:, 0], modB[:, 0])], tmp)
        GATE = 2 * D // BANK

        with nc.Block() as block:
            @block.sync
            def _(sp):
                sp.dma_start(crow[0:1, :], c_prompt).then_inc(s_c, 16)
                sp.dma_start(crow[1:NCOND, :], c_sample).then_inc(s_c, 16)
                with nc.allow_non_contiguous_dma(reason="small per-channel vectors"):
                    sp.dma_start(preg[:, :, :], pre_g.rearrange("l (k p) -> p l k", p=P)).then_inc(s_small, 16)
                    sp.dma_start(kvg[:, :], kv_g.rearrange("(k p) -> p k", p=P)).then_inc(s_small, 16)
                    sp.dma_start(asc[:, :], a_scale.rearrange("a (k p) -> p (a k)", p=P)).then_inc(s_small, 16)
                for j, (l, n) in enumerate(chunks):
                    if j >= 2:
                        sp.wait_ge(s_m, j - 1)
                        sp.wait_ge(s_mrow, j - 1)
                    sp.dma_start(adaw[:, j % 2], w_tiles(ada_w[l], 0, KD, n * BANK, BANK)).then_inc(s_aw[j % 2], 16)
                    sp.dma_start(adab[:, j % 2], ada_b[l:l + 1, n * BANK:(n + 1) * BANK].broadcast_to(
                        [NCOND, BANK])).then_inc(s_ab[j % 2], 16)
                    if j == 1:
                        sp.dma_start(x_tok[:, 0:QB, :], x_p).then_inc(s_x, 16)
                        sp.dma_start(x_tok[0:NS, QB, :], x_s).then_inc(s_x, 16)

            @block.gpsimd
            def _(pool):
                pool.memset(ident[:, :], 0.0).then_inc(s_id, 1)
                pool.memset(sel_p[:, :], 1.0).then_inc(s_id, 1)
                pool.memset(sel_s[:, :], 1.0).then_inc(s_id, 1)
                pool.wait_ge(s_id, 3)
                pool.affine_select(out=ident[:, :], in_=ident[:, :], compare_op=ALU.not_equal, fill=1.0,
                                   base=0, pattern=[[-1, P]], channel_multiplier=1).then_inc(s_const, 1)
                pool.affine_select(out=sel_p[:, :], in_=sel_p[:, :], compare_op=ALU.is_ge, fill=0.0,
                                   base=0, pattern=[[0, P]], channel_multiplier=-1).then_inc(s_const, 1)
                pool.affine_select(out=sel_s[:, :], in_=sel_s[:, :], compare_op=ALU.is_ge, fill=0.0,
                                   base=NT, pattern=[[1, NS]], channel_multiplier=-NT).then_inc(s_id, 1)
                pool.wait_ge(s_id, 4)
                pool.affine_select(out=sel_s[:, :], in_=sel_s[:, :], compare_op=ALU.is_ge, fill=0.0,
                                   base=-1, pattern=[[-1, NS]], channel_multiplier=NT).then_inc(s_const, 1)
                for j, (l, n) in enumerate(chunks):
                    if n >= GATE:
                        pool.wait_ge(s_mrow, j + 1)
                        pool.dma_start(gate_d[l, :, (n - GATE) * BANK:(n - GATE + 1) * BANK],
                                       mrow[:, j % 2]).then_inc(s_gate[j % 2], 16)
                pool.wait_ge(s_gate[0], 32)
                pool.wait_ge(s_gate[1], 32)

            @block.scalar
            def _(act):
                act.wait_ge(s_c, 32)
                act.activation(srow[:, :], crow[:, :], ACT.Silu).then_inc(s_silu, 1)
                act.wait_ge(s_x, 32)
                act.wait_ge(s_ss_init, 1)
                for i in range(TT):
                    r = rows_of(i)
                    if i:
                        act.wait_ge(s_ss, i)
                    act.activation(junk[0:r, :], x_tok[0:r, i, :], ACT.Square,
                                   accum_out=ss[0:r, i:i + 1]).then_inc(s_ss, 1)
                act.wait_ge(s_var, 1)
                act.activation(rstd[:, :], rstd[:, :], ACT.Sqrt).then_inc(s_std, 1)
                normed.act(act)

            @block.tensor
            def _(pe):
                pe.wait_ge(s_silu, 1)
                pe.wait_ge(s_const, 3)
                for k in range(KD):
                    mm = pe.transpose(ps[:, 4, k * NCOND:(k + 1) * NCOND], srow[:, k * P:(k + 1) * P],
                                      ident[0:NCOND, 0:NCOND])
                mm.then_inc(s_cT, 1)
                pe.wait_ge(s_scT, 1)

                turned = 0
                for j, (l, n) in enumerate(chunks):
                    pe.wait_ge(s_aw[j % 2], 16 * (j // 2 + 1))
                    if j >= 2:
                        pe.wait_ge(s_mrow, j - 1)
                    for k in range(KD):
                        mm = pe.matmul(ps[0:NCOND, 6 + j % 2, :], scT[:, k, :], adaw[:, j % 2, k, :],
                                       start=(k == 0), stop=(k == KD - 1))
                    mm.then_inc(s_m, 1)
                    if n < GATE:
                        pe.wait_ge(s_mrow, j + 1)
                        if turned:
                            pe.wait_ge(s_mod, turned)
                        for i in range(BANK // P):
                            mm = pe.transpose(ps[:, 5, i * NCOND:(i + 1) * NCOND],
                                              mrow[:, j % 2, i * P:(i + 1) * P], ident[0:NCOND, 0:NCOND])
                        mm.then_inc(s_mT, 1)
                        turned += 1
                normed.pe(pe, x_tok, s_xn, lambda i: i + 1)

            @block.vector
            def _(dve):
                dve.memset(ss[:, :], 1.0).then_inc(s_ss_init, 1)
                dve.wait_ge(s_cT, 1)
                dve.tensor_copy(scT[:, :, :], ps[:, 4, 0:KD * NCOND].rearrange("p (k c) -> p k c", k=KD)).then_inc(s_scT, 1)
                turned = 0
                gates = [0, 0]
                for j, (l, n) in enumerate(chunks):
                    dve.wait_ge(s_m, j + 1)
                    dve.wait_ge(s_ab[j % 2], 16 * (j // 2 + 1))
                    if gates[j % 2]:
                        dve.wait_ge(s_gate[j % 2], 16 * gates[j % 2])
                    if turned:
                        dve.wait_ge(s_mT, turned)
                    dve.tensor_tensor(mrow[:, j % 2], ps[0:NCOND, 6 + j % 2, :], adab[:, j % 2], ALU.add).then_inc(s_mrow, 1)
                    if n >= GATE:
                        gates[j % 2] += 1
                        continue
                    turned += 1
                    dve.wait_ge(s_mT, turned)
                    for i in range(BANK // P):
                        k = (n % 2) * (BANK // P) + i
                        src = ps[:, 5, i * NCOND:(i + 1) * NCOND]
                        if n < D // BANK:
                            ins = dve.tensor_copy(modB[:, l, k, :], src)
                        else:
                            if turned == 3 and i == 0:
                                dve.wait_ge(s_small, 48)
                            ins = dve.tensor_scalar(modA[:, l, k, :], src, 1.0, preg[:, l, k:k + 1], ALU.add, ALU.mult)
                    ins.then_inc(s_mod, 1)
                dve.wait_ge(s_ss, TT)
                dve.tensor_scalar(rstd[:, :], ss[:, :], 1.0 / D, EPS, ALU.mult, ALU.add).then_inc(s_var, 1)
                dve.wait_ge(s_std, 1)
                link(dve, dve.reciprocal(rstd[:, :], rstd[:, :]))
                for i in range(TT):
                    r = rows_of(i)
                    dve.tensor_scalar(x_tok[0:r, i, :], x_tok[0:r, i, :], rstd[0:r, i:i + 1], None,
                                      ALU.mult).then_inc(s_xn, 1)
                dve.wait_ge(s_mod, turned)
                normed.dve(dve, link)

    def stage_pooling():
        a = Arena(free)
        w = weight_ring("a", a)
        U = a.take("U", [P, 2, UW])
        win = a.take("win", [P, 2, UW])
        pooled = a.take("pooled", [P, T])
        sz = a.take("sz", [P, 2, T])
        g = a.take("g", [P, 2, T])
        hist = Arena(actL_at + (KD + GT) * T * 4).take("hist", [NB * HIST, W_A])
        pk = a.take("pk", [P, 2, HIST + NB * HIST])
        po_p = a.take("po_p", [HIST, 2, P])
        po_s = a.take("po_s", [NB * HIST, 2, P])
        inv = a.take("inv", [P, HIST])

        PH = KD
        jobs, kinds = [], []
        for gr in range(NG):
            c0 = gr * GT * P
            for i in range(GT):
                jobs.append(w_tiles(a_in_w[0], 0, KD, c0 + i * P, P))
                kinds.append(("u", gr, i))
            for i0 in range(0, GT, 2):
                for i in (i0, i0 + 1):
                    jobs.append(w_tiles(a_in_w[0], 0, KD, W_A + c0 + i * P, P))
                    kinds.append(("z", gr, i))
                for i in (i0, i0 + 1):
                    jobs.append(w_tiles(a_grp_w[0, gr], 0, GT, i * P, P))
                    kinds.append(("m", gr, i))

        s_hist, s_inv, s_pad = sem("s_hist"), sem("s_inv"), sem("s_pad")
        s_hT, s_hU = sem("s_hT"), sem("s_hU")
        s_U = sem("s_U")
        s_pooled, s_ph, s_pl = sem("s_pooled"), sem("s_ph"), sem("s_pl")
        s_pk, s_pkT, s_pkfree = sem("s_pk"), sem("s_pkT"), sem("s_po")
        s_sz, s_g = sem("s_sz"), sem("s_g")
        s_gout = [sem(f"s_gout{i}") for i in range(2)]
        link = chainer("dve_chain2")
        U_s = [U[:, i, HIST + SEQ:UW].rearrange("p (b s) -> p b s", s=SEG) for i in range(2)]
        W_s = [win[:, i, HIST + SEQ:UW].rearrange("p (b s) -> p b s", s=SEG) for i in range(2)]

        with nc.Block() as block:
            @block.sync
            def _(sp):
                sp.dma_start(hist[:, :], state_pool[0].rearrange("b r c -> (b r) c")).then_inc(s_hist, 16)
                stream_weights(sp, w, jobs)

            @block.gpsimd
            def _(pool):
                for t in range(HIST):
                    pool.memset(inv[:, t:t + 1], 1.0 / (t + 1)).then_inc(s_inv, 1)
                for i in range(2):
                    pool.memset(U[:, i, 0:HIST], 0.0).then_inc(s_pad, 1)
                    pool.memset(win[:, i, :], 0.0).then_inc(s_pad, 1)
                split_weights(pool, w, jobs)

            @block.tensor
            def _(pe):
                def finish_tile(j):
                    pe.wait_ge(s_pk, j + 1)
                    if j:
                        pe.wait_ge(s_pkfree, 2 * j)
                    pe.transpose(ps[0:HIST, 7, 0:P], pk[:, j % 2, 0:HIST], ident[:, :])
                    pe.transpose(ps[0:NB * HIST, 7, P:2 * P], pk[:, j % 2, HIST:], ident[:, :]).then_inc(s_pkT, 1)

                pe.wait_ge(s_hist, 16)
                late = None
                for n, (kind, gr, i) in enumerate(kinds):
                    j = gr * GT + i
                    if kind == "u":
                        if j:
                            pe.wait_ge(s_hU, j)
                        pe.transpose(ps[:, 6, 0:NB * HIST], hist[:, j * P:(j + 1) * P],
                                     ident[0:NB * HIST, 0:NB * HIST]).then_inc(s_hT, 1)
                    if n >= 2:
                        was, gw, iw = kinds[n - 2]
                        pe.wait_ge({"u": s_U, "z": s_sz, "m": s_g}[was], gw * GT + iw + 1)
                    if kind == "m":
                        pe.wait_ge(s_pl, (gr + 1) * GT)
                        product(pe, w, n, GT, acc[n % 2], actH, actL, PH)
                    else:
                        product(pe, w, n, KD, acc[n % 2], actH, actL, 0)
                    if late is not None:
                        finish_tile(late)
                    late = j if kind == "u" else None

            @block.scalar
            def _(act):
                late_u, late_g = [], []

                def finish_tile(j):
                    act.wait_ge(s_pkT, j + 1)
                    if j >= 2:
                        act.wait_ge(s_pout[j % 2], 32 * (j // 2))
                    act.copy(po_p[:, j % 2], ps[0:HIST, 7, 0:P]).then_inc(s_pkfree, 1)
                    act.copy(po_s[:, j % 2], ps[0:NB * HIST, 7, P:2 * P]).then_inc(s_pkfree, 1)
                    act.wait_ge(s_pkfree, 2 * (j + 1))
                    c = slice(j * P, (j + 1) * P)
                    act.dma_start(pool_prompt[0, 0, :, c], po_p[:, j % 2]).then_inc(s_pout[j % 2], 16)
                    act.dma_start(pool_sample[0].rearrange("b r c -> (b r) c")[:, c],
                                  po_s[:, j % 2]).then_inc(s_pout[j % 2], 16)

                def store_g(j):
                    act.wait_ge(s_g, j + 1)
                    act.dma_start(g_d[j], g[:, j % 2]).then_inc(s_gout[j % 2], 16)

                for n, (kind, gr, i) in enumerate(kinds):
                    j = gr * GT + i
                    A = acc[n % 2]
                    if kind == "m":
                        late_g.append(j)
                        continue
                    act.wait_ge(w["used"], n + 1)
                    if kind == "u":
                        if j < 2:
                            act.wait_ge(s_pad, 4)
                        else:
                            act.wait_ge(s_pk, j - 1)
                        act.copy(U[:, j % 2, HIST:HIST + 2 * CH].rearrange("p (c t) -> p c t", c=2),
                                 A[:, 0:2, 0:CH])
                        act.copy(U[:, j % 2, HIST + 2 * CH:HIST + SEQ], A[:, 2, 0:SEQ - 2 * CH])
                        act.copy(U_s[j % 2][:, :, HIST:SEG],
                                 A[:, 2, SEQ - 2 * CH:CH].rearrange("p (b t) -> p b t", b=NB)).then_inc(s_U, 1)
                        act.wait_ge(s_pooled, j + 1)
                        act.copy(actH[:, PH + i, :], pooled[:, :]).then_inc(s_ph, 1)
                        late_u.append(j)
                    else:
                        if j >= 2:
                            act.wait_ge(s_g, j - 1)
                        act.activation(as_thirds(sz[:, j % 2]), thirds(A), ACT.Silu).then_inc(s_sz, 1)
                    while late_u and (late_u[0] < j or kind != "u"):
                        finish_tile(late_u.pop(0))
                    while late_g and late_g[0] < j - 1:
                        store_g(late_g.pop(0))
                for j in late_g:
                    store_g(j)
                for i in range(2):
                    act.wait_ge(s_gout[i], 16 * KA // 2)
                    act.wait_ge(s_pout[i], 32 * KA // 2)

            @block.vector
            def _(dve):
                dve.wait_ge(s_inv, HIST)
                dve.wait_ge(s_pad, 4)
                for n, (kind, gr, i) in enumerate(kinds):
                    j = gr * GT + i
                    u = U[:, j % 2]
                    if kind == "u":
                        size_w = WINDOWS[gr]
                        dve.wait_ge(s_hT, j + 1)
                        dve.tensor_copy(U_s[j % 2][:, :, 0:HIST],
                                        ps[:, 6, 0:NB * HIST].rearrange("p (b r) -> p b r", b=NB)).then_inc(s_hU, 1)
                        dve.wait_ge(s_hU, j + 1)
                        dve.wait_ge(s_U, j + 1)
                        src, step, at = u, 1, 0
                        while step < size_w:
                            lo = 2 * step - 1
                            link(dve, dve.tensor_tensor(win[:, at, lo:UW], src[:, lo:UW], src[:, lo - step:UW - step], ALU.add))
                            src, ws, at, step = win[:, at], W_s[at], 1 - at, 2 * step
                        if j:
                            dve.wait_ge(s_ph, j)
                            dve.wait_ge(s_pl, j)
                        link(dve, dve.scalar_tensor_tensor(
                            out=pooled[:, 0:SEQ], in0=src[:, HIST:HIST + SEQ], scalar=1.0 / size_w,
                            in1=u[:, HIST:HIST + SEQ], op0=ALU.mult, op1=ALU.subtract))
                        cut = size_w - 1
                        link(dve, dve.tensor_tensor(pooled[:, 0:cut], src[:, HIST:HIST + cut], inv[:, 0:cut], ALU.mult))
                        link(dve, dve.tensor_tensor(pooled[:, 0:cut], pooled[:, 0:cut], u[:, HIST:HIST + cut], ALU.subtract))
                        dve.scalar_tensor_tensor(
                            out=pooled[:, SEQ:T].rearrange("p (b t) -> p b t", b=NB), in0=ws[:, :, HIST:SEG],
                            scalar=1.0 / size_w, in1=U_s[j % 2][:, :, HIST:SEG], op0=ALU.mult,
                            op1=ALU.subtract).then_inc(s_pooled, 1)
                        if j >= 2:
                            dve.wait_ge(s_pkT, j - 1)
                        dve.tensor_copy(pk[:, j % 2, 0:HIST], u[:, SEQ:SEQ + HIST])
                        dve.tensor_copy(pk[:, j % 2, HIST:].rearrange("p (b r) -> p b r", b=NB),
                                        U_s[j % 2][:, :, NT:SEG]).then_inc(s_pk, 1)
                        dve.wait_ge(s_ph, j + 1)
                        dve.tensor_tensor(actL[:, PH + i, :], pooled[:, :], actH[:, PH + i, :].bitcast(F32),
                                          ALU.subtract).then_inc(s_pl, 1)
                    elif kind == "m":
                        dve.wait_ge(w["used"], n + 1)
                        dve.wait_ge(s_sz, j + 1)
                        if j >= 2:
                            dve.wait_ge(s_gout[j % 2], 16 * (j // 2))
                        dve.scalar_tensor_tensor(out=as_thirds(g[:, j % 2]), in0=thirds(acc[n % 2]),
                                                 scalar=asc[:, j:j + 1], in1=as_thirds(sz[:, j % 2]),
                                                 op0=ALU.mult, op1=ALU.mult).then_inc(s_g, 1)

    class TokenRows:

        PARTS = (range(0, 4), range(4, 8), range(8, 9))

        def __init__(self, tag):
            self.turned = sem(f"rows_turned_{tag}")
            self.read = sem(f"rows_read_{tag}")

        def pe(self, pe, m, src):
            for q, tiles in enumerate(self.PARTS):
                c = 3 * m + q
                bank = 6 + c % 2
                if c >= 2:
                    pe.wait_ge(self.read, c - 1)
                for i in tiles:
                    r = rows_of(i)
                    mm = pe.transpose(ps[0:r, bank, (i % 4) * P:(i % 4 + 1) * P],
                                      src[:, i * P:i * P + r], ident[:, :])
                mm.then_inc(self.turned, 1)

        def dve(self, dve, m, dst):
            for q, tiles in enumerate(self.PARTS):
                bank = 6 + (3 * m + q) % 2
                dve.wait_ge(self.turned, 3 * m + q + 1)
                r = rows_of(tiles[0])
                dve.tensor_copy(dst[0:r, tiles[0]:tiles[-1] + 1, :],
                                ps[0:r, bank, 0:len(tiles) * P].rearrange("p (i n) -> p i n", n=P)).then_inc(self.read, 1)

    def stage_out(tag, mat, halves, y_tok, a, mov_hi, mov_lo, load, keep_src):
        w = weight_ring(tag, a)
        yT = a.take(f"yT_{tag}", [P, 2, T])
        nk = halves * KD
        if load is not None:
            src = Arena(y_at).take(f"mov_{tag}", [P, 4, T])
            s_in = [sem(f"s_in_{tag}{i}") for i in range(4)]
        jobs = [w_tiles(mat, h * KD, KD, n * P, P) for n in range(KD) for h in range(halves)]
        s_high, s_low = sem(f"s_high_{tag}"), sem(f"s_low_{tag}")
        s_yT = sem(f"s_yT_{tag}")
        rows = TokenRows(tag)

        def moving(k):
            return src[:, k % 4] if load is not None else keep_src[:, k]

        with nc.Block() as block:
            @block.sync
            def _(sp):
                def load_moving(k):
                    if k >= 4:
                        sp.wait_ge(s_low, k - 3)
                    sp.dma_start(src[:, k % 4], load[k]).then_inc(s_in[k % 4], 16)

                if load is not None:
                    for k in range(nk):
                        load_moving(k)
                stream_weights(sp, w, jobs)

            @block.gpsimd
            def _(pool):
                split_weights(pool, w, jobs)

            @block.tensor
            def _(pe):
                for n in range(KD):
                    if n >= 2:
                        pe.wait_ge(s_yT, n - 1)
                    for h in range(halves):
                        if n == 0:
                            pe.wait_ge(s_low, (h + 1) * KD)
                        product(pe, w, n * halves + h, KD, acc[n % 2], mov_hi, mov_lo, h * KD,
                                first=h == 0, last=h == halves - 1)
                    if n:
                        pe.wait_ge(s_yT, n)
                        rows.pe(pe, n - 1, yT[:, (n - 1) % 2])
                pe.wait_ge(s_yT, KD)
                rows.pe(pe, KD - 1, yT[:, (KD - 1) % 2])

            @block.scalar
            def _(act):
                for k in range(nk):
                    if load is not None:
                        act.wait_ge(s_in[k % 4], 16 * (k // 4 + 1))
                    act.copy(mov_hi[:, k, :], moving(k)).then_inc(s_high, 1)
                for n in range(KD):
                    act.wait_ge(w["used"], (n + 1) * halves)
                    if n >= 2:
                        act.wait_ge(rows.turned, 3 * (n - 1))
                    act.copy(as_thirds(yT[:, n % 2]), thirds(acc[n % 2])).then_inc(s_yT, 1)

            @block.vector
            def _(dve):
                for k in range(nk):
                    dve.wait_ge(s_high, k + 1)
                    dve.tensor_tensor(mov_lo[:, k, :], moving(k), mov_hi[:, k, :].bitcast(F32),
                                      ALU.subtract).then_inc(s_low, 1)
                for n in range(KD):
                    rows.dve(dve, n, y_tok[:, :, n * P:(n + 1) * P])

    y_at = free

    def stage_residual(layer, y_tok, a, x_src, targets):
        tag = f"res{layer}"
        grow = a.take(f"grow{layer}", [NCOND, D])
        postg = a.take(f"postg{layer}", [P, D])
        G = a.take(f"G{layer}", [P, 2, D])
        x_in = a.take(f"x_in{layer}", [P, 2, D])
        junk = a.take(f"junk{layer}", [P, D])
        ss = a.take(f"ssr{layer}", [P, 2, TT])
        rstd = a.take(f"rstdr{layer}", [P, 2, TT])
        s_g, s_gm, s_G = sem(f"s_gin_{tag}"), sem(f"s_gm_{tag}"), sem(f"s_G_{tag}")
        s_in = [sem(f"s_xin_{tag}{i}") for i in range(2)]
        s_init, s_ss, s_var, s_std = (sem(f"{n}_{tag}") for n in ("s_init", "s_ss", "s_var", "s_std"))
        s_new, s_xn, s_out = sem(f"s_new_{tag}"), sem(f"s_xn_{tag}"), s_xout[layer]
        link = chainer(f"dve_chain_{tag}")
        normed = None
        if targets:
            normed = NormedTranspose(f"l{layer + 1}", targets, a.take(f"tmpr{layer}", [P, 4, BANK]))

        with nc.Block() as block:
            @block.sync
            def _(sp):
                sp.dma_start(grow[:, :], gate_d[layer]).then_inc(s_g, 16)
                sp.dma_start(postg[:, :], post_g[layer:layer + 1, :].broadcast_to([P, D])).then_inc(s_g, 16)
                for i in range(TT):
                    if i >= 2:
                        sp.wait_ge(s_new, i - 1)
                    sp.dma_start(x_in[0:rows_of(i), i % 2, :], x_src(i)).then_inc(s_in[i % 2], 16)

            @block.tensor
            def _(pe):
                pe.wait_ge(s_g, 32)
                for h in range(2):
                    c = slice(h * BANK, (h + 1) * BANK)
                    pe.matmul(ps[:, h, :], sel_p[:, :], grow[:, c], start=True, stop=True).then_inc(s_gm, 1)
                    pe.matmul(ps[0:NS, 2 + h, :], sel_s[:, :], grow[:, c], start=True, stop=True).then_inc(s_gm, 1)
                if normed:
                    pe.wait_ge(s_G, 4)
                    normed.pe(pe, y_tok, s_xn, lambda i: i + 1)

            @block.scalar
            def _(act):
                act.wait_ge(s_init, 1)
                for i in range(TT):
                    r = rows_of(i)
                    if i:
                        act.wait_ge(s_ss, i)
                    act.activation(junk[0:r, :], y_tok[0:r, i, :], ACT.Square,
                                   accum_out=ss[0:r, 0, i:i + 1]).then_inc(s_ss, 1)
                act.wait_ge(s_var, 1)
                act.activation(rstd[:, 0], rstd[:, 0], ACT.Sqrt).then_inc(s_std, 1)
                for i in range(TT):
                    r = rows_of(i)
                    act.wait_ge(s_new, i + 1)
                    if normed:
                        act.dma_start(x1_d[i, 0:r], y_tok[0:r, i, :]).then_inc(s_out, 16)
                        act.wait_ge(s_ss, TT + i)
                        act.activation(junk[0:r, :], y_tok[0:r, i, :], ACT.Square,
                                       accum_out=ss[0:r, 1, i:i + 1]).then_inc(s_ss, 1)
                    else:
                        act.dma_start(yp[:, i, :] if i < QB else ys, y_tok[0:r, i, :]).then_inc(s_out, 16)
                if normed:
                    act.wait_ge(s_var, 2)
                    act.activation(rstd[:, 1], rstd[:, 1], ACT.Sqrt).then_inc(s_std, 1)
                    normed.act(act)
                act.wait_ge(s_out, 16 * TT)

            @block.vector
            def _(dve):
                dve.memset(ss[:, :, :], 1.0).then_inc(s_init, 1)
                for h in range(2):
                    c = slice(h * BANK, (h + 1) * BANK)
                    for q, r in ((0, P), (1, NS)):
                        dve.wait_ge(s_gm, 2 * h + q + 1)
                        dve.tensor_tensor(G[0:r, q, c], ps[0:r, 2 * q + h, :], postg[0:r, c], ALU.mult).then_inc(s_G, 1)
                dve.wait_ge(s_ss, TT)
                dve.tensor_scalar(rstd[:, 0], ss[:, 0], 1.0 / D, EPS, ALU.mult, ALU.add).then_inc(s_var, 1)
                dve.wait_ge(s_std, 1)
                link(dve, dve.reciprocal(rstd[:, 0], rstd[:, 0]))
                dve.wait_ge(s_G, 4)
                for i in range(TT):
                    r, q = rows_of(i), i // QB
                    link(dve, dve.scalar_tensor_tensor(out=y_tok[0:r, i, :], in0=y_tok[0:r, i, :],
                                                       scalar=rstd[0:r, 0, i:i + 1], in1=G[0:r, q, :],
                                                       op0=ALU.mult, op1=ALU.mult))
                    dve.wait_ge(s_in[i % 2], 16 * (i // 2 + 1))
                    dve.tensor_tensor(y_tok[0:r, i, :], y_tok[0:r, i, :], x_in[0:r, i % 2, :], ALU.add).then_inc(s_new, 1)
                if normed:
                    dve.wait_ge(s_ss, 2 * TT)
                    dve.tensor_scalar(rstd[:, 1], ss[:, 1], 1.0 / D, EPS, ALU.mult, ALU.add).then_inc(s_var, 1)
                    dve.wait_ge(s_std, 2)
                    link(dve, dve.reciprocal(rstd[:, 1], rstd[:, 1]))
                    dve.wait_ge(s_out, 16 * TT)
                    for i in range(TT):
                        r = rows_of(i)
                        dve.tensor_scalar(y_tok[0:r, i, :], y_tok[0:r, i, :], rstd[0:r, 1, i:i + 1], None,
                                          ALU.mult).then_inc(s_xn, 1)
                    normed.dve(dve, link)

    def stage_projections():
        a = Arena(free)
        w = weight_ring("c", a)
        o = a.take("o", [P, 2, T])
        tk = a.take("tk", [P, 2, TT, P])
        fx = a.take("fx", [NH, T])
        fe = a.take("fe", [NH, T])
        lfT = a.take("lfT", [NH, T])
        F = a.take("F", [NH, SEQ])
        fb = a.take("fb", [NH, 1])
        lrow = a.take("lrow", [P, TT, NH])
        kinds = [("k", p) for p in range(NP)] + [(x, p) for x in "vqz" for p in range(NP)]
        kinds.insert(2, ("f", 0))
        W = NH * HD
        col = {"k": (kv_w, 0), "v": (kv_w, W), "f": (kv_w, 2 * W), "q": (b_in_w[0], 0), "z": (b_in_w[0], W)}
        jobs = [w_tiles(col[x][0], 0, KD, col[x][1] + p * P, NH if x == "f" else P) for x, p in kinds]
        tiles = [x for x in kinds if x[0] != "f"]
        order = {x: m for m, x in enumerate(tiles)}
        turn = {x: m for m, x in enumerate(t for t in tiles if t[0] in "kv")}
        store = {"k": kT_d, "q": qT_d, "z": zT_d}

        s_o = sem("s_o")
        s_oout = [sem(f"s_oout{i}") for i in range(2)]
        s_fb, s_fx, s_fe, s_lf, s_F, s_ones = (sem(n) for n in ("s_fb", "s_fx", "s_fe", "s_lf", "s_F", "s_ones"))
        s_lT, s_lrow = sem("s_lT"), sem("s_lrow")
        link, alink = chainer("dve_chain4"), chainer("act_chain4")
        rows = TokenRows("c")
        outs_before = {}
        count = [0, 0]
        for x, m in order.items():
            outs_before[x] = count[m % 2]
            count[m % 2] += x[0] in store

        def store_rows(act, x):
            t = turn[x]
            act.wait_ge(rows.read, 3 * (t + 1))
            big, small = (kp, ks) if x[0] == "k" else (vp, vs)
            c = slice(x[1] * P, (x[1] + 1) * P)
            act.dma_start(big[:, :, c], tk[:, t % 2, 0:QB, :]).then_inc(s_tout[t % 2], 16)
            act.dma_start(small[:, c], tk[0:NS, t % 2, QB, :]).then_inc(s_tout[t % 2], 16)

        with nc.Block() as block:
            @block.sync
            def _(sp):
                with nc.allow_non_contiguous_dma(reason="one value a head"):
                    sp.dma_start(fb[:, :], f_b.rearrange("(h a) -> h a", a=1)).then_inc(s_fb, 16)
                stream_weights(sp, w, jobs)

            @block.gpsimd
            def _(pool):
                split_weights(pool, w, jobs)

            @block.tensor
            def _(pe):
                late = None
                for n, x in enumerate(kinds):
                    if n >= 2:
                        was = kinds[n - 2]
                        if was[0] == "f":
                            pe.wait_ge(s_fx, 1)
                        else:
                            pe.wait_ge(s_o, order[was] + 1)
                    product(pe, w, n, KD, acc[n % 2], actH, actL, 0 if x[0] in "kvf" else KD)
                    if late:
                        pe.wait_ge(s_o, order[late] + 1)
                        rows.pe(pe, turn[late], o[:, order[late] % 2])
                    late = x if x[0] in "kv" else None
                pe.wait_ge(s_lf, 1)
                pe.wait_ge(s_F, 1)
                pe.wait_ge(s_o, len(tiles))
                for i in range(TT):
                    r = rows_of(i)
                    mm = pe.transpose(ps[0:r, 0, i * NH:(i + 1) * NH], lfT[:, i * P:i * P + r], ident[0:NH, 0:NH])
                for i in range(QB):
                    mm = pe.transpose(ps[:, 0, (TT + i) * NH:(TT + i + 1) * NH], F[:, i * P:(i + 1) * P],
                                      ident[0:NH, 0:NH])
                mm.then_inc(s_lT, 1)

            @block.scalar
            def _(act):
                late = None
                for n, x in enumerate(kinds):
                    if x[0] == "f":
                        act.wait_ge(s_fx, 1)
                        alink(act, act.activation(fe[:, :], fx[:, :], ACT.Abs))
                        alink(act, act.activation(fe[:, :], fe[:, :], ACT.Exp, scale=-1.0))
                        act.activation(fe[:, :], fe[:, :], ACT.Ln, bias=1.0).then_inc(s_fe, 1)
                        continue
                    m = order[x]
                    act.wait_ge(w["used"], n + 1)
                    if outs_before[x]:
                        act.wait_ge(s_oout[m % 2], 16 * outs_before[x])
                    if m >= 2 and tiles[m - 2][0] in "kv":
                        act.wait_ge(rows.turned, 3 * (turn[tiles[m - 2]] + 1))
                    dst, src = as_thirds(o[:, m % 2]), thirds(acc[n % 2])
                    if x[0] == "z":
                        act.activation(dst, src, ACT.Silu).then_inc(s_o, 1)
                    elif x[0] == "q":
                        act.activation(dst, src, ACT.Copy, scale=HD ** -0.5).then_inc(s_o, 1)
                    else:
                        act.copy(dst, src).then_inc(s_o, 1)
                    if late:
                        store_rows(act, late)
                    late = x if x[0] in "kv" else None
                    if x[0] in store:
                        act.wait_ge(s_o, m + 1)
                        act.dma_start(store[x[0]][x[1]], o[:, m % 2]).then_inc(s_oout[m % 2], 16)
                act.wait_ge(s_F, 1)
                act.wait_ge(s_lrow, 1)
                act.dma_start(negF_d, fe[:, 0:SEQ]).then_inc(s_lout, 16)
                act.dma_start(lfp, lrow[:, 0:QB, :]).then_inc(s_lout, 16)
                act.dma_start(lfs, lrow[0:NS, QB, :]).then_inc(s_lout, 16)
                act.wait_ge(s_lout, 48)
                for i in range(2):
                    act.wait_ge(s_oout[i], 16 * count[i])
                    act.wait_ge(s_tout[i], 32 * NP)

            @block.vector
            def _(dve):
                dve.memset(F[:, :], 1.0).then_inc(s_ones, 1)
                for n, x in enumerate(kinds):
                    if x[0] == "f":
                        dve.wait_ge(w["used"], n + 1)
                        dve.wait_ge(s_fb, 16)
                        dve.tensor_scalar(as_thirds(fx[:, :]), acc[n % 2][0:NH, :, 0:CH], fb[:, 0:1], None,
                                          ALU.add).then_inc(s_fx, 1)
                        dve.wait_ge(s_fe, 1)
                        dve.wait_ge(s_fx, 1)
                        link(dve, dve.tensor_scalar(fx[:, :], fx[:, :], 0.0, None, ALU.min))
                        dve.tensor_tensor(lfT[:, :], fx[:, :], fe[:, :], ALU.subtract).then_inc(s_lf, 1)
                        dve.wait_ge(s_lf, 1)
                        dve.wait_ge(s_ones, 1)
                        link(dve, dve.tensor_tensor_scan(fx[:, 0:SEQ], F[:, :], lfT[:, 0:SEQ], 0.0,
                                                         op0=ALU.mult, op1=ALU.add))
                        link(dve, dve.tensor_scalar(fe[:, 0:SEQ], fx[:, 0:SEQ], -1.0, None, ALU.mult))
                        dve.tensor_copy(F[:, :], fx[:, 0:SEQ]).then_inc(s_F, 1)
                    elif x[0] in "kv":
                        t = turn[x]
                        if t >= 2:
                            dve.wait_ge(s_tout[t % 2], 32 * (t // 2))
                        rows.dve(dve, t, tk[:, t % 2])
                dve.wait_ge(s_lT, 1)
                link(dve, dve.tensor_copy(lrow[:, 0:QB, :], ps[:, 0, 0:QB * NH].rearrange("p (i h) -> p i h", h=NH)))
                link(dve, dve.tensor_copy(lf_s[:, :], ps[0:NS, 0, QB * NH:TT * NH]))
                link(dve, dve.tensor_copy(Ftok[:, :, :], ps[:, 0, TT * NH:(TT + QB) * NH].rearrange(
                    "p (i h) -> p i h", h=NH)))
                dve.tensor_copy(lrow[0:NS, QB, :], lf_s[:, :]).then_inc(s_lrow, 1)

    def stage_attention(og):
        a = Arena(og_end)
        KR, VR = 6, 6
        K_at = a.at
        K = a.take("K", [P, KR, D])
        V = a.take("V", [P, VR, D])
        KT = a.take("KT", [P, 2, D])
        qT = a.take("qT", [P, 2, SEQ])
        kT = a.take("kT", [P, 2, SEQ])
        zT = a.take("zT", [P, 2, SEQ])
        Vt = a.take("Vt", [P, 2, QB, P])
        nF = a.take("nF", [P, 2, 2, SEQ])
        Sb = [a.take("S_long", [P, SEQ]), a.take("S_short", [P, BANK])]
        PT = [a.take("PT_long", [P, SEQ]), a.take("PT_short", [P, BANK])]
        o_tok = a.take("o_tok", [P, 2, QB, P])
        nmax = a.take("nmax", [P, 4])
        rsum = a.take("rsum", [P, 4])
        rinv = a.take("rinv", [P, 4])
        q_s = a.take("q_s", [P, NP, NS])
        k_s = a.take("k_s", [P, NP, NS])
        z_s = a.take("z_s", [P, NP, NS])
        v_s = a.take("v_s", [NS, D])
        qblk = a.take("qblk", [P, NP, NB, 2 * NT])
        newT = a.take("newT", [NS, NB, NP, 2 * NT])
        sT = a.take("sT", [P, NPG, NR])
        Sd = a.take("Sd", [NR, PAST + NS])
        PTd = a.take("PTd", [P, 2, NPG, NR])
        PTn = a.take("PTn", [NS, 2, NR])
        pt = a.take("pt", [1, NB * NPG], I32)
        E_all = a.take("E_all", [P, NB, NR])
        G = a.take("Gf", [P, PAST + NS])
        nmask = a.take("nmask", [NR, 2 * NS - NT])
        dstat = a.take("dstat", [NR, 4])
        zrow = a.take("zrow", [1, P])
        b = Arena(K_at)
        LF = b.take("LF", [P, NPG, NB * NH])
        LT = b.take("LT", [P, PAST + NT])
        Fs = b.take("Fs", [P, PAST + NT])
        X = b.take("X", [NS, NB, NH])
        bm = b.take("bm", [NS, NB, NH])
        tsel = b.take("tsel", [NS, NT])
        one = b.take("one", [P, 1])
        mpre = b.take("mpre", [NR, NH, 2 * NS - NT])

        ORDER = (7, 0, 6, 1, 5, 2, 4, 3)
        UN = 2 * QB
        NU = NP * UN
        V0 = UN + 7
        STEPS = NB * NPG + V0

        def unit(u):
            return u // UN, u % UN // QB, ORDER[u % QB]

        def s_bank(u):
            return ps[:, 0:2, :].rearrange("p b n -> p (b n)") if u % 2 == 0 else ps[:, 2, :]

        s_pt, s_set = sem("s_pt"), sem("s_set")
        s_lfc = sem("s_lfc")
        s_pair = [sem(f"s_pair{i}") for i in range(2)]
        s_K = [sem(f"s_K{i}") for i in range(KR)]
        s_V = [sem(f"s_V{i}") for i in range(VR)]
        s_c, s_ones = sem("s_cst5"), sem("s_ones5")
        s_lT5, s_LT, s_X, s_newf, s_G5 = (sem(n) for n in ("s_lT5", "s_LT", "s_X", "s_newf", "s_G5"))
        s_qblk, s_qz, s_nT, s_newT = sem("s_qblk"), sem("s_qz"), sem("s_nT"), sem("s_newT")
        s_S, s_bias, s_mask, s_max, s_exp = (sem(n) for n in ("s_S", "s_bias", "s_mask", "s_max", "s_exp"))
        s_PT, s_PTe, s_O, s_On = (sem(n) for n in ("s_PT", "s_PTe", "s_O", "s_On"))
        s_oT, s_og = sem("s_oT", ), sem("s_og")
        s_Kt, s_KeA, s_KeB, s_sc, s_sTe = (sem(n) for n in ("s_Kt", "s_KeA", "s_KeB", "s_sc", "s_sTe"))
        s_row, s_rowe, s_dmax, s_dexp, s_dn = (sem(n) for n in ("s_row", "s_rowe", "s_dmax", "s_dexp", "s_dn"))
        s_pd, s_pde, s_pv, s_ogs = (sem(n) for n in ("s_pd", "s_pde", "s_pv", "s_ogs"))
        link, plink = chainer("dve_chain5"), chainer("pool_chain5")
        vp_p, k_rows, v_rows = vp, cache_k.rearrange("g k h d -> g k (h d)"), cache_v.rearrange("g k h d -> g k (h d)")
        NPAIR = 6

        loads = []
        for t in range(NB * NPG):
            loads.append((t - KR + 1.5, "K", t))
            loads.append((t + V0 - VR + 1.6, "V", t))
        for p in range(1, NP):
            loads.append((UN * (p - 1) + 3.7, "pair", p))
        loads.sort()

        with nc.Block() as block:
            @block.sync
            def _(sp):
                def pair_loads(p):
                    i = p % 2
                    if p >= 2:
                        sp.wait_ge(s_S, UN * (p - 1))
                        sp.wait_ge(s_bias, UN * (p - 1))
                        sp.wait_ge(s_O, UN * (p - 1))
                        sp.wait_ge(s_og, 2 * (p - 1))
                    sp.dma_start(qT[:, i], qT_d[p, :, 0:SEQ]).then_inc(s_pair[i], 16)
                    sp.dma_start(kT[:, i], kT_d[p, :, 0:SEQ]).then_inc(s_pair[i], 16)
                    sp.dma_start(zT[:, i], zT_d[p, :, 0:SEQ]).then_inc(s_pair[i], 16)
                    sp.dma_start(Vt[:, i], vp_p[:, :, p * P:(p + 1) * P]).then_inc(s_pair[i], 16)
                    for h in range(2):
                        sp.dma_start(nF[:, i, h], negF_d[2 * p + h:2 * p + h + 1, :].broadcast_to([P, SEQ])).then_inc(
                            s_pair[i], 16)

                sp.dma_start(pt[:, :], page_table.rearrange("(a b) g -> a (b g)", a=1)).then_inc(s_pt, 16)
                sp.dma_start(q_s[:, :, :], qT_d[:, :, SEQ:T].rearrange("k p n -> p k n")).then_inc(s_set, 16)
                sp.dma_start(k_s[:, :, :], kT_d[:, :, SEQ:T].rearrange("k p n -> p k n")).then_inc(s_set, 16)
                sp.dma_start(z_s[:, :, :], zT_d[:, :, SEQ:T].rearrange("k p n -> p k n")).then_inc(s_set, 16)
                sp.dma_start(v_s[:, :], vs).then_inc(s_set, 16)
                sp.wait_ge(s_pt, 16)
                reg = sp.alloc_register("page")

                def page(t):
                    sp.reg_load(reg, pt[0:1, t:t + 1])
                    return bass.ds(sp.snap(reg, min_val=0, max_val=n_phys - 1), 1)

                for t in range(NB * NPG):
                    bq, g = t // NPG, t % NPG
                    sp.dma_start(LF[:, g, bq * NH:(bq + 1) * NH],
                                 cache_logf[page(t)].rearrange("a k h -> (a k) h")).then_inc(s_lfc, 16)
                pair_loads(0)
                sp.wait_ge(s_G5, 1)
                for _, what, t in loads:
                    if what == "pair":
                        pair_loads(t)
                    elif what == "K":
                        if t >= KR:
                            sp.wait_ge(s_Kt, t - KR + 1)
                        sp.dma_start(K[:, t % KR], k_rows[page(t)].rearrange("a k n -> (a k) n")).then_inc(
                            s_K[t % KR], 16)
                    else:
                        if t >= VR:
                            sp.wait_ge(s_pv, t - VR + 1)
                        sp.dma_start(V[:, t % VR], v_rows[page(t)].rearrange("a k n -> (a k) n")).then_inc(
                            s_V[t % VR], 16)

            @block.gpsimd
            def _(pool):
                pool.memset(E_all[:, :, :], 0.0).then_inc(s_ones, 1)
                pool.memset(mpre[:, :, :], 1.0).then_inc(s_ones, 1)
                pool.memset(bm[:, :, :], 1.0).then_inc(s_ones, 1)
                pool.memset(one[:, :], 1.0).then_inc(s_ones, 1)
                pool.memset(qblk[:, :, :, :], 0.0).then_inc(s_ones, 1)
                pool.memset(zrow[:, :], 0.0).then_inc(s_ones, 1)
                pool.wait_ge(s_ones, 6)
                v = E_all[:, :, :].rearrange("p b (h q) -> p b h q", q=NT)
                plink(pool, pool.affine_select(out=v, in_=v, compare_op=ALU.not_equal, fill=1.0, base=0,
                                               pattern=[[-NH, NB], [-1, NH], [0, NT]], channel_multiplier=1))
                v = bm[:, :, :]
                plink(pool, pool.affine_select(out=v, in_=v, compare_op=ALU.is_ge, fill=0.0, base=0,
                                               pattern=[[-NT, NB], [0, NH]], channel_multiplier=1))
                plink(pool, pool.affine_select(out=v, in_=v, compare_op=ALU.is_ge, fill=0.0, base=NT - 1,
                                               pattern=[[NT, NB], [0, NH]], channel_multiplier=-1))
                v, n = mpre[:, :, :], 2 * NS - NT
                plink(pool, pool.affine_select(out=v, in_=v, compare_op=ALU.is_ge, fill=0.0, base=NS - NT,
                                               pattern=[[-NT, NH], [-1, n]], channel_multiplier=1))
                plink(pool, pool.affine_select(out=v, in_=v, compare_op=ALU.is_ge, fill=0.0, base=NT - 1,
                                               pattern=[[NT, NH], [0, n]], channel_multiplier=-1))
                pool.affine_select(out=v, in_=v, compare_op=ALU.is_ge, fill=0.0, base=-(NS - NT),
                                   pattern=[[0, NH], [1, n]], channel_multiplier=0).then_inc(s_c, 1)
                for u in range(NU):
                    i = unit(u)[2]
                    pool.wait_ge(s_bias, u + 1)
                    blk = Sb[u % 2][:, i * P:(i + 1) * P]
                    pool.affine_select(out=blk, in_=blk, compare_op=ALU.is_ge, fill=NEG, base=0,
                                       pattern=[[-1, P]], channel_multiplier=1).then_inc(s_mask, 1)

            @block.tensor
            def _(pe):
                pe.wait_ge(s_lfc, 16 * NB * NPG)
                for g in range(NPG):
                    mm = pe.transpose(ps[:, g // 4, g % 4 * P:(g % 4 + 1) * P], LF[:, g, :], ident[:, :])
                mm.then_inc(s_lT5, 1)
                pe.wait_ge(s_X, 2)
                pe.matmul(ps[:, 4, 0:NT], X[:, :, :].rearrange("p b h -> p (b h)"), tsel[:, :],
                          start=True, stop=True).then_inc(s_newf, 1)
                pe.wait_ge(s_qblk, 2)
                pe.wait_ge(s_set, 64)
                for p in range(NP):
                    mm = pe.matmul(ps[0:NS, 5, p * NR:(p + 1) * NR], k_s[:, p, :],
                                   qblk[:, p].rearrange("p b c -> p (b c)"), start=True, stop=True)
                mm.then_inc(s_nT, 1)
                pe.wait_ge(s_newT, 1)
                pe.wait_ge(s_G5, 1)

                def scores(u):
                    p, h, i = unit(u)
                    if u % UN == 0:
                        pe.wait_ge(s_pair[p % 2], 16 * NPAIR * (p // 2 + 1))
                    if u >= 2:
                        pe.wait_ge(s_PTe, u - 1)
                    n, bank, hs = (i + 1) * P, s_bank(u), slice(h * HD, (h + 1) * HD)
                    for c in range(0, n, BANK):
                        e = min(c + BANK, n)
                        mm = pe.matmul(bank[:, c:e], qT[hs, p % 2, i * P:(i + 1) * P], kT[hs, p % 2, c:e],
                                       start=True, stop=True)
                    mm.then_inc(s_S, 1)

                def turn_probs(u):
                    i, bank = unit(u)[2], s_bank(u)
                    pe.wait_ge(s_exp, u + 1)
                    for j in range(i + 1):
                        mm = pe.transpose(bank[:, j * P:(j + 1) * P], Sb[u % 2][:, j * P:(j + 1) * P], ident[:, :])
                    mm.then_inc(s_PT, 1)

                def values(u):
                    p, h, i = unit(u)
                    pe.wait_ge(s_PTe, u + 1)
                    if u:
                        pe.wait_ge(s_On, u)
                    for j in range(i + 1):
                        mm = pe.matmul(ps[:, 3, 0:HD], PT[u % 2][:, j * P:(j + 1) * P],
                                       Vt[:, p % 2, j, h * HD:(h + 1) * HD], start=(j == 0), stop=(j == i))
                    mm.then_inc(s_O, 1)

                def turn_out(p, half, units):
                    pe.wait_ge(s_On, units)
                    for i in range(4):
                        mm = pe.transpose(ps[:, 3, i * P:(i + 1) * P], o_tok[:, p % 2, 4 * half + i, :], ident[:, :])
                    mm.then_inc(s_oT, 1)

                def turn_K(t):
                    pe.wait_ge(s_K[t % KR], 16 * (t // KR + 1))
                    if t:
                        pe.wait_ge(s_KeA, t)
                        pe.wait_ge(s_KeB, t)
                    for c in range(NP):
                        mm = pe.transpose(ps[:, 5 + c // 4, c % 4 * P:(c % 4 + 1) * P],
                                          K[:, t % KR, c * P:(c + 1) * P], ident[:, :])
                    mm.then_inc(s_Kt, 1)

                def page_scores(t):
                    bq, g = t // NPG, t % NPG
                    pe.wait_ge(s_KeA, t + 1)
                    pe.wait_ge(s_KeB, t + 1)
                    if t % 8 == 0 and t:
                        pe.wait_ge(s_sTe, t // 8)
                    for c in range(NP):
                        mm = pe.matmul(ps[:, 7, g % 8 * NR + 8 * c:g % 8 * NR + 8 * c + 8],
                                       KT[:, t % 2, c * P:(c + 1) * P], qblk[:, c, bq, :], start=True, stop=True)
                    mm.then_inc(s_sc, 1)

                def row_chunk(bq, c):
                    bank = 5 + c % 2
                    if c >= 2:
                        pe.wait_ge(s_rowe, 5 * bq + c - 1)
                    if c < 4:
                        out = ps[0:NR, bank, :]
                        pe.wait_ge(s_sTe, 2 * bq + 2)
                        pe.matmul(out, E_all[:, bq, :], G[:, c * BANK:(c + 1) * BANK], start=True, stop=True,
                                  skip_group_check=True)
                        for g in range(4):
                            mm = pe.matmul(ps[0:NR, bank, g * P:(g + 1) * P], sT[:, 4 * c + g, :], ident[:, :],
                                           start=False, stop=True, skip_group_check=True)
                    else:
                        out = ps[0:NR, bank, 0:NS]
                        pe.matmul(out, E_all[:, bq, :], G[:, PAST:PAST + NS], start=True, stop=False)
                        mm = pe.matmul(out, newT[:, bq].rearrange("n k c -> n (k c)"), ident[0:NS, 0:NS], start=False, stop=True)
                    mm.then_inc(s_row, 1)

                def turn_dprobs(bq, part):
                    bank = 5 + part % 2
                    pe.wait_ge(s_dn, bq + 1)
                    if part >= 2:
                        pe.wait_ge(s_pde, 3 * bq + part - 1)
                    if part < 2:
                        for g in range(8):
                            mm = pe.transpose(ps[:, bank, g * NR:(g + 1) * NR],
                                              Sd[:, (8 * part + g) * P:(8 * part + g + 1) * P], ident[0:NR, 0:NR])
                    else:
                        mm = pe.transpose(ps[0:NS, bank, 0:NR], Sd[:, PAST:PAST + NS], ident[0:NR, 0:NR])
                    mm.then_inc(s_pd, 1)

                def page_values(t):
                    bq, g = t // NPG, t % NPG
                    pe.wait_ge(s_V[t % VR], 16 * (t // VR + 1))
                    if g == 0:
                        pe.wait_ge(s_pde, 3 * (bq + 1))
                        if bq:
                            pe.wait_ge(s_ogs, bq)
                        pe.matmul(ps[:, 4, 0:NR], zrow[:, :], zrow[:, 0:NR], start=True, stop=True)
                        for c in range(NP):
                            pe.matmul(ps[:, 4, 8 * c:8 * c + 8], v_s[:, c * P:(c + 1) * P],
                                      PTn[:, bq % 2, 8 * c:8 * c + 8], start=False, stop=True,
                                      skip_group_check=True)
                    for c in range(NP):
                        mm = pe.matmul(ps[:, 4, 8 * c:8 * c + 8], V[:, t % VR, c * P:(c + 1) * P],
                                       PTd[:, bq % 2, g, 8 * c:8 * c + 8], start=False, stop=True,
                                       skip_group_check=True)
                    mm.then_inc(s_pv, 1)

                scores(0)
                scores(1)
                for s in range(STEPS):
                    g, bq = s % NPG, s // NPG - 1
                    if s < NU:
                        turn_probs(s)
                    if 0 <= bq < NB:
                        if g in (1, 2):
                            pe.wait_ge(s_KeA, min(s, NB * NPG))
                            pe.wait_ge(s_KeB, min(s, NB * NPG))
                            for c in ((0, 1) if g == 1 else (2, 3, 4)):
                                row_chunk(bq, c)
                            pe.wait_ge(s_rowe, 5 * bq + (2 if g == 1 else 5))
                        if g == 5:
                            pe.wait_ge(s_KeA, min(s, NB * NPG))
                            pe.wait_ge(s_KeB, min(s, NB * NPG))
                            for part in range(3):
                                turn_dprobs(bq, part)
                            pe.wait_ge(s_pde, 3 * (bq + 1))
                    if s < NB * NPG:
                        turn_K(s)
                    if 1 <= s <= NB * NPG:
                        page_scores(s - 1)
                    if s >= V0:
                        page_values(s - V0)
                    if s > UN and s % UN in (1, 2) and s // UN <= NP:
                        turn_out(s // UN - 1, s % UN - 1, min(s - 1, NU))
                    if 1 <= s <= NU:
                        if s % UN in (1, 2) and s > UN:
                            pe.wait_ge(s_og, 2 * (s // UN - 1) + s % UN)
                        values(s - 1)
                    if s + 2 < NU:
                        scores(s + 2)

            @block.scalar
            def _(act):
                act.wait_ge(s_lT5, 1)
                act.copy(LT[:, 0:PAST].rearrange("p (b n) -> p b n", b=4), ps[:, 0:4, :]).then_inc(s_LT, 1)
                act.wait_ge(s_newf, 1)
                act.copy(LT[:, PAST:PAST + NT], ps[:, 4, 0:NT]).then_inc(s_LT, 1)

                def exps(u):
                    n, t = (unit(u)[2] + 1) * P, Sb[u % 2]
                    act.wait_ge(s_max, u + 1)
                    act.activation(t[:, 0:n], t[:, 0:n], ACT.Exp, bias=nmax[:, u % 4:u % 4 + 1],
                                   accum_out=rsum[:, u % 4:u % 4 + 1]).then_inc(s_exp, 1)

                exps(0)
                exps(1)
                for s in range(STEPS):
                    g, bq = s % NPG, s // NPG - 1
                    if s < NU:
                        n = (unit(s)[2] + 1) * P
                        act.wait_ge(s_PT, s + 1)
                        if s >= 2:
                            act.wait_ge(s_O, s - 1)
                        act.copy(PT[s % 2][:, 0:n], s_bank(s)[:, 0:n]).then_inc(s_PTe, 1)
                    if 0 <= bq < NB and g == 5:
                        for part in range(3):
                            act.wait_ge(s_pd, 3 * bq + part + 1)
                            if part < 2:
                                act.copy(PTd[:, bq % 2, 8 * part:8 * part + 8, :].rearrange("p g r -> p (g r)"),
                                         ps[:, 5 + part, :]).then_inc(s_pde, 1)
                            else:
                                act.copy(PTn[:, bq % 2, :], ps[0:NS, 5, 0:NR]).then_inc(s_pde, 1)
                    if s < NB * NPG:
                        act.wait_ge(s_Kt, s + 1)
                        if s >= 2:
                            act.wait_ge(s_sc, s - 1)
                        act.copy(KT[:, s % 2, 0:BANK], ps[:, 5, :]).then_inc(s_KeA, 1)
                    if s % 8 == 0 and 1 <= s <= NB * NPG:
                        half = s // 8 - 1
                        act.wait_ge(s_sc, s)
                        if half >= 2:
                            act.wait_ge(s_row, 5 * (half // 2 - 1) + 4)
                        act.copy(sT[:, 8 * (half % 2):8 * (half % 2) + 8, :].rearrange("p g r -> p (g r)"),
                                 ps[:, 7, :]).then_inc(s_sTe, 1)
                    if 0 <= bq < NB:
                        if g == 4:
                            act.wait_ge(s_dmax, bq + 1)
                            act.activation(Sd[:, :], Sd[:, :], ACT.Exp, bias=dstat[:, 0:1],
                                           accum_out=dstat[:, 1:2]).then_inc(s_dexp, 1)
                    if s + 2 < NU:
                        exps(s + 2)

            @block.vector
            def _(dve):
                dve.wait_ge(s_c, 1)
                dve.tensor_tensor(X[:, :, :], bm[:, :, :], lf_s[:, :].unsqueeze(1).broadcast_to([NS, NB, NH]),
                                  ALU.mult).then_inc(s_X, 1)
                dve.tensor_reduce(tsel[:, :], ident[0:NS, 0:NS].rearrange("p (b t) -> p t b", t=NT), AX_X,
                                  ALU.add).then_inc(s_X, 1)
                dve.wait_ge(s_set, 64)
                for h in range(2):
                    r = slice(h * HD, (h + 1) * HD)
                    dve.tensor_copy(qblk[r, :, :, h * NT:(h + 1) * NT],
                                    q_s[r, :, :].rearrange("p k (b t) -> p k b t", t=NT)).then_inc(s_qblk, 1)
                link(dve, dve.tensor_reduce(nmask[:, :], mpre[:, :, :].rearrange("p h c -> p c h"), AX_X, ALU.add))
                link(dve, dve.tensor_scalar(nmask[:, :], nmask[:, :], 1.0, -NEG, ALU.subtract, ALU.mult))
                dve.wait_ge(s_nT, 1)
                dve.tensor_copy(newT[:, :, :, :].rearrange("n b k c -> n k b c"),
                                ps[0:NS, 5, :].rearrange("n (k b c) -> n k b c", k=NP, b=NB)).then_inc(s_newT, 1)
                dve.wait_ge(s_LT, 2)
                n = PAST + NT
                link(dve, dve.tensor_tensor_scan(Fs[:, :], one[:, 0:1].broadcast_to([P, n]), LT[:, :], 0.0,
                                                 op0=ALU.mult, op1=ALU.add))
                link(dve, dve.tensor_scalar(Fs[:, :], Fs[:, :], Fs[:, n - 1:n], -1.0, ALU.subtract, ALU.mult))
                link(dve, dve.tensor_copy(G[:, 0:PAST], Fs[:, 0:PAST]))
                dve.tensor_copy(G[:, PAST:PAST + NS].rearrange("p (b t) -> p b t", b=NB),
                                Fs[:, PAST:n].unsqueeze(1).broadcast_to([P, NB, NT])).then_inc(s_G5, 1)

                def logits(u):
                    p, h, i = unit(u)
                    m, t = (i + 1) * P, Sb[u % 2]
                    dve.wait_ge(s_S, u + 1)
                    if u % UN == 0:
                        dve.wait_ge(s_pair[p % 2], 16 * NPAIR * (p // 2 + 1))
                    dve.scalar_tensor_tensor(out=t[:, 0:m], in0=nF[:, p % 2, h, 0:m],
                                             scalar=Ftok[:, i, 2 * p + h:2 * p + h + 1], in1=s_bank(u)[:, 0:m],
                                             op0=ALU.add, op1=ALU.add).then_inc(s_bias, 1)
                    dve.wait_ge(s_mask, u + 1)
                    dve.tensor_reduce(nmax[:, u % 4:u % 4 + 1], t[:, 0:m], AX_X, ALU.max, negate=True).then_inc(s_max, 1)

                logits(0)
                logits(1)
                for s in range(STEPS):
                    g, bq = s % NPG, s // NPG - 1
                    if 0 <= bq < NB and g in (1, 2):
                        for c in ((0, 1) if g == 1 else (2, 3, 4)):
                            dve.wait_ge(s_row, 5 * bq + c + 1)
                            if c == 0 and bq:
                                dve.wait_ge(s_pd, 3 * bq)
                            if c < 4:
                                dve.tensor_copy(Sd[:, c * BANK:(c + 1) * BANK], ps[0:NR, 5 + c % 2, :]).then_inc(s_rowe, 1)
                            else:
                                mk = nmask[:, NS - NT - NT * bq:2 * NS - NT - NT * bq]
                                dve.tensor_tensor(Sd[:, PAST:PAST + NS], ps[0:NR, 5, 0:NS], mk, ALU.add).then_inc(s_rowe, 1)
                    if s < NB * NPG:
                        dve.wait_ge(s_Kt, s + 1)
                        if s >= 2:
                            dve.wait_ge(s_sc, s - 1)
                        dve.tensor_copy(KT[:, s % 2, BANK:D], ps[:, 6, :]).then_inc(s_KeB, 1)
                    if 0 <= bq < NB:
                        if g == 3:
                            dve.wait_ge(s_rowe, 5 * (bq + 1))
                            dve.tensor_reduce(dstat[:, 0:1], Sd[:, :], AX_X, ALU.max, negate=True).then_inc(s_dmax, 1)
                    if s > UN and s % UN in (1, 2) and s // UN <= NP:
                        p, half = s // UN - 1, s % UN - 1
                        dve.wait_ge(s_oT, 2 * p + half + 1)
                        c = slice(half * BANK, (half + 1) * BANK)
                        dve.tensor_tensor(og[:, p, c], ps[:, 3, :], zT[:, p % 2, c], ALU.mult).then_inc(s_og, 1)
                    if 1 <= s <= NU:
                        u = s - 1
                        p, h, i = unit(u)
                        dve.wait_ge(s_exp, u + 1)
                        link(dve, dve.reciprocal(rinv[:, u % 4:u % 4 + 1], rsum[:, u % 4:u % 4 + 1]))
                        dve.wait_ge(s_O, u + 1)
                        dve.tensor_scalar(o_tok[:, p % 2, i, h * HD:(h + 1) * HD], ps[:, 3, 0:HD],
                                          rinv[:, u % 4:u % 4 + 1], None, ALU.mult).then_inc(s_On, 1)
                    if 0 <= bq < NB and g == 4:
                        dve.wait_ge(s_dexp, bq + 1)
                        link(dve, dve.reciprocal(dstat[:, 2:3], dstat[:, 1:2]))
                        dve.tensor_scalar(Sd[:, :], Sd[:, :], dstat[:, 2:3], None, ALU.mult).then_inc(s_dn, 1)
                    if s >= V0 and (s - V0) % NPG == NPG - 1:
                        bv = (s - V0) // NPG
                        dve.wait_ge(s_pv, NPG * (bv + 1))
                        o4 = ps[:, 4, 0:NR].rearrange("p (k h t) -> p k h t", k=NP, h=2)
                        for h in range(2):
                            r, c = slice(h * HD, (h + 1) * HD), slice(bv * NT, (bv + 1) * NT)
                            ins = dve.tensor_tensor(og[r, :, SEQ + bv * NT:SEQ + (bv + 1) * NT], o4[r, :, h, :],
                                                    z_s[r, :, c], ALU.mult)
                        ins.then_inc(s_ogs, 1)
                    if s + 2 < NU:
                        logits(s + 2)

    stage_conditioning()
    end_stage()
    stage_pooling()
    end_stage()
    arena = Arena(y_at)
    y_tok = arena.take("y_tok", [P, TT, D])
    stage_out("b", a_out_w[0], 2, y_tok, arena, actH, actL, g_d, None)
    end_stage()
    arena = Arena(y_at)
    arena.at += TT * D * 4
    stage_residual(0, y_tok, arena, lambda i: x_p[:, i, :] if i < QB else x_s,
                   [(0, kvg, None), (KD, modA[:, 1], modB[:, 1])])
    end_stage()
    stage_projections()
    end_stage()
    after = Arena(act_at)
    og = after.take("og", [P, NP, T])
    og_end = after.at
    stage_attention(og)
    end_stage()
    ogH = after.take("ogH", [P, NP, T], F32R)
    ogL = after.take("ogL", [P, NP, T], F32R)
    y2 = after.take("y2_tok", [P, TT, D])
    y2_end = after.at
    stage_out("d", b_out_w[0], 1, y2, after, ogH, ogL, None, og)
    end_stage()
    after = Arena(y2_end)
    stage_residual(1, y2, after, lambda i: x1_d[i, 0:rows_of(i)], None)
    ctx.close()


_INS = ["x_prompt", "x_sample", "state_pool", "cache_k", "cache_v", "cache_logf", "page_table", "c_prompt",
        "c_sample", "ada_w", "ada_b", "pre_g", "post_g", "a_in_w", "a_grp_w", "a_scale", "a_out_w", "kv_g",
        "kv_w", "f_b", "b_in_w", "b_out_w"]
_OUTS = [(1, SEQ, D), (NB, NT, D), (1, 1, HIST, W_A), (1, NB, HIST, W_A), (1, SEQ, NH, HD), (1, SEQ, NH, HD),
         (1, SEQ, NH), (NB, NT, NH, HD), (NB, NT, NH, HD), (NB, NT, NH)]


def kernel(**inputs):
    import numpy as _np
    import concourse.bacc as _bacc
    from concourse import mybir as _mybir
    from concourse.bass_utils import run_bass_kernel_spmd as _run

    nc = _bacc.Bacc("TRN2", target_bir_lowering=False, num_devices=1)
    arrays, args = {}, []
    for name in _INS:
        a = _np.ascontiguousarray(inputs[name])
        arrays[f"in_{name}_dram"] = a
        args.append(nc.dram_tensor(f"in_{name}_dram", a.shape, _mybir.dt.from_np(a.dtype), kind="ExternalInput").ap())
    for i, shape in enumerate(_OUTS):
        args.append(nc.dram_tensor(f"out_{i}_dram", shape, _mybir.dt.float32, kind="ExternalOutput").ap())
    build(nc, *args)
    r = _run(nc, [arrays], core_ids=[0])
    return tuple(r.results[0][f"out_{i}_dram"] for i in range(len(_OUTS)))
```

```python
from contextlib import ExitStack

import concourse.bass as bass
from concourse import mybir

ALU = mybir.AluOpType
ACT = mybir.ActivationFunctionType
AX_X = mybir.AxisListType.X
F32 = mybir.dt.float32
F32R = mybir.dt.float32r
I32 = mybir.dt.int32

P = 128
D = 1024
KD = D // P
SEQ = 1024
QB = SEQ // P
NB = 8
NT = 4
NS = NB * NT
T = SEQ + NS
TT = QB + 1
NCH = 3
CH = T // NCH
W_A = 2 * D
KA = W_A // P
WINDOWS = (2, 4, 8, 16)
NG = len(WINDOWS)
GT = KA // NG
HIST = max(WINDOWS) - 1
SEG = HIST + NT
UW = HIST + SEQ + NB * SEG
NCOND = 1 + NB
NH = 16
HD = 64
NP = NH // 2
PAGE = 128
NPG = 16
PAST = NPG * PAGE
NR = NH * NT
EPS = 1e-6
NEG = -1e30
BANK = 512
RAW = 2
SPL = 2
KR = 4
VR = 4


def rows_of(i):
    return P if i < QB else NS


def stream_weights(sp, w, jobs):
    for j, src in enumerate(jobs):
        stream_weight(sp, w, j, src)


def stream_weight(sp, w, j, src):
    if j >= RAW:
        sp.wait_ge(w["split"], j - RAW + 1)
    sp.dma_start(w["raw"][:, j % RAW, 0:src.shape[1], 0:src.shape[2]], src).then_inc(
        w["landed"][j % RAW], 16)


def split_weights(pool, w, jobs):
    for j, src in enumerate(jobs):
        kt = src.shape[1]
        raw, hi, lo = (w[n][:, j % r, 0:kt, :] for n, r in (("raw", RAW), ("hi", SPL), ("lo", SPL)))
        pool.wait_ge(w["landed"][j % RAW], 16 * (j // RAW + 1))
        if j >= SPL:
            pool.wait_ge(w["used"], j - SPL + 1)
        pool.tensor_copy(hi, raw).then_inc(w["hi_ready"], 1)
        pool.wait_ge(w["hi_ready"], j + 1)
        pool.tensor_tensor(lo, raw, hi.bitcast(F32), ALU.subtract).then_inc(w["split"], 1)


def product(pe, w, j, kt, acc, act_hi, act_lo, k0, first=True, last=True):
    pe.wait_ge(w["split"], j + 1)
    hi, lo = w["hi"], w["lo"]
    for k in range(kt):
        for s, (wt, act) in enumerate(((hi, act_hi), (hi, act_lo), (lo, act_hi))):
            for c in range(NCH):
                mm = pe.matmul(acc[:, c, 0:CH], wt[:, j % SPL, k, :], act[:, k0 + k, c * CH:(c + 1) * CH],
                               start=first and k == 0 and s == 0, stop=last and k == kt - 1 and s == 2)
    mm.then_inc(w["used"], 1)


def thirds(acc):
    return acc[:, :, 0:CH]


def as_thirds(ap):
    return ap.rearrange("p (c t) -> p c t", c=NCH)


def build(nc, x_prompt, x_sample, state_pool, cache_k, cache_v, cache_logf, page_table, c_prompt,
          c_sample, ada_w, ada_b, pre_g, post_g, a_in_w, a_grp_w, a_scale, a_out_w, kv_g, kv_w,
          f_b, b_in_w, b_out_w, y_prompt, y_sample, pool_prompt, pool_sample, k_prompt, v_prompt,
          logf_prompt, k_sample, v_sample, logf_sample):
    ctx = ExitStack()
    n_phys = cache_k.shape[0]
    base = (nc.sbuf_base + 31) // 32 * 32
    top = nc.sbuf_usable_end // 32 * 32
    size = {F32: 4, F32R: 4, I32: 4}

    class Arena:

        def __init__(self, at):
            self.at = at

        def take(self, name, shape, dt=F32):
            n = size[dt]
            for d in shape[1:]:
                n *= d
            t = nc.alloc_sbuf_tensor_at(name, shape, dt, offset=self.at)
            self.at = (self.at + n + 31) // 32 * 32
            assert self.at <= top, (name, self.at - top)
            return t

    stage_sems = []

    def sem(name):
        stage_sems.append(nc.alloc_semaphore(name))
        return stage_sems[-1]

    s_pout = [nc.alloc_semaphore(f"s_pout{i}") for i in range(2)]
    s_tout = [nc.alloc_semaphore(f"s_tout{i}") for i in range(2)]
    s_lout = nc.alloc_semaphore("s_lout")
    s_xout = [nc.alloc_semaphore(f"s_xout{i}") for i in range(2)]

    def end_stage():
        nc.clear_and_free_semaphores(list(stage_sems))
        stage_sems.clear()
        nc.all_engine_barrier()

    def scratch(name, shape):
        return nc.dram_tensor(name, shape, F32, kind="Internal").ap()

    gate_d = scratch("gate_d", (2, NCOND, D))
    g_d = scratch("g_d", (KA, P, T))
    x1_d = scratch("x1_d", (TT, P, D))
    qT_d = scratch("qT_d", (NP, P, T))
    kT_d = scratch("kT_d", (NP, P, T))
    zT_d = scratch("zT_d", (NP, P, T))
    negF_d = scratch("negF_d", (NH, SEQ))

    x_p = x_prompt.rearrange("a (t p) d -> p (a t) d", p=P)
    x_s = x_sample.rearrange("b t d -> (b t) d")
    yp = y_prompt.rearrange("a (t p) d -> p (a t) d", p=P)
    ys = y_sample.rearrange("b t d -> (b t) d")
    kp = k_prompt.rearrange("a (t p) h d -> p (a t) (h d)", p=P)
    vp = v_prompt.rearrange("a (t p) h d -> p (a t) (h d)", p=P)
    ks = k_sample.rearrange("b t h d -> (b t) (h d)")
    vs = v_sample.rearrange("b t h d -> (b t) (h d)")
    lfp = logf_prompt.rearrange("a (t p) h -> p (a t) h", p=P)
    lfs = logf_sample.rearrange("b t h -> (b t) h")

    def w_tiles(mat, k0, kt, n0, n):
        return mat[k0 * P:(k0 + kt) * P, n0:n0 + n].rearrange("(k p) n -> p k n", p=P)

    keep = Arena(base)
    ident = keep.take("ident", [P, P])
    modA = keep.take("modA", [P, 2, KD, NCOND])
    modB = keep.take("modB", [P, 2, KD, NCOND])
    kvg = keep.take("kvg", [P, KD])
    asc = keep.take("asc", [P, KA])
    sel_p = keep.take("sel_p", [NCOND, P])
    sel_s = keep.take("sel_s", [NCOND, NS])
    Ftok = keep.take("Ftok", [P, QB, NH])
    lf_s = keep.take("lf_s", [NS, NH])
    pt = keep.take("pt", [1, NB * NPG], I32)
    act_at = keep.at
    actH = keep.take("actH", [P, KA, T], F32R)
    actL_at = keep.at
    actL = keep.take("actL", [P, KA, T], F32R)
    free = keep.at

    K_at = top - (KR + VR) * D * 4
    LF_at = top - NPG * NB * NH * 4
    upper = Arena(LF_at)
    LF = upper.take("LF", [P, NPG, NB * NH])

    ps = ctx.enter_context(nc.psum_tensor("ps", [P, 8, BANK], F32))
    acc = [ps[:, 0:3, :], ps[:, 3:6, :]]

    def weight_ring(tag, arena):
        return {
            "raw": arena.take(f"w_raw_{tag}", [P, RAW, KD, P]),
            "hi": arena.take(f"w_hi_{tag}", [P, SPL, KD, P], F32R),
            "lo": arena.take(f"w_lo_{tag}", [P, SPL, KD, P], F32R),
            "landed": [sem(f"w_landed_{tag}{i}") for i in range(RAW)],
            "hi_ready": sem(f"w_hi_ready_{tag}"),
            "split": sem(f"w_split_{tag}"),
            "used": sem(f"w_used_{tag}"),
        }

    def chainer(name):
        s, n = sem(name), [0]

        def link(eng, ins):
            n[0] += 1
            ins.then_inc(s, 1)
            eng.wait_ge(s, n[0])
        return link

    def b_t(ap):
        return ap[:, :, 1:NCOND].unsqueeze(3).broadcast_to([P, KD, NB, NT])

    class NormedTranspose:

        BANKS = 4
        TMP = 4

        def __init__(self, tag, targets, tmp):
            self.targets, self.tmp = targets, tmp
            self.turned = sem(f"turned_{tag}")
            self.high = sem(f"high_{tag}")
            self.low = sem(f"low_{tag}")
            self.full = sem(f"full_{tag}")
            self.rounds = [(g, k) for g in range(QB // 4) for k in range(KD)]

        def pe(self, pe, x_tok, x_ready, x_count):
            nt = len(self.targets)
            for n, (g, k) in enumerate(self.rounds):
                pe.wait_ge(x_ready, x_count(4 * g + 3))
                if n >= self.BANKS:
                    pe.wait_ge(self.full, nt * (n - self.BANKS + 1))
                for i in range(4):
                    mm = pe.transpose(ps[:, n % self.BANKS, i * P:(i + 1) * P],
                                      x_tok[:, 4 * g + i, k * P:(k + 1) * P], ident[:, :])
                mm.then_inc(self.turned, 1)
            n = len(self.rounds)
            pe.wait_ge(x_ready, x_count(QB))
            pe.wait_ge(self.full, nt * (n - self.BANKS + 1))
            for k in range(KD):
                mm = pe.transpose(ps[:, n % self.BANKS, k * NS:(k + 1) * NS],
                                  x_tok[0:NS, QB, k * P:(k + 1) * P], ident[0:NS, 0:NS])
            mm.then_inc(self.turned, 1)

        def act(self, act):
            m = 0
            for g, k in self.rounds:
                for k0, A, B in self.targets:
                    act.wait_ge(self.full, m + 1)
                    act.copy(actH[:, k0 + k, g * BANK:(g + 1) * BANK], self.tmp[:, m % self.TMP, :]).then_inc(self.high, 1)
                    m += 1

        def dve(self, dve, link):
            tmp, m = self.tmp, 0

            def low(m, k0, g, k):
                cols = slice(g * BANK, (g + 1) * BANK)
                dve.wait_ge(self.high, m + 1)
                dve.tensor_tensor(actL[:, k0 + k, cols], tmp[:, m % self.TMP, :],
                                  actH[:, k0 + k, cols].bitcast(F32), ALU.subtract).then_inc(self.low, 1)

            behind = []
            for n, (g, k) in enumerate(self.rounds):
                dve.wait_ge(self.turned, n + 1)
                for k0, A, B in self.targets:
                    src, t = ps[:, n % self.BANKS, :], tmp[:, m % self.TMP, :]
                    if m >= self.TMP:
                        dve.wait_ge(self.low, m - self.TMP + 1)
                    if B is not None:
                        ins = dve.tensor_scalar(t, src, A[:, k, 0:1], B[:, k, 0:1], ALU.mult, ALU.add)
                    else:
                        ins = dve.tensor_scalar(t, src, A[:, k:k + 1], None, ALU.mult)
                    ins.then_inc(self.full, 1)
                    behind.append((m, k0, g, k))
                    m += 1
                    if len(behind) > 2:
                        low(*behind.pop(0))
            for b in behind:
                low(*b)
            dve.wait_ge(self.low, m)
            n = len(self.rounds)
            dve.wait_ge(self.turned, n + 1)
            src = ps[:, n % self.BANKS, 0:KD * NS]
            t = tmp[:, 0, 0:KD * NS]
            for k0, A, B in self.targets:
                hi, lo = (x[:, k0:k0 + KD, SEQ:T] for x in (actH, actL))
                v = t.rearrange("p (k b t) -> p k b t", k=KD, b=NB)
                s4 = src.rearrange("p (k b t) -> p k b t", k=KD, b=NB)
                for k in range(KD):
                    if B is not None:
                        bc = A[:, k, 1:NCOND].unsqueeze(2).broadcast_to([P, NB, NT])
                        link(dve, dve.tensor_tensor(v[:, k], s4[:, k], bc, ALU.mult))
                        bc = B[:, k, 1:NCOND].unsqueeze(2).broadcast_to([P, NB, NT])
                        link(dve, dve.tensor_tensor(v[:, k], v[:, k], bc, ALU.add))
                    else:
                        link(dve, dve.tensor_scalar(v[:, k], s4[:, k], A[:, k:k + 1], None, ALU.mult))
                t3 = t.rearrange("p (k n) -> p k n", k=KD)
                link(dve, dve.tensor_copy(hi, t3))
                link(dve, dve.tensor_tensor(lo, t3, hi.bitcast(F32), ALU.subtract))

    def stage_conditioning():
        a = Arena(free)
        crow = a.take("crow", [NCOND, D])
        srow = a.take("srow", [NCOND, D])
        scT = a.take("scT", [P, KD, NCOND])
        adab = a.take("adab", [NCOND, 2, BANK])
        mrow = a.take("mrow", [NCOND, 2, BANK])
        preg = a.take("preg", [P, 2, KD])
        x_tok = a.take("x_tok1", [P, TT, D])
        junk = a.take("junk1", [P, D])
        ss = a.take("ss1", [P, TT])
        rstd = a.take("rstd1", [P, TT])
        tmp = a.take("tmp1", [P, 4, BANK])
        adaw = Arena(actL_at + KD * T * 4).take("adaw", [P, 2, KD, BANK])

        chunks = [(l, n) for l in range(2) for n in range(3 * D // BANK)]
        s_c, s_small, s_x = sem("s_c"), sem("s_small"), sem("s_x")
        s_aw = [sem(f"s_aw{i}") for i in range(2)]
        s_ab = [sem(f"s_ab{i}") for i in range(2)]
        s_gate = [sem(f"s_gate{i}") for i in range(2)]
        s_const, s_id = sem("s_const"), sem("s_id")
        s_silu, s_cT, s_scT = sem("s_silu"), sem("s_cT"), sem("s_scT")
        s_m, s_mrow, s_mT, s_mod = sem("s_m"), sem("s_mrow"), sem("s_mT"), sem("s_mod")
        s_ss_init = sem("s_ss_init")
        s_ss, s_var, s_std, s_xn = sem("s_ss"), sem("s_var"), sem("s_std"), sem("s_xn")
        link = chainer("dve_chain1")
        alink = chainer("act_chain1")
        normed = NormedTranspose("l0", [(0, modA[:, 0], modB[:, 0])], tmp)
        GATE = 2 * D // BANK

        with nc.Block() as block:
            @block.sync
            def _(sp):
                sp.dma_start(crow[0:1, :], c_prompt).then_inc(s_c, 16)
                sp.dma_start(crow[1:NCOND, :], c_sample).then_inc(s_c, 16)
                with nc.allow_non_contiguous_dma(reason="small per-channel vectors"):
                    sp.dma_start(preg[:, :, :], pre_g.rearrange("l (k p) -> p l k", p=P)).then_inc(s_small, 16)
                    sp.dma_start(kvg[:, :], kv_g.rearrange("(k p) -> p k", p=P)).then_inc(s_small, 16)
                    sp.dma_start(asc[:, :], a_scale.rearrange("a (k p) -> p (a k)", p=P)).then_inc(s_small, 16)
                for j, (l, n) in enumerate(chunks):
                    if j >= 2:
                        sp.wait_ge(s_m, j - 1)
                        sp.wait_ge(s_mrow, j - 1)
                    sp.dma_start(adaw[:, j % 2], w_tiles(ada_w[l], 0, KD, n * BANK, BANK)).then_inc(s_aw[j % 2], 16)
                    sp.dma_start(adab[:, j % 2], ada_b[l:l + 1, n * BANK:(n + 1) * BANK].broadcast_to(
                        [NCOND, BANK])).then_inc(s_ab[j % 2], 16)
                    if j == 1:
                        sp.dma_start(x_tok[:, 0:QB, :], x_p).then_inc(s_x, 16)
                        sp.dma_start(x_tok[0:NS, QB, :], x_s).then_inc(s_x, 16)

            @block.gpsimd
            def _(pool):
                pool.memset(ident[:, :], 0.0).then_inc(s_id, 1)
                pool.memset(sel_p[:, :], 1.0).then_inc(s_id, 1)
                pool.memset(sel_s[:, :], 1.0).then_inc(s_id, 1)
                pool.wait_ge(s_id, 3)
                pool.affine_select(out=ident[:, :], in_=ident[:, :], compare_op=ALU.not_equal, fill=1.0,
                                   base=0, pattern=[[-1, P]], channel_multiplier=1).then_inc(s_const, 1)
                pool.affine_select(out=sel_p[:, :], in_=sel_p[:, :], compare_op=ALU.is_ge, fill=0.0,
                                   base=0, pattern=[[0, P]], channel_multiplier=-1).then_inc(s_const, 1)
                pool.affine_select(out=sel_s[:, :], in_=sel_s[:, :], compare_op=ALU.is_ge, fill=0.0,
                                   base=NT, pattern=[[1, NS]], channel_multiplier=-NT).then_inc(s_id, 1)
                pool.wait_ge(s_id, 4)
                pool.affine_select(out=sel_s[:, :], in_=sel_s[:, :], compare_op=ALU.is_ge, fill=0.0,
                                   base=-1, pattern=[[-1, NS]], channel_multiplier=NT).then_inc(s_const, 1)
                for j, (l, n) in enumerate(chunks):
                    if n >= GATE:
                        pool.wait_ge(s_mrow, j + 1)
                        pool.dma_start(gate_d[l, :, (n - GATE) * BANK:(n - GATE + 1) * BANK],
                                       mrow[:, j % 2]).then_inc(s_gate[j % 2], 16)
                pool.wait_ge(s_gate[0], 32)
                pool.wait_ge(s_gate[1], 32)

            @block.scalar
            def _(act):
                act.wait_ge(s_c, 32)
                act.activation(srow[:, :], crow[:, :], ACT.Silu).then_inc(s_silu, 1)
                act.wait_ge(s_x, 32)
                act.wait_ge(s_ss_init, 1)
                for i in range(TT):
                    r = rows_of(i)
                    if i:
                        act.wait_ge(s_ss, i)
                    act.activation(junk[0:r, :], x_tok[0:r, i, :], ACT.Square,
                                   accum_out=ss[0:r, i:i + 1]).then_inc(s_ss, 1)
                act.wait_ge(s_var, 1)
                act.activation(rstd[:, :], rstd[:, :], ACT.Sqrt).then_inc(s_std, 1)
                normed.act(act)

            @block.tensor
            def _(pe):
                pe.wait_ge(s_silu, 1)
                pe.wait_ge(s_const, 3)
                for k in range(KD):
                    mm = pe.transpose(ps[:, 4, k * NCOND:(k + 1) * NCOND], srow[:, k * P:(k + 1) * P],
                                      ident[0:NCOND, 0:NCOND])
                mm.then_inc(s_cT, 1)
                pe.wait_ge(s_scT, 1)

                turned = 0
                for j, (l, n) in enumerate(chunks):
                    pe.wait_ge(s_aw[j % 2], 16 * (j // 2 + 1))
                    if j >= 2:
                        pe.wait_ge(s_mrow, j - 1)
                    for k in range(KD):
                        mm = pe.matmul(ps[0:NCOND, 6 + j % 2, :], scT[:, k, :], adaw[:, j % 2, k, :],
                                       start=(k == 0), stop=(k == KD - 1))
                    mm.then_inc(s_m, 1)
                    if n < GATE:
                        pe.wait_ge(s_mrow, j + 1)
                        if turned:
                            pe.wait_ge(s_mod, turned)
                        for i in range(BANK // P):
                            mm = pe.transpose(ps[:, 5, i * NCOND:(i + 1) * NCOND],
                                              mrow[:, j % 2, i * P:(i + 1) * P], ident[0:NCOND, 0:NCOND])
                        mm.then_inc(s_mT, 1)
                        turned += 1
                normed.pe(pe, x_tok, s_xn, lambda i: i + 1)

            @block.vector
            def _(dve):
                dve.memset(ss[:, :], 1.0).then_inc(s_ss_init, 1)
                dve.wait_ge(s_cT, 1)
                dve.tensor_copy(scT[:, :, :], ps[:, 4, 0:KD * NCOND].rearrange("p (k c) -> p k c", k=KD)).then_inc(s_scT, 1)
                turned = 0
                gates = [0, 0]
                for j, (l, n) in enumerate(chunks):
                    dve.wait_ge(s_m, j + 1)
                    dve.wait_ge(s_ab[j % 2], 16 * (j // 2 + 1))
                    if gates[j % 2]:
                        dve.wait_ge(s_gate[j % 2], 16 * gates[j % 2])
                    if turned:
                        dve.wait_ge(s_mT, turned)
                    dve.tensor_tensor(mrow[:, j % 2], ps[0:NCOND, 6 + j % 2, :], adab[:, j % 2], ALU.add).then_inc(s_mrow, 1)
                    if n >= GATE:
                        gates[j % 2] += 1
                        continue
                    turned += 1
                    dve.wait_ge(s_mT, turned)
                    for i in range(BANK // P):
                        k = (n % 2) * (BANK // P) + i
                        src = ps[:, 5, i * NCOND:(i + 1) * NCOND]
                        if n < D // BANK:
                            ins = dve.tensor_copy(modB[:, l, k, :], src)
                        else:
                            if turned == 3 and i == 0:
                                dve.wait_ge(s_small, 48)
                            ins = dve.tensor_scalar(modA[:, l, k, :], src, 1.0, preg[:, l, k:k + 1], ALU.add, ALU.mult)
                    ins.then_inc(s_mod, 1)
                dve.wait_ge(s_ss, TT)
                dve.tensor_scalar(rstd[:, :], ss[:, :], 1.0 / D, EPS, ALU.mult, ALU.add).then_inc(s_var, 1)
                dve.wait_ge(s_std, 1)
                link(dve, dve.reciprocal(rstd[:, :], rstd[:, :]))
                for i in range(TT):
                    r = rows_of(i)
                    dve.tensor_scalar(x_tok[0:r, i, :], x_tok[0:r, i, :], rstd[0:r, i:i + 1], None,
                                      ALU.mult).then_inc(s_xn, 1)
                dve.wait_ge(s_mod, turned)
                normed.dve(dve, link)

    def stage_pooling():
        a = Arena(free)
        w = weight_ring("a", a)
        U = a.take("U", [P, 2, UW])
        win = a.take("win", [P, 2, UW])
        pooled = a.take("pooled", [P, T])
        sz = a.take("sz", [P, 2, T])
        g = a.take("g", [P, 2, T])
        hist = Arena(actL_at + (KD + GT) * T * 4).take("hist", [NB * HIST, W_A])
        pk = a.take("pk", [P, 2, HIST + NB * HIST])
        po_p = a.take("po_p", [HIST, 2, P])
        po_s = a.take("po_s", [NB * HIST, 2, P])
        inv = a.take("inv", [P, HIST])

        PH = KD
        jobs, kinds = [], []
        for gr in range(NG):
            c0 = gr * GT * P
            for i in range(GT):
                jobs.append(w_tiles(a_in_w[0], 0, KD, c0 + i * P, P))
                kinds.append(("u", gr, i))
            for i0 in range(0, GT, 2):
                for i in (i0, i0 + 1):
                    jobs.append(w_tiles(a_in_w[0], 0, KD, W_A + c0 + i * P, P))
                    kinds.append(("z", gr, i))
                for i in (i0, i0 + 1):
                    jobs.append(w_tiles(a_grp_w[0, gr], 0, GT, i * P, P))
                    kinds.append(("m", gr, i))

        s_hist, s_inv, s_pad = sem("s_hist"), sem("s_inv"), sem("s_pad")
        s_hT, s_hU = sem("s_hT"), sem("s_hU")
        s_U = sem("s_U")
        s_pooled, s_ph, s_pl = sem("s_pooled"), sem("s_ph"), sem("s_pl")
        s_pk, s_pkT, s_pkfree = sem("s_pk"), sem("s_pkT"), sem("s_po")
        s_sz, s_g = sem("s_sz"), sem("s_g")
        s_gout = [sem(f"s_gout{i}") for i in range(2)]
        link = chainer("dve_chain2")
        U_s = [U[:, i, HIST + SEQ:UW].rearrange("p (b s) -> p b s", s=SEG) for i in range(2)]
        W_s = [win[:, i, HIST + SEQ:UW].rearrange("p (b s) -> p b s", s=SEG) for i in range(2)]

        with nc.Block() as block:
            @block.sync
            def _(sp):
                sp.dma_start(hist[:, :], state_pool[0].rearrange("b r c -> (b r) c")).then_inc(s_hist, 16)
                stream_weights(sp, w, jobs)

            @block.gpsimd
            def _(pool):
                for t in range(HIST):
                    pool.memset(inv[:, t:t + 1], 1.0 / (t + 1)).then_inc(s_inv, 1)
                for i in range(2):
                    pool.memset(U[:, i, 0:HIST], 0.0).then_inc(s_pad, 1)
                    pool.memset(win[:, i, :], 0.0).then_inc(s_pad, 1)
                split_weights(pool, w, jobs)

            @block.tensor
            def _(pe):
                def finish_tile(j):
                    pe.wait_ge(s_pk, j + 1)
                    if j:
                        pe.wait_ge(s_pkfree, 2 * j)
                    pe.transpose(ps[0:HIST, 7, 0:P], pk[:, j % 2, 0:HIST], ident[:, :])
                    pe.transpose(ps[0:NB * HIST, 7, P:2 * P], pk[:, j % 2, HIST:], ident[:, :]).then_inc(s_pkT, 1)

                pe.wait_ge(s_hist, 16)
                late = None
                for n, (kind, gr, i) in enumerate(kinds):
                    j = gr * GT + i
                    if kind == "u":
                        if j:
                            pe.wait_ge(s_hU, j)
                        pe.transpose(ps[:, 6, 0:NB * HIST], hist[:, j * P:(j + 1) * P],
                                     ident[0:NB * HIST, 0:NB * HIST]).then_inc(s_hT, 1)
                    if n >= 2:
                        was, gw, iw = kinds[n - 2]
                        pe.wait_ge({"u": s_U, "z": s_sz, "m": s_g}[was], gw * GT + iw + 1)
                    if kind == "m":
                        pe.wait_ge(s_pl, (gr + 1) * GT)
                        product(pe, w, n, GT, acc[n % 2], actH, actL, PH)
                    else:
                        product(pe, w, n, KD, acc[n % 2], actH, actL, 0)
                    if late is not None:
                        finish_tile(late)
                    late = j if kind == "u" else None

            @block.scalar
            def _(act):
                late_u, late_g = [], []

                def finish_tile(j):
                    act.wait_ge(s_pkT, j + 1)
                    if j >= 2:
                        act.wait_ge(s_pout[j % 2], 32 * (j // 2))
                    act.copy(po_p[:, j % 2], ps[0:HIST, 7, 0:P]).then_inc(s_pkfree, 1)
                    act.copy(po_s[:, j % 2], ps[0:NB * HIST, 7, P:2 * P]).then_inc(s_pkfree, 1)
                    act.wait_ge(s_pkfree, 2 * (j + 1))
                    c = slice(j * P, (j + 1) * P)
                    act.dma_start(pool_prompt[0, 0, :, c], po_p[:, j % 2]).then_inc(s_pout[j % 2], 16)
                    act.dma_start(pool_sample[0].rearrange("b r c -> (b r) c")[:, c],
                                  po_s[:, j % 2]).then_inc(s_pout[j % 2], 16)

                def store_g(j):
                    act.wait_ge(s_g, j + 1)
                    act.dma_start(g_d[j], g[:, j % 2]).then_inc(s_gout[j % 2], 16)

                for n, (kind, gr, i) in enumerate(kinds):
                    j = gr * GT + i
                    A = acc[n % 2]
                    if kind == "m":
                        late_g.append(j)
                        continue
                    act.wait_ge(w["used"], n + 1)
                    if kind == "u":
                        if j < 2:
                            act.wait_ge(s_pad, 4)
                        else:
                            act.wait_ge(s_pk, j - 1)
                        act.copy(U[:, j % 2, HIST:HIST + 2 * CH].rearrange("p (c t) -> p c t", c=2),
                                 A[:, 0:2, 0:CH])
                        act.copy(U[:, j % 2, HIST + 2 * CH:HIST + SEQ], A[:, 2, 0:SEQ - 2 * CH])
                        act.copy(U_s[j % 2][:, :, HIST:SEG],
                                 A[:, 2, SEQ - 2 * CH:CH].rearrange("p (b t) -> p b t", b=NB)).then_inc(s_U, 1)
                        act.wait_ge(s_pooled, j + 1)
                        act.copy(actH[:, PH + i, :], pooled[:, :]).then_inc(s_ph, 1)
                        late_u.append(j)
                    else:
                        if j >= 2:
                            act.wait_ge(s_g, j - 1)
                        act.activation(as_thirds(sz[:, j % 2]), thirds(A), ACT.Silu).then_inc(s_sz, 1)
                    while late_u and (late_u[0] < j or kind != "u"):
                        finish_tile(late_u.pop(0))
                    while late_g and late_g[0] < j - 1:
                        store_g(late_g.pop(0))
                for j in late_g:
                    store_g(j)
                for i in range(2):
                    act.wait_ge(s_gout[i], 16 * KA // 2)
                    act.wait_ge(s_pout[i], 32 * KA // 2)

            @block.vector
            def _(dve):
                dve.wait_ge(s_inv, HIST)
                dve.wait_ge(s_pad, 4)
                for n, (kind, gr, i) in enumerate(kinds):
                    j = gr * GT + i
                    u = U[:, j % 2]
                    if kind == "u":
                        size_w = WINDOWS[gr]
                        dve.wait_ge(s_hT, j + 1)
                        dve.tensor_copy(U_s[j % 2][:, :, 0:HIST],
                                        ps[:, 6, 0:NB * HIST].rearrange("p (b r) -> p b r", b=NB)).then_inc(s_hU, 1)
                        dve.wait_ge(s_hU, j + 1)
                        dve.wait_ge(s_U, j + 1)
                        src, step, at = u, 1, 0
                        while step < size_w:
                            lo = 2 * step - 1
                            link(dve, dve.tensor_tensor(win[:, at, lo:UW], src[:, lo:UW], src[:, lo - step:UW - step], ALU.add))
                            src, ws, at, step = win[:, at], W_s[at], 1 - at, 2 * step
                        if j:
                            dve.wait_ge(s_ph, j)
                            dve.wait_ge(s_pl, j)
                        link(dve, dve.scalar_tensor_tensor(
                            out=pooled[:, 0:SEQ], in0=src[:, HIST:HIST + SEQ], scalar=1.0 / size_w,
                            in1=u[:, HIST:HIST + SEQ], op0=ALU.mult, op1=ALU.subtract))
                        cut = size_w - 1
                        link(dve, dve.tensor_tensor(pooled[:, 0:cut], src[:, HIST:HIST + cut], inv[:, 0:cut], ALU.mult))
                        link(dve, dve.tensor_tensor(pooled[:, 0:cut], pooled[:, 0:cut], u[:, HIST:HIST + cut], ALU.subtract))
                        dve.scalar_tensor_tensor(
                            out=pooled[:, SEQ:T].rearrange("p (b t) -> p b t", b=NB), in0=ws[:, :, HIST:SEG],
                            scalar=1.0 / size_w, in1=U_s[j % 2][:, :, HIST:SEG], op0=ALU.mult,
                            op1=ALU.subtract).then_inc(s_pooled, 1)
                        if j >= 2:
                            dve.wait_ge(s_pkT, j - 1)
                        dve.tensor_copy(pk[:, j % 2, 0:HIST], u[:, SEQ:SEQ + HIST])
                        dve.tensor_copy(pk[:, j % 2, HIST:].rearrange("p (b r) -> p b r", b=NB),
                                        U_s[j % 2][:, :, NT:SEG]).then_inc(s_pk, 1)
                        dve.wait_ge(s_ph, j + 1)
                        dve.tensor_tensor(actL[:, PH + i, :], pooled[:, :], actH[:, PH + i, :].bitcast(F32),
                                          ALU.subtract).then_inc(s_pl, 1)
                    elif kind == "m":
                        dve.wait_ge(w["used"], n + 1)
                        dve.wait_ge(s_sz, j + 1)
                        if j >= 2:
                            dve.wait_ge(s_gout[j % 2], 16 * (j // 2))
                        dve.scalar_tensor_tensor(out=as_thirds(g[:, j % 2]), in0=thirds(acc[n % 2]),
                                                 scalar=asc[:, j:j + 1], in1=as_thirds(sz[:, j % 2]),
                                                 op0=ALU.mult, op1=ALU.mult).then_inc(s_g, 1)

    class TokenRows:

        PARTS = (range(0, 4), range(4, 8), range(8, 9))

        def __init__(self, tag):
            self.turned = sem(f"rows_turned_{tag}")
            self.read = sem(f"rows_read_{tag}")

        def pe(self, pe, m, src):
            for q, tiles in enumerate(self.PARTS):
                c = 3 * m + q
                bank = 6 + c % 2
                if c >= 2:
                    pe.wait_ge(self.read, c - 1)
                for i in tiles:
                    r = rows_of(i)
                    mm = pe.transpose(ps[0:r, bank, (i % 4) * P:(i % 4 + 1) * P],
                                      src[:, i * P:i * P + r], ident[:, :])
                mm.then_inc(self.turned, 1)

        def dve(self, dve, m, dst):
            for q, tiles in enumerate(self.PARTS):
                bank = 6 + (3 * m + q) % 2
                dve.wait_ge(self.turned, 3 * m + q + 1)
                r = rows_of(tiles[0])
                dve.tensor_copy(dst[0:r, tiles[0]:tiles[-1] + 1, :],
                                ps[0:r, bank, 0:len(tiles) * P].rearrange("p (i n) -> p i n", n=P)).then_inc(self.read, 1)

    def stage_out(tag, mat, halves, y_tok, a, mov_hi, mov_lo, load, keep_src):
        w = weight_ring(tag, a)
        yT = a.take(f"yT_{tag}", [P, 2, T])
        nk = halves * KD
        if load is not None:
            src = Arena(y_at).take(f"mov_{tag}", [P, 4, T])
            s_in = [sem(f"s_in_{tag}{i}") for i in range(4)]
        jobs = [w_tiles(mat, h * KD, KD, n * P, P) for n in range(KD) for h in range(halves)]
        s_high, s_low = sem(f"s_high_{tag}"), sem(f"s_low_{tag}")
        s_yT = sem(f"s_yT_{tag}")
        rows = TokenRows(tag)

        def moving(k):
            return src[:, k % 4] if load is not None else keep_src[:, k]

        with nc.Block() as block:
            @block.sync
            def _(sp):
                def load_moving(k):
                    if k >= 4:
                        sp.wait_ge(s_low, k - 3)
                    sp.dma_start(src[:, k % 4], load[k]).then_inc(s_in[k % 4], 16)

                if load is not None:
                    for k in range(nk):
                        load_moving(k)
                stream_weights(sp, w, jobs)

            @block.gpsimd
            def _(pool):
                split_weights(pool, w, jobs)

            @block.tensor
            def _(pe):
                for n in range(KD):
                    if n >= 2:
                        pe.wait_ge(s_yT, n - 1)
                    for h in range(halves):
                        if n == 0:
                            pe.wait_ge(s_low, (h + 1) * KD)
                        product(pe, w, n * halves + h, KD, acc[n % 2], mov_hi, mov_lo, h * KD,
                                first=h == 0, last=h == halves - 1)
                    if n:
                        pe.wait_ge(s_yT, n)
                        rows.pe(pe, n - 1, yT[:, (n - 1) % 2])
                pe.wait_ge(s_yT, KD)
                rows.pe(pe, KD - 1, yT[:, (KD - 1) % 2])

            @block.scalar
            def _(act):
                for k in range(nk):
                    if load is not None:
                        act.wait_ge(s_in[k % 4], 16 * (k // 4 + 1))
                    act.copy(mov_hi[:, k, :], moving(k)).then_inc(s_high, 1)
                for n in range(KD):
                    act.wait_ge(w["used"], (n + 1) * halves)
                    if n >= 2:
                        act.wait_ge(rows.turned, 3 * (n - 1))
                    act.copy(as_thirds(yT[:, n % 2]), thirds(acc[n % 2])).then_inc(s_yT, 1)

            @block.vector
            def _(dve):
                for k in range(nk):
                    dve.wait_ge(s_high, k + 1)
                    dve.tensor_tensor(mov_lo[:, k, :], moving(k), mov_hi[:, k, :].bitcast(F32),
                                      ALU.subtract).then_inc(s_low, 1)
                for n in range(KD):
                    rows.dve(dve, n, y_tok[:, :, n * P:(n + 1) * P])

    y_at = free

    def stage_residual(layer, y_tok, a, x_src, targets):
        tag = f"res{layer}"
        grow = a.take(f"grow{layer}", [NCOND, D])
        postg = a.take(f"postg{layer}", [P, D])
        G = a.take(f"G{layer}", [P, 2, D])
        x_in = a.take(f"x_in{layer}", [P, 2, D])
        junk = a.take(f"junk{layer}", [P, D])
        ss = a.take(f"ssr{layer}", [P, 2, TT])
        rstd = a.take(f"rstdr{layer}", [P, 2, TT])
        s_g, s_gm, s_G = sem(f"s_gin_{tag}"), sem(f"s_gm_{tag}"), sem(f"s_G_{tag}")
        s_in = [sem(f"s_xin_{tag}{i}") for i in range(2)]
        s_init, s_ss, s_var, s_std = (sem(f"{n}_{tag}") for n in ("s_init", "s_ss", "s_var", "s_std"))
        s_new, s_xn, s_out = sem(f"s_new_{tag}"), sem(f"s_xn_{tag}"), s_xout[layer]
        link = chainer(f"dve_chain_{tag}")
        normed = None
        if targets:
            normed = NormedTranspose(f"l{layer + 1}", targets, a.take(f"tmpr{layer}", [P, 4, BANK]))

        with nc.Block() as block:
            @block.sync
            def _(sp):
                sp.dma_start(grow[:, :], gate_d[layer]).then_inc(s_g, 16)
                sp.dma_start(postg[:, :], post_g[layer:layer + 1, :].broadcast_to([P, D])).then_inc(s_g, 16)
                for i in range(TT):
                    if i >= 2:
                        sp.wait_ge(s_new, i - 1)
                    sp.dma_start(x_in[0:rows_of(i), i % 2, :], x_src(i)).then_inc(s_in[i % 2], 16)

            @block.tensor
            def _(pe):
                pe.wait_ge(s_g, 32)
                for h in range(2):
                    c = slice(h * BANK, (h + 1) * BANK)
                    pe.matmul(ps[:, h, :], sel_p[:, :], grow[:, c], start=True, stop=True).then_inc(s_gm, 1)
                    pe.matmul(ps[0:NS, 2 + h, :], sel_s[:, :], grow[:, c], start=True, stop=True).then_inc(s_gm, 1)
                if normed:
                    pe.wait_ge(s_G, 4)
                    normed.pe(pe, y_tok, s_xn, lambda i: i + 1)

            @block.scalar
            def _(act):
                act.wait_ge(s_init, 1)
                for i in range(TT):
                    r = rows_of(i)
                    if i:
                        act.wait_ge(s_ss, i)
                    act.activation(junk[0:r, :], y_tok[0:r, i, :], ACT.Square,
                                   accum_out=ss[0:r, 0, i:i + 1]).then_inc(s_ss, 1)
                act.wait_ge(s_var, 1)
                act.activation(rstd[:, 0], rstd[:, 0], ACT.Sqrt).then_inc(s_std, 1)
                for i in range(TT):
                    r = rows_of(i)
                    act.wait_ge(s_new, i + 1)
                    if normed:
                        act.dma_start(x1_d[i, 0:r], y_tok[0:r, i, :]).then_inc(s_out, 16)
                        act.wait_ge(s_ss, TT + i)
                        act.activation(junk[0:r, :], y_tok[0:r, i, :], ACT.Square,
                                       accum_out=ss[0:r, 1, i:i + 1]).then_inc(s_ss, 1)
                    else:
                        act.dma_start(yp[:, i, :] if i < QB else ys, y_tok[0:r, i, :]).then_inc(s_out, 16)
                if normed:
                    act.wait_ge(s_var, 2)
                    act.activation(rstd[:, 1], rstd[:, 1], ACT.Sqrt).then_inc(s_std, 1)
                    normed.act(act)
                act.wait_ge(s_out, 16 * TT)

            @block.vector
            def _(dve):
                dve.memset(ss[:, :, :], 1.0).then_inc(s_init, 1)
                for h in range(2):
                    c = slice(h * BANK, (h + 1) * BANK)
                    for q, r in ((0, P), (1, NS)):
                        dve.wait_ge(s_gm, 2 * h + q + 1)
                        dve.tensor_tensor(G[0:r, q, c], ps[0:r, 2 * q + h, :], postg[0:r, c], ALU.mult).then_inc(s_G, 1)
                dve.wait_ge(s_ss, TT)
                dve.tensor_scalar(rstd[:, 0], ss[:, 0], 1.0 / D, EPS, ALU.mult, ALU.add).then_inc(s_var, 1)
                dve.wait_ge(s_std, 1)
                link(dve, dve.reciprocal(rstd[:, 0], rstd[:, 0]))
                dve.wait_ge(s_G, 4)
                for i in range(TT):
                    r, q = rows_of(i), i // QB
                    link(dve, dve.scalar_tensor_tensor(out=y_tok[0:r, i, :], in0=y_tok[0:r, i, :],
                                                       scalar=rstd[0:r, 0, i:i + 1], in1=G[0:r, q, :],
                                                       op0=ALU.mult, op1=ALU.mult))
                    dve.wait_ge(s_in[i % 2], 16 * (i // 2 + 1))
                    dve.tensor_tensor(y_tok[0:r, i, :], y_tok[0:r, i, :], x_in[0:r, i % 2, :], ALU.add).then_inc(s_new, 1)
                if normed:
                    dve.wait_ge(s_ss, 2 * TT)
                    dve.tensor_scalar(rstd[:, 1], ss[:, 1], 1.0 / D, EPS, ALU.mult, ALU.add).then_inc(s_var, 1)
                    dve.wait_ge(s_std, 2)
                    link(dve, dve.reciprocal(rstd[:, 1], rstd[:, 1]))
                    dve.wait_ge(s_out, 16 * TT)
                    for i in range(TT):
                        r = rows_of(i)
                        dve.tensor_scalar(y_tok[0:r, i, :], y_tok[0:r, i, :], rstd[0:r, 1, i:i + 1], None,
                                          ALU.mult).then_inc(s_xn, 1)
                    normed.dve(dve, link)

    def stage_projections():
        a = Arena(free)
        w = weight_ring("c", a)
        o = a.take("o", [P, 2, T])
        tk = a.take("tk", [P, 2, TT, P])
        fx = a.take("fx", [NH, T])
        fe = a.take("fe", [NH, T])
        lfT = a.take("lfT", [NH, T])
        F = a.take("F", [NH, SEQ])
        fb = a.take("fb", [NH, 1])
        lrow = a.take("lrow", [P, TT, NH])
        kinds = [("k", p) for p in range(NP)] + [(x, p) for x in "vqz" for p in range(NP)]
        kinds.insert(2, ("f", 0))
        W = NH * HD
        col = {"k": (kv_w, 0), "v": (kv_w, W), "f": (kv_w, 2 * W), "q": (b_in_w[0], 0), "z": (b_in_w[0], W)}
        jobs = [w_tiles(col[x][0], 0, KD, col[x][1] + p * P, NH if x == "f" else P) for x, p in kinds]
        tiles = [x for x in kinds if x[0] != "f"]
        order = {x: m for m, x in enumerate(tiles)}
        turn = {x: m for m, x in enumerate(t for t in tiles if t[0] in "kv")}
        store = {"k": kT_d, "q": qT_d, "z": zT_d}

        assert a.at <= LF_at
        s_pt, s_lfc = sem("s_pt"), sem("s_lfc")
        s_o = sem("s_o")
        s_oout = [sem(f"s_oout{i}") for i in range(2)]
        s_fb, s_fx, s_fe, s_lf, s_F, s_ones = (sem(n) for n in ("s_fb", "s_fx", "s_fe", "s_lf", "s_F", "s_ones"))
        s_lT, s_lrow = sem("s_lT"), sem("s_lrow")
        link, alink = chainer("dve_chain4"), chainer("act_chain4")
        rows = TokenRows("c")
        outs_before = {}
        count = [0, 0]
        for x, m in order.items():
            outs_before[x] = count[m % 2]
            count[m % 2] += x[0] in store

        def store_rows(act, x):
            t = turn[x]
            act.wait_ge(rows.read, 3 * (t + 1))
            big, small = (kp, ks) if x[0] == "k" else (vp, vs)
            c = slice(x[1] * P, (x[1] + 1) * P)
            act.dma_start(big[:, :, c], tk[:, t % 2, 0:QB, :]).then_inc(s_tout[t % 2], 16)
            act.dma_start(small[:, c], tk[0:NS, t % 2, QB, :]).then_inc(s_tout[t % 2], 16)

        with nc.Block() as block:
            @block.sync
            def _(sp):
                with nc.allow_non_contiguous_dma(reason="one value a head"):
                    sp.dma_start(fb[:, :], f_b.rearrange("(h a) -> h a", a=1)).then_inc(s_fb, 16)
                sp.dma_start(pt[:, :], page_table.rearrange("(a b) g -> a (b g)", a=1)).then_inc(s_pt, 16)
                sp.wait_ge(s_pt, 16)
                reg = sp.alloc_register("page4")
                for j, src in enumerate(jobs):
                    stream_weight(sp, w, j, src)
                    for t in range(4 * j, min(4 * j + 4, NB * NPG)):
                        sp.reg_load(reg, pt[0:1, t:t + 1])
                        page = bass.ds(sp.snap(reg, min_val=0, max_val=n_phys - 1), 1)
                        sp.dma_start(LF[:, t % NPG, t // NPG * NH:(t // NPG + 1) * NH],
                                     cache_logf[page].rearrange("a k h -> (a k) h")).then_inc(s_lfc, 16)
                sp.wait_ge(s_lfc, 16 * NB * NPG)

            @block.gpsimd
            def _(pool):
                split_weights(pool, w, jobs)

            @block.tensor
            def _(pe):
                late = None
                for n, x in enumerate(kinds):
                    if n >= 2:
                        was = kinds[n - 2]
                        if was[0] == "f":
                            pe.wait_ge(s_fx, 1)
                        else:
                            pe.wait_ge(s_o, order[was] + 1)
                    product(pe, w, n, KD, acc[n % 2], actH, actL, 0 if x[0] in "kvf" else KD)
                    if late:
                        pe.wait_ge(s_o, order[late] + 1)
                        rows.pe(pe, turn[late], o[:, order[late] % 2])
                    late = x if x[0] in "kv" else None
                pe.wait_ge(s_lf, 1)
                pe.wait_ge(s_F, 1)
                pe.wait_ge(s_o, len(tiles))
                for i in range(TT):
                    r = rows_of(i)
                    mm = pe.transpose(ps[0:r, 0, i * NH:(i + 1) * NH], lfT[:, i * P:i * P + r], ident[0:NH, 0:NH])
                for i in range(QB):
                    mm = pe.transpose(ps[:, 0, (TT + i) * NH:(TT + i + 1) * NH], F[:, i * P:(i + 1) * P],
                                      ident[0:NH, 0:NH])
                mm.then_inc(s_lT, 1)

            @block.scalar
            def _(act):
                late = None
                for n, x in enumerate(kinds):
                    if x[0] == "f":
                        act.wait_ge(s_fx, 1)
                        alink(act, act.activation(fe[:, :], fx[:, :], ACT.Abs))
                        alink(act, act.activation(fe[:, :], fe[:, :], ACT.Exp, scale=-1.0))
                        act.activation(fe[:, :], fe[:, :], ACT.Ln, bias=1.0).then_inc(s_fe, 1)
                        continue
                    m = order[x]
                    act.wait_ge(w["used"], n + 1)
                    if outs_before[x]:
                        act.wait_ge(s_oout[m % 2], 16 * outs_before[x])
                    if m >= 2 and tiles[m - 2][0] in "kv":
                        act.wait_ge(rows.turned, 3 * (turn[tiles[m - 2]] + 1))
                    dst, src = as_thirds(o[:, m % 2]), thirds(acc[n % 2])
                    if x[0] == "z":
                        act.activation(dst, src, ACT.Silu).then_inc(s_o, 1)
                    elif x[0] == "q":
                        act.activation(dst, src, ACT.Copy, scale=HD ** -0.5).then_inc(s_o, 1)
                    else:
                        act.copy(dst, src).then_inc(s_o, 1)
                    if late:
                        store_rows(act, late)
                    late = x if x[0] in "kv" else None
                    if x[0] in store:
                        act.wait_ge(s_o, m + 1)
                        act.dma_start(store[x[0]][x[1]], o[:, m % 2]).then_inc(s_oout[m % 2], 16)
                act.wait_ge(s_F, 1)
                act.wait_ge(s_lrow, 1)
                act.dma_start(negF_d, fe[:, 0:SEQ]).then_inc(s_lout, 16)
                act.dma_start(lfp, lrow[:, 0:QB, :]).then_inc(s_lout, 16)
                act.dma_start(lfs, lrow[0:NS, QB, :]).then_inc(s_lout, 16)
                act.wait_ge(s_lout, 48)
                for i in range(2):
                    act.wait_ge(s_oout[i], 16 * count[i])
                    act.wait_ge(s_tout[i], 32 * NP)

            @block.vector
            def _(dve):
                dve.memset(F[:, :], 1.0).then_inc(s_ones, 1)
                for n, x in enumerate(kinds):
                    if x[0] == "f":
                        dve.wait_ge(w["used"], n + 1)
                        dve.wait_ge(s_fb, 16)
                        dve.tensor_scalar(as_thirds(fx[:, :]), acc[n % 2][0:NH, :, 0:CH], fb[:, 0:1], None,
                                          ALU.add).then_inc(s_fx, 1)
                        dve.wait_ge(s_fe, 1)
                        dve.wait_ge(s_fx, 1)
                        link(dve, dve.tensor_scalar(fx[:, :], fx[:, :], 0.0, None, ALU.min))
                        dve.tensor_tensor(lfT[:, :], fx[:, :], fe[:, :], ALU.subtract).then_inc(s_lf, 1)
                        dve.wait_ge(s_lf, 1)
                        dve.wait_ge(s_ones, 1)
                        link(dve, dve.tensor_tensor_scan(fx[:, 0:SEQ], F[:, :], lfT[:, 0:SEQ], 0.0,
                                                         op0=ALU.mult, op1=ALU.add))
                        link(dve, dve.tensor_scalar(fe[:, 0:SEQ], fx[:, 0:SEQ], -1.0, None, ALU.mult))
                        dve.tensor_copy(F[:, :], fx[:, 0:SEQ]).then_inc(s_F, 1)
                    elif x[0] in "kv":
                        t = turn[x]
                        if t >= 2:
                            dve.wait_ge(s_tout[t % 2], 32 * (t // 2))
                        rows.dve(dve, t, tk[:, t % 2])
                dve.wait_ge(s_lT, 1)
                link(dve, dve.tensor_copy(lrow[:, 0:QB, :], ps[:, 0, 0:QB * NH].rearrange("p (i h) -> p i h", h=NH)))
                link(dve, dve.tensor_copy(lf_s[:, :], ps[0:NS, 0, QB * NH:TT * NH]))
                link(dve, dve.tensor_copy(Ftok[:, :, :], ps[:, 0, TT * NH:(TT + QB) * NH].rearrange(
                    "p (i h) -> p i h", h=NH)))
                dve.tensor_copy(lrow[0:NS, QB, :], lf_s[:, :]).then_inc(s_lrow, 1)

    def stage_attention(og):
        a = Arena(og_end)
        KT = a.take("KT", [P, 2, D])
        qT = a.take("qT", [P, 2, SEQ])
        kT = a.take("kT", [P, 2, SEQ])
        zT = a.take("zT", [P, 2, SEQ])
        Vt = a.take("Vt", [P, 2, QB, P])
        nF = a.take("nF", [P, 2, SEQ])
        Sb = [a.take("S_long", [P, SEQ]), a.take("S_short", [P, BANK])]
        PT = [a.take("PT_long", [P, SEQ]), a.take("PT_short", [P, BANK])]
        o_tok = a.take("o_tok", [P, 2, QB, P])
        nmax = a.take("nmax", [P, 4])
        rsum = a.take("rsum", [P, 4])
        rinv = a.take("rinv", [P, 4])
        q_s = a.take("q_s", [P, NP, NS])
        k_s = a.take("k_s", [P, NP, NS])
        z_s = a.take("z_s", [P, NP, NS])
        v_s = a.take("v_s", [NS, D])
        QW = NR + 2 * NT
        qst = a.take("qst", [P, NB, NP * QW])
        newT = a.take("newT", [NS, NB, NP, 2 * NT])
        Sd = a.take("Sd", [NR, 2, PAST + NS])
        PTd = a.take("PTd", [P, NPG, NR])
        PTn = a.take("PTn", [NS, NR])
        O_sb = a.take("O_sb", [NR, D])
        E_all = a.take("E_all", [P, NB, NR])
        G = a.take("Gf", [P, PAST + NS])
        nmask = a.take("nmask", [NR, 2 * NS - NT])
        dstat = a.take("dstat", [NR, 2, 4])
        assert a.at <= K_at, a.at - K_at
        a = Arena(K_at)
        K = a.take("K", [P, KR, D])
        V = a.take("V", [P, VR, D])
        b = Arena(K_at)
        LT = b.take("LT", [P, PAST + NT])
        Fs = b.take("Fs", [P, PAST + NT])
        X = b.take("X", [NS, NB, NH])
        bm = b.take("bm", [NS, NB, NH])
        tsel = b.take("tsel", [NS, NT])
        one = b.take("one", [P, 1])
        mpre = b.take("mpre", [NR, NH, 2 * NS - NT])
        assert b.at <= LF_at

        ORDER = (7, 0, 6, 1, 5, 2, 4, 3)
        UN = 2 * QB
        NU = NP * UN
        PAGES = NB * NPG
        V0 = UN + 7
        STEPS = PAGES + V0 + 1
        G_OUT, G_PTD, G_PTN, G_PTD2, G_OS = (2, 3), 4, 5, 9, 7

        def unit(u):
            return u // UN, u % UN // QB, ORDER[u % QB]

        def s_bank(u):
            return ps[:, 0:2, :].rearrange("p b n -> p (b n)") if u % 2 == 0 else ps[:, 2, :]

        def side_work(s):
            g, r = s % UN, s // UN - 1
            if r < 0:
                return None
            if g in G_OUT and r < NP:
                return "out", r, G_OUT.index(g)
            if g in (G_PTD, G_PTN, G_PTD2) and r < NB:
                return "probs", r, (G_PTD, G_PTN, G_PTD2).index(g)
            if g == G_OS and 1 <= r <= NB:
                return "sample", r - 1, 0
            return None

        s_set = sem("s_set")
        s_pair = [sem(f"s_pair{i}") for i in range(2)]
        s_nF = [sem(f"s_nF{i}") for i in range(2)]
        s_K = [sem(f"s_K{i}") for i in range(KR)]
        s_V = [sem(f"s_V{i}") for i in range(VR)]
        s_c, s_ones = sem("s_cst5"), sem("s_ones5")
        s_lT5, s_LT, s_X, s_newf, s_G5 = (sem(n) for n in ("s_lT5", "s_LT", "s_X", "s_newf", "s_G5"))
        s_qst, s_nT, s_newT = sem("s_qst"), sem("s_nT"), sem("s_newT")
        s_S, s_bias, s_mask, s_max, s_exp = (sem(n) for n in ("s_S", "s_bias", "s_mask", "s_max", "s_exp"))
        s_PT, s_PTe, s_O, s_On = (sem(n) for n in ("s_PT", "s_PTe", "s_O", "s_On"))
        s_Kt, s_KeA, s_KeB, s_sc, s_rowe = (sem(n) for n in ("s_Kt", "s_KeA", "s_KeB", "s_sc", "s_rowe"))
        s_dmax, s_dexp = sem("s_dmax"), sem("s_dexp")
        s_pv, s_osb = sem("s_pv"), sem("s_osb")
        s_side, s_side_read = sem("s_side"), sem("s_side_read")
        link, plink = chainer("dve_chain5"), chainer("pool_chain5")
        k_rows, v_rows = cache_k.rearrange("g k h d -> g k (h d)"), cache_v.rearrange("g k h d -> g k (h d)")
        NPAIR = 4

        sides_before = [sum(side_work(x) is not None for x in range(s)) for s in range(STEPS + 1)]

        loads = []
        for t in range(PAGES):
            loads.append((t - KR + 1.5, "K", t))
            loads.append((t + V0 - VR + 1.6, "V", t))
        for p in range(1, NP):
            loads.append((UN * (p - 1) + 5.7, "pair", p))
            loads.append((UN * p - QB + 3.8, "nF", 2 * p))
        for p in range(NP):
            loads.append((UN * p + 3.8 if p else -9.0, "nF", 2 * p + 1))
        loads.sort()

        with nc.Block() as block:
            @block.sync
            def _(sp):
                def pair_loads(p):
                    i = p % 2
                    if p >= 2:
                        sp.wait_ge(s_S, UN * (p - 1))
                        sp.wait_ge(s_O, UN * (p - 1))
                        sp.wait_ge(s_side_read, sides_before[UN * (p - 1) + G_OUT[1]] + 1)
                    sp.dma_start(qT[:, i], qT_d[p, :, 0:SEQ]).then_inc(s_pair[i], 16)
                    sp.dma_start(kT[:, i], kT_d[p, :, 0:SEQ]).then_inc(s_pair[i], 16)
                    sp.dma_start(zT[:, i], zT_d[p, :, 0:SEQ]).then_inc(s_pair[i], 16)
                    sp.dma_start(Vt[:, i], vp[:, :, p * P:(p + 1) * P]).then_inc(s_pair[i], 16)

                def head_load(h):
                    if h >= 2:
                        sp.wait_ge(s_bias, QB * (h - 1))
                    sp.dma_start(nF[:, h % 2], negF_d[h:h + 1, :].broadcast_to([P, SEQ])).then_inc(s_nF[h % 2], 16)

                sp.dma_start(q_s[:, :, :], qT_d[:, :, SEQ:T].rearrange("k p n -> p k n")).then_inc(s_set, 16)
                sp.dma_start(k_s[:, :, :], kT_d[:, :, SEQ:T].rearrange("k p n -> p k n")).then_inc(s_set, 16)
                sp.dma_start(z_s[:, :, :], zT_d[:, :, SEQ:T].rearrange("k p n -> p k n")).then_inc(s_set, 16)
                sp.dma_start(v_s[:, :], vs).then_inc(s_set, 16)
                reg = sp.alloc_register("page5")

                def page(t):
                    sp.reg_load(reg, pt[0:1, t:t + 1])
                    return bass.ds(sp.snap(reg, min_val=0, max_val=n_phys - 1), 1)

                pair_loads(0)
                head_load(0)
                sp.wait_ge(s_G5, 1)
                for _, what, t in loads:
                    if what == "pair":
                        pair_loads(t)
                    elif what == "nF":
                        head_load(t)
                    elif what == "K":
                        if t >= KR:
                            sp.wait_ge(s_Kt, t - KR + 1)
                        sp.dma_start(K[:, t % KR], k_rows[page(t)].rearrange("a k n -> (a k) n")).then_inc(
                            s_K[t % KR], 16)
                    else:
                        if t >= VR:
                            sp.wait_ge(s_pv, t - VR + 1)
                        sp.dma_start(V[:, t % VR], v_rows[page(t)].rearrange("a k n -> (a k) n")).then_inc(
                            s_V[t % VR], 16)

            @block.gpsimd
            def _(pool):
                pool.memset(qst[:, :, :], 0.0).then_inc(s_ones, 1)
                pool.memset(bm[:, :, :], 1.0).then_inc(s_ones, 1)
                pool.memset(one[:, :], 1.0).then_inc(s_ones, 1)
                pool.memset(E_all[:, :, :], 0.0).then_inc(s_ones, 1)
                pool.memset(mpre[:, :, :], 1.0).then_inc(s_ones, 1)
                pool.wait_ge(s_ones, 5)
                v = bm[:, :, :]
                plink(pool, pool.affine_select(out=v, in_=v, compare_op=ALU.is_ge, fill=0.0, base=0,
                                               pattern=[[-NT, NB], [0, NH]], channel_multiplier=1))
                pool.affine_select(out=v, in_=v, compare_op=ALU.is_ge, fill=0.0, base=NT - 1,
                                   pattern=[[NT, NB], [0, NH]], channel_multiplier=-1).then_inc(s_c, 1)
                v = E_all[:, :, :].rearrange("p b (h q) -> p b h q", q=NT)
                plink(pool, pool.affine_select(out=v, in_=v, compare_op=ALU.not_equal, fill=1.0, base=0,
                                               pattern=[[-NH, NB], [-1, NH], [0, NT]], channel_multiplier=1))
                v, n = mpre[:, :, :], 2 * NS - NT
                plink(pool, pool.affine_select(out=v, in_=v, compare_op=ALU.is_ge, fill=0.0, base=NS - NT,
                                               pattern=[[-NT, NH], [-1, n]], channel_multiplier=1))
                plink(pool, pool.affine_select(out=v, in_=v, compare_op=ALU.is_ge, fill=0.0, base=NT - 1,
                                               pattern=[[NT, NH], [0, n]], channel_multiplier=-1))
                pool.affine_select(out=v, in_=v, compare_op=ALU.is_ge, fill=0.0, base=-(NS - NT),
                                   pattern=[[0, NH], [1, n]], channel_multiplier=0).then_inc(s_c, 1)
                for u in range(NU):
                    i = unit(u)[2]
                    pool.wait_ge(s_bias, u + 1)
                    blk = Sb[u % 2][:, i * P:(i + 1) * P]
                    pool.affine_select(out=blk, in_=blk, compare_op=ALU.is_ge, fill=NEG, base=0,
                                       pattern=[[-1, P]], channel_multiplier=1).then_inc(s_mask, 1)

            @block.tensor
            def _(pe):
                for g in range(NPG):
                    mm = pe.transpose(ps[:, g // 4, g % 4 * P:(g % 4 + 1) * P], LF[:, g, :], ident[:, :])
                mm.then_inc(s_lT5, 1)
                pe.wait_ge(s_X, 2)
                pe.matmul(ps[:, 4, 0:NT], X[:, :, :].rearrange("p b h -> p (b h)"), tsel[:, :],
                          start=True, stop=True).then_inc(s_newf, 1)
                pe.wait_ge(s_qst, 2)
                pe.wait_ge(s_set, 64)
                q4 = qst[:, :, :].rearrange("p b (c w) -> p b c w", w=QW)
                for p in range(NP):
                    mm = pe.matmul(ps[0:NS, 5, p * NR:(p + 1) * NR].rearrange("n (b c) -> n b c", b=NB), k_s[:, p, :],
                                   q4[:, :, p, 0:2 * NT], start=True, stop=True)
                mm.then_inc(s_nT, 1)
                pe.wait_ge(s_newT, 1)
                pe.wait_ge(s_G5, 1)

                def scores(u):
                    p, h, i = unit(u)
                    if u % UN == 0:
                        pe.wait_ge(s_pair[p % 2], 16 * NPAIR * (p // 2 + 1))
                    if u >= 2:
                        pe.wait_ge(s_PTe, u - 1)
                    n, bank, hs = (i + 1) * P, s_bank(u), slice(h * HD, (h + 1) * HD)
                    for c in range(0, n, BANK):
                        e = min(c + BANK, n)
                        mm = pe.matmul(bank[:, c:e], qT[hs, p % 2, i * P:(i + 1) * P], kT[hs, p % 2, c:e],
                                       start=True, stop=True)
                    mm.then_inc(s_S, 1)

                def turn_probs(u):
                    i, bank = unit(u)[2], s_bank(u)
                    pe.wait_ge(s_exp, u + 1)
                    for j in range(i + 1):
                        mm = pe.transpose(bank[:, j * P:(j + 1) * P], Sb[u % 2][:, j * P:(j + 1) * P], ident[:, :])
                    mm.then_inc(s_PT, 1)

                def values(u):
                    p, h, i = unit(u)
                    pe.wait_ge(s_PTe, u + 1)
                    for j in range(i + 1):
                        mm = pe.matmul(ps[:, 3, 0:P], PT[u % 2][:, j * P:(j + 1) * P],
                                       Vt[:, p % 2, j, :], start=(j == 0), stop=(j == i))
                    mm.then_inc(s_O, 1)

                def turn_K(t):
                    pe.wait_ge(s_K[t % KR], 16 * (t // KR + 1))
                    if t:
                        pe.wait_ge(s_KeA, t)
                        pe.wait_ge(s_KeB, t)
                    for c in range(NP):
                        mm = pe.transpose(ps[:, 6 + c // 4, c % 4 * P:(c % 4 + 1) * P],
                                          K[:, t % KR, c * P:(c + 1) * P], ident[:, :])
                    mm.then_inc(s_Kt, 1)

                def page_scores(t):
                    bq, g = t // NPG, t % NPG
                    pe.wait_ge(s_KeA, t + 1)
                    pe.wait_ge(s_KeB, t + 1)
                    out = ps[0:NR, 3, P:2 * P]
                    pe.matmul(out, E_all[:, bq, :], G[:, g * P:(g + 1) * P], start=True, stop=False)
                    for c in range(NP):
                        mm = pe.matmul(out, qst[:, bq, c * NR:(c + 1) * NR], KT[:, t % 2, c * P:(c + 1) * P],
                                       start=False, stop=(c == NP - 1))
                    if g == NPG - 1:
                        out = ps[0:NR, 3, 2 * P:2 * P + NS]
                        pe.matmul(out, E_all[:, bq, :], G[:, PAST:PAST + NS], start=True, stop=False)
                        mm = pe.matmul(out, newT[:, bq].rearrange("n k c -> n (k c)"), ident[0:NS, 0:NS],
                                       start=False, stop=True)
                    mm.then_inc(s_sc, 1)

                def page_values(t):
                    bq, g = t // NPG, t % NPG
                    pe.wait_ge(s_V[t % VR], 16 * (t // VR + 1))
                    if g == 0:
                        pe.wait_ge(s_side_read, sides_before[UN * (bq + 1) + G_PTN] + 1)
                        if bq:
                            pe.wait_ge(s_osb, bq)
                        for c in range(2):
                            pe.matmul(ps[0:NR, 4 + c, :], PTn[:, :], v_s[:, c * BANK:(c + 1) * BANK],
                                      start=True, stop=False)
                    if g == NPG // 2:
                        pe.wait_ge(s_side_read, sides_before[UN * (bq + 1) + G_PTD2] + 1)
                    for c in range(2):
                        mm = pe.matmul(ps[0:NR, 4 + c, :], PTd[:, g, :], V[:, t % VR, c * BANK:(c + 1) * BANK],
                                       start=False, stop=(g == NPG - 1))
                    mm.then_inc(s_pv, 1)

                def side(s, what, r, part):
                    if s < PAGES:
                        pe.wait_ge(s_KeA, s + 1)
                    if what == "out":
                        pe.wait_ge(s_On, UN * (r + 1))
                        for i in range(4):
                            mm = pe.transpose(ps[:, 6, i * P:(i + 1) * P], o_tok[:, r % 2, 4 * part + i, :],
                                              ident[:, :])
                    elif what == "sample":
                        pe.wait_ge(s_osb, r + 1)
                        for c in range(NP):
                            mm = pe.matmul(ps[:, 6, 8 * c:8 * c + 8], O_sb[:, c * P:(c + 1) * P],
                                           ident[0:NR, 8 * c:8 * c + 8], start=True, stop=True)
                    elif part == 1:
                        mm = pe.transpose(ps[0:NS, 6, 0:NR], Sd[:, r % 2, PAST:PAST + NS], ident[0:NR, 0:NR])
                    else:
                        pe.wait_ge(s_dexp, r + 1)
                        for g in range(8):
                            at = (4 * part + g) * P
                            mm = pe.transpose(ps[:, 6, g * NR:(g + 1) * NR], Sd[:, r % 2, at:at + P],
                                              ident[0:NR, 0:NR])
                    mm.then_inc(s_side, 1)

                scores(0)
                scores(1)
                for s in range(STEPS):
                    if sides_before[s]:
                        pe.wait_ge(s_side_read, sides_before[s])
                    if s < PAGES:
                        turn_K(s)
                    if s < NU:
                        turn_probs(s)
                    if V0 <= s < V0 + PAGES:
                        page_values(s - V0)
                    if side_work(s):
                        side(s, *side_work(s))
                    if 2 <= s <= NU:
                        pe.wait_ge(s_On, s - 1)
                        pe.wait_ge(s_rowe, s - 1)
                    if 1 <= s <= NU:
                        values(s - 1)
                        page_scores(s - 1)
                    if s + 2 < NU:
                        scores(s + 2)

            @block.scalar
            def _(act):
                act.wait_ge(s_lT5, 1)
                act.copy(LT[:, 0:PAST].rearrange("p (b n) -> p b n", b=4), ps[:, 0:4, :]).then_inc(s_LT, 1)
                act.wait_ge(s_newf, 1)
                act.copy(LT[:, PAST:PAST + NT], ps[:, 4, 0:NT]).then_inc(s_LT, 1)

                def exps(u):
                    n, t = (unit(u)[2] + 1) * P, Sb[u % 2]
                    act.wait_ge(s_max, u + 1)
                    act.activation(t[:, 0:n], t[:, 0:n], ACT.Exp, bias=nmax[:, u % 4:u % 4 + 1],
                                   accum_out=rsum[:, u % 4:u % 4 + 1]).then_inc(s_exp, 1)

                exps(0)
                for s in range(STEPS):
                    r, work = s // UN - 1, side_work(s)
                    if s < PAGES:
                        act.wait_ge(s_Kt, s + 1)
                        if s >= 2:
                            act.wait_ge(s_sc, s - 1)
                        act.copy(KT[:, s % 2, 0:BANK], ps[:, 6, :]).then_inc(s_KeA, 1)
                    if s < NU:
                        n = (unit(s)[2] + 1) * P
                        act.wait_ge(s_PT, s + 1)
                        if s >= 2:
                            act.wait_ge(s_O, s - 1)
                        act.copy(PT[s % 2][:, 0:n], s_bank(s)[:, 0:n]).then_inc(s_PTe, 1)
                    if work and work[0] == "probs":
                        act.wait_ge(s_side, sides_before[s] + 1)
                        if work[2] == 1:
                            act.copy(PTn[:, :], ps[0:NS, 6, 0:NR]).then_inc(s_side_read, 1)
                        else:
                            h = 4 * work[2]
                            act.copy(PTd[:, h:h + 8, :].rearrange("p g r -> p (g r)"),
                                     ps[:, 6, :]).then_inc(s_side_read, 1)
                    if s + 1 < NU:
                        exps(s + 1)
                    if 0 <= r < NB and s % UN == 2:
                        st = dstat[:, r % 2]
                        act.wait_ge(s_dmax, r + 1)
                        act.activation(Sd[:, r % 2, :], Sd[:, r % 2, :], ACT.Exp, bias=st[:, 0:1],
                                       accum_out=st[:, 1:2]).then_inc(s_dexp, 1)

            @block.vector
            def _(dve):
                dve.wait_ge(s_c, 1)
                dve.tensor_tensor(X[:, :, :], bm[:, :, :], lf_s[:, :].unsqueeze(1).broadcast_to([NS, NB, NH]),
                                  ALU.mult).then_inc(s_X, 1)
                dve.tensor_reduce(tsel[:, :], ident[0:NS, 0:NS].rearrange("p (b t) -> p t b", t=NT), AX_X,
                                  ALU.add).then_inc(s_X, 1)
                dve.wait_ge(s_set, 64)
                q4 = qst[:, :, :].rearrange("p b (c w) -> p b c w", w=QW)
                for h in range(2):
                    r = slice(h * HD, (h + 1) * HD)
                    dve.tensor_copy(q4[r, :, :, h * NT:(h + 1) * NT],
                                    q_s[r, :, :].rearrange("p k (b t) -> p b k t", t=NT)).then_inc(s_qst, 1)
                dve.wait_ge(s_LT, 2)
                n = PAST + NT
                link(dve, dve.tensor_tensor_scan(Fs[:, :], one[:, 0:1].broadcast_to([P, n]), LT[:, :], 0.0,
                                                 op0=ALU.mult, op1=ALU.add))
                link(dve, dve.tensor_scalar(Fs[:, :], Fs[:, :], Fs[:, n - 1:n], -1.0, ALU.subtract, ALU.mult))
                dve.tensor_copy(G[:, 0:PAST], Fs[:, 0:PAST])
                link(dve, dve.tensor_copy(G[:, PAST:PAST + NS].rearrange("p (b t) -> p b t", b=NB),
                                          Fs[:, PAST:n].unsqueeze(1).broadcast_to([P, NB, NT])))
                dve.wait_ge(s_c, 2)
                link(dve, dve.tensor_reduce(nmask[:, :], mpre[:, :, :].rearrange("p h c -> p c h"), AX_X, ALU.add))
                dve.tensor_scalar(nmask[:, :], nmask[:, :], 1.0, -NEG, ALU.subtract, ALU.mult).then_inc(s_G5, 1)
                dve.wait_ge(s_nT, 1)
                dve.tensor_copy(newT[:, :, :, :].rearrange("n b k c -> n k b c"),
                                ps[0:NS, 5, :].rearrange("n (k b c) -> n k b c", k=NP, b=NB)).then_inc(s_newT, 1)

                def logits(u):
                    p, h, i = unit(u)
                    m, t = (i + 1) * P, Sb[u % 2]
                    dve.wait_ge(s_S, u + 1)
                    if u % QB == 0:
                        dve.wait_ge(s_nF[h], 16 * (p + 1))
                    dve.scalar_tensor_tensor(out=t[:, 0:m], in0=nF[:, h, 0:m],
                                             scalar=Ftok[:, i, 2 * p + h:2 * p + h + 1], in1=s_bank(u)[:, 0:m],
                                             op0=ALU.add, op1=ALU.add).then_inc(s_bias, 1)

                def row_max(u):
                    m = (unit(u)[2] + 1) * P
                    dve.wait_ge(s_mask, u + 1)
                    dve.tensor_reduce(nmax[:, u % 4:u % 4 + 1], Sb[u % 2][:, 0:m], AX_X, ALU.max,
                                      negate=True).then_inc(s_max, 1)

                def normalise(u):
                    p, h, i = unit(u)
                    dve.wait_ge(s_sc, u + 1)
                    dve.tensor_scalar(o_tok[:, p % 2, i, h * HD:(h + 1) * HD], ps[:, 3, h * HD:(h + 1) * HD],
                                      rinv[:, u % 4:u % 4 + 1], None, ALU.mult).then_inc(s_On, 1)

                def page_rows(t):
                    bq, g = t // NPG, t % NPG
                    if g == 0 and bq >= 2:
                        dve.wait_ge(s_side, sides_before[UN * (bq - 1) + G_PTD2] + 1)
                    mm = dve.tensor_copy(Sd[:, bq % 2, g * P:(g + 1) * P], ps[0:NR, 3, P:2 * P])
                    if g == NPG - 1:
                        mk = nmask[:, NS - NT - NT * bq:2 * NS - NT - NT * bq]
                        mm = dve.tensor_tensor(Sd[:, bq % 2, PAST:PAST + NS], ps[0:NR, 3, 2 * P:2 * P + NS], mk, ALU.add)
                    mm.then_inc(s_rowe, 1)

                logits(0)
                row_max(0)
                for s in range(STEPS):
                    r, g, work = s // UN - 1, s % UN, side_work(s)
                    if 2 <= s < NU + 2:
                        normalise(s - 2)
                        page_rows(s - 2)
                    if s + 1 < NU:
                        logits(s + 1)
                    if s < NU:
                        dve.wait_ge(s_exp, s + 1)
                        dve.reciprocal(rinv[:, s % 4:s % 4 + 1], rsum[:, s % 4:s % 4 + 1])
                    if s < PAGES:
                        dve.wait_ge(s_Kt, s + 1)
                        if s >= 2:
                            dve.wait_ge(s_sc, s - 1)
                        dve.tensor_copy(KT[:, s % 2, BANK:D], ps[:, 7, :]).then_inc(s_KeB, 1)
                    if s + 1 < NU:
                        row_max(s + 1)
                    if 0 <= r < NB and g == 2:
                        dve.wait_ge(s_rowe, NPG * (r + 1))
                        dve.tensor_reduce(dstat[:, r % 2, 0:1], Sd[:, r % 2, :], AX_X, ALU.max,
                                          negate=True).then_inc(s_dmax, 1)
                    if s >= V0 and (s - V0) % NPG == NPG - 1:
                        bv = (s - V0) // NPG
                        st = dstat[:, bv % 2]
                        dve.wait_ge(s_dexp, bv + 1)
                        link(dve, dve.reciprocal(st[:, 2:3], st[:, 1:2]))
                        dve.wait_ge(s_pv, NPG * (bv + 1))
                        if bv:
                            dve.wait_ge(s_side, sides_before[UN * (bv + 1) + G_OS] + 1)
                        dve.tensor_scalar(O_sb[:, :].rearrange("p (b n) -> p b n", b=2), ps[0:NR, 4:6, :],
                                          st[:, 2:3], None, ALU.mult).then_inc(s_osb, 1)
                    if work and work[0] != "probs":
                        what, r, part = work
                        dve.wait_ge(s_side, sides_before[s] + 1)
                        if what == "out":
                            c = slice(part * BANK, (part + 1) * BANK)
                            dve.tensor_tensor(og[:, r, c], ps[:, 6, :], zT[:, r % 2, c], ALU.mult).then_inc(s_side_read, 1)
                        else:
                            o4 = ps[:, 6, 0:NR].rearrange("p (k h t) -> p k h t", k=NP, h=2)
                            for h in range(2):
                                rows, c = slice(h * HD, (h + 1) * HD), slice(r * NT, (r + 1) * NT)
                                ins = dve.tensor_tensor(og[rows, :, SEQ + r * NT:SEQ + (r + 1) * NT], o4[rows, :, h, :],
                                                        z_s[rows, :, c], ALU.mult)
                            ins.then_inc(s_side_read, 1)

    stage_conditioning()
    end_stage()
    stage_pooling()
    end_stage()
    arena = Arena(y_at)
    y_tok = arena.take("y_tok", [P, TT, D])
    stage_out("b", a_out_w[0], 2, y_tok, arena, actH, actL, g_d, None)
    end_stage()
    arena = Arena(y_at)
    arena.at += TT * D * 4
    stage_residual(0, y_tok, arena, lambda i: x_p[:, i, :] if i < QB else x_s,
                   [(0, kvg, None), (KD, modA[:, 1], modB[:, 1])])
    end_stage()
    stage_projections()
    end_stage()
    after = Arena(act_at)
    og = after.take("og", [P, NP, T])
    og_end = after.at
    stage_attention(og)
    end_stage()
    ogH = after.take("ogH", [P, NP, T], F32R)
    ogL = after.take("ogL", [P, NP, T], F32R)
    y2 = after.take("y2_tok", [P, TT, D])
    y2_end = after.at
    stage_out("d", b_out_w[0], 1, y2, after, ogH, ogL, None, og)
    end_stage()
    after = Arena(y2_end)
    stage_residual(1, y2, after, lambda i: x1_d[i, 0:rows_of(i)], None)
    ctx.close()


_INS = ["x_prompt", "x_sample", "state_pool", "cache_k", "cache_v", "cache_logf", "page_table", "c_prompt",
        "c_sample", "ada_w", "ada_b", "pre_g", "post_g", "a_in_w", "a_grp_w", "a_scale", "a_out_w", "kv_g",
        "kv_w", "f_b", "b_in_w", "b_out_w"]
_OUTS = [(1, SEQ, D), (NB, NT, D), (1, 1, HIST, W_A), (1, NB, HIST, W_A), (1, SEQ, NH, HD), (1, SEQ, NH, HD),
         (1, SEQ, NH), (NB, NT, NH, HD), (NB, NT, NH, HD), (NB, NT, NH)]


def kernel(**inputs):
    import numpy as _np
    import concourse.bacc as _bacc
    from concourse import mybir as _mybir
    from concourse.bass_utils import run_bass_kernel_spmd as _run

    nc = _bacc.Bacc("TRN2", target_bir_lowering=False, num_devices=1)
    arrays, args = {}, []
    for name in _INS:
        a = _np.ascontiguousarray(inputs[name])
        arrays[f"in_{name}_dram"] = a
        args.append(nc.dram_tensor(f"in_{name}_dram", a.shape, _mybir.dt.from_np(a.dtype), kind="ExternalInput").ap())
    for i, shape in enumerate(_OUTS):
        args.append(nc.dram_tensor(f"out_{i}_dram", shape, _mybir.dt.float32, kind="ExternalOutput").ap())
    build(nc, *args)
    r = _run(nc, [arrays], core_ids=[0])
    return tuple(r.results[0][f"out_{i}_dram"] for i in range(len(_OUTS)))
```

```python
from contextlib import ExitStack

import concourse.bass as bass
from concourse import mybir

ALU = mybir.AluOpType
ACT = mybir.ActivationFunctionType
AX_X = mybir.AxisListType.X
F32 = mybir.dt.float32
F32R = mybir.dt.float32r
I32 = mybir.dt.int32

P = 128
D = 1024
KD = D // P
SEQ = 1024
QB = SEQ // P
NB = 8
NT = 4
NS = NB * NT
T = SEQ + NS
TT = QB + 1
NCH = 3
CH = T // NCH
W_A = 2 * D
KA = W_A // P
WINDOWS = (2, 4, 8, 16)
NG = len(WINDOWS)
GT = KA // NG
HIST = max(WINDOWS) - 1
SEG = HIST + NT
UW = HIST + SEQ + NB * SEG
NCOND = 1 + NB
NH = 16
HD = 64
NP = NH // 2
PAGE = 128
NPG = 16
PAST = NPG * PAGE
NR = NH * NT
EPS = 1e-6
NEG = -1e30
BANK = 512
RAW = 2
SPL = 2
XR = 3
KR = 3
VR = 2


def rows_of(i):
    return P if i < QB else NS


def stream_weights(sp, w, jobs):
    for j, src in enumerate(jobs):
        stream_weight(sp, w, j, src)


def stream_weight(sp, w, j, src):
    if j >= RAW:
        sp.wait_ge(w["split"], j - RAW + 1)
    sp.dma_start(w["raw"][:, j % RAW, 0:src.shape[1], 0:src.shape[2]], src).then_inc(
        w["landed"][j % RAW], 16)


def split_first_high(act, w, src):
    kt = src.shape[1]
    act.wait_ge(w["landed"][0], 16)
    act.copy(w["hi"][:, 0, 0:kt, :], w["raw"][:, 0, 0:kt, :]).then_inc(w["hi_ready"], 1)


def split_first_low(dve, w, src):
    kt = src.shape[1]
    dve.wait_ge(w["hi_ready"], 1)
    dve.tensor_tensor(w["lo"][:, 0, 0:kt, :], w["raw"][:, 0, 0:kt, :], w["hi"][:, 0, 0:kt, :].bitcast(F32),
                      ALU.subtract).then_inc(w["split"], 1)


def split_weights(pool, w, jobs):
    pool.wait_ge(w["split"], 1)
    for j, src in enumerate(jobs):
        if j == 0:
            continue
        kt = src.shape[1]
        raw, hi, lo = (w[n][:, j % r, 0:kt, :] for n, r in (("raw", RAW), ("hi", SPL), ("lo", SPL)))
        pool.wait_ge(w["landed"][j % RAW], 16 * (j // RAW + 1))
        if j >= SPL:
            pool.wait_ge(w["used"], j - SPL + 1)
        pool.tensor_copy(hi, raw).then_inc(w["hi_ready"], 1)
        pool.wait_ge(w["hi_ready"], j + 1)
        pool.tensor_tensor(lo, raw, hi.bitcast(F32), ALU.subtract).then_inc(w["split"], 1)


def product(pe, w, j, kt, acc, act_hi, act_lo, k0, first=True, last=True, moving_ready=None):
    pe.wait_ge(w["split"], j + 1)
    hi, lo = w["hi"], w["lo"]
    for k in range(kt):
        if moving_ready is not None:
            pe.wait_ge(moving_ready, k0 + k + 1)
        for s, (wt, act) in enumerate(((hi, act_hi), (hi, act_lo), (lo, act_hi))):
            for c in range(NCH):
                mm = pe.matmul(acc[:, c, 0:CH], wt[:, j % SPL, k, :], act[:, k0 + k, c * CH:(c + 1) * CH],
                               start=first and k == 0 and s == 0, stop=last and k == kt - 1 and s == 2)
    mm.then_inc(w["used"], 1)


def thirds(acc):
    return acc[:, :, 0:CH]


def as_thirds(ap):
    return ap.rearrange("p (c t) -> p c t", c=NCH)


def build(nc, x_prompt, x_sample, state_pool, cache_k, cache_v, cache_logf, page_table, c_prompt,
          c_sample, ada_w, ada_b, pre_g, post_g, a_in_w, a_grp_w, a_scale, a_out_w, kv_g, kv_w,
          f_b, b_in_w, b_out_w, y_prompt, y_sample, pool_prompt, pool_sample, k_prompt, v_prompt,
          logf_prompt, k_sample, v_sample, logf_sample):
    ctx = ExitStack()
    n_phys = cache_k.shape[0]
    base = (nc.sbuf_base + 31) // 32 * 32
    top = nc.sbuf_usable_end // 32 * 32
    size = {F32: 4, F32R: 4, I32: 4}

    class Arena:

        def __init__(self, at):
            self.at = at

        def take(self, name, shape, dt=F32):
            n = size[dt]
            for d in shape[1:]:
                n *= d
            t = nc.alloc_sbuf_tensor_at(name, shape, dt, offset=self.at)
            self.at = (self.at + n + 31) // 32 * 32
            assert self.at <= top, (name, self.at - top)
            return t

    stage_sems = []

    def sem(name):
        stage_sems.append(nc.alloc_semaphore(name))
        return stage_sems[-1]

    s_pout = [nc.alloc_semaphore(f"s_pout{i}") for i in range(2)]
    s_tout = [nc.alloc_semaphore(f"s_tout{i}") for i in range(2)]
    s_lout = nc.alloc_semaphore("s_lout")
    s_xout = [nc.alloc_semaphore(f"s_xout{i}") for i in range(2)]

    def end_stage():
        nc.clear_and_free_semaphores(list(stage_sems))
        stage_sems.clear()
        nc.all_engine_barrier()

    def scratch(name, shape):
        return nc.dram_tensor(name, shape, F32, kind="Internal").ap()

    gate_d = scratch("gate_d", (2, NCOND, D))
    g_d = scratch("g_d", (KA, P, T))
    x1_d = scratch("x1_d", (TT, P, D))
    qT_d = scratch("qT_d", (NP, P, T))
    kT_d = scratch("kT_d", (NP, P, T))
    zT_d = scratch("zT_d", (NP, P, T))
    og_d = scratch("og_d", (NP, P, T))
    negF_d = scratch("negF_d", (NH, SEQ))

    x_p = x_prompt.rearrange("a (t p) d -> p (a t) d", p=P)
    x_s = x_sample.rearrange("b t d -> (b t) d")
    yp = y_prompt.rearrange("a (t p) d -> p (a t) d", p=P)
    ys = y_sample.rearrange("b t d -> (b t) d")
    kp = k_prompt.rearrange("a (t p) h d -> p (a t) (h d)", p=P)
    vp = v_prompt.rearrange("a (t p) h d -> p (a t) (h d)", p=P)
    ks = k_sample.rearrange("b t h d -> (b t) (h d)")
    vs = v_sample.rearrange("b t h d -> (b t) (h d)")
    lfp = logf_prompt.rearrange("a (t p) h -> p (a t) h", p=P)
    lfs = logf_sample.rearrange("b t h -> (b t) h")

    def w_tiles(mat, k0, kt, n0, n):
        return mat[k0 * P:(k0 + kt) * P, n0:n0 + n].rearrange("(k p) n -> p k n", p=P)

    keep = Arena(base)
    ident = keep.take("ident", [P, P])
    modA = keep.take("modA", [P, 2, KD, NCOND])
    modB = keep.take("modB", [P, 2, KD, NCOND])
    kvg = keep.take("kvg", [P, KD])
    asc = keep.take("asc", [P, KA])
    Ftok = keep.take("Ftok", [P, QB, NH])
    lf_s = keep.take("lf_s", [NS, NH])
    pt = keep.take("pt", [1, NB * NPG], I32)
    ssq = keep.take("ssq", [P, TT, KD])
    act_at = keep.at
    actH = keep.take("actH", [P, KA, T], F32R)
    actL_at = keep.at
    actL = keep.take("actL", [P, KA, T], F32R)
    free = keep.at

    K_at = top - (KR + VR) * D * 4
    LF_at = top - NPG * NB * NH * 4
    upper = Arena(LF_at)
    LF = upper.take("LF", [P, NPG, NB * NH])

    ps = ctx.enter_context(nc.psum_tensor("ps", [P, 8, BANK], F32))
    acc = [ps[:, 0:3, :], ps[:, 3:6, :]]

    def weight_ring(tag, arena):
        return {
            "raw": arena.take(f"w_raw_{tag}", [P, RAW, KD, P]),
            "hi": arena.take(f"w_hi_{tag}", [P, SPL, KD, P], F32R),
            "lo": arena.take(f"w_lo_{tag}", [P, SPL, KD, P], F32R),
            "landed": [sem(f"w_landed_{tag}{i}") for i in range(RAW)],
            "hi_ready": sem(f"w_hi_ready_{tag}"),
            "split": sem(f"w_split_{tag}"),
            "used": sem(f"w_used_{tag}"),
        }

    def chainer(name):
        s, n = sem(name), [0]

        def link(eng, ins):
            n[0] += 1
            ins.then_inc(s, 1)
            eng.wait_ge(s, n[0])
        return link

    def b_t(ap):
        return ap[:, :, 1:NCOND].unsqueeze(3).broadcast_to([P, KD, NB, NT])

    class NormedTranspose:

        BANKS = 4
        TMP = 4

        def __init__(self, tag, targets, tmp):
            self.targets, self.tmp = targets, tmp
            self.turned = sem(f"turned_{tag}")
            self.high = sem(f"high_{tag}")
            self.low = [sem(f"low{i}_{tag}") for i in range(2)]
            self.full = sem(f"full_{tag}")
            self.rounds = [(g, k) for g in range(QB // 4) for k in range(KD)]

        def parts(self, lo, hi):
            nt = len(self.targets)
            for n in range(lo, hi):
                g, k = self.rounds[n]
                for i, (k0, A, B) in enumerate(self.targets):
                    yield n * nt + i, k0, A, B, g, k, n

        def pe(self, pe, x_tok, x_ready, x_count, lo=0, hi=None):
            nt, hi = len(self.targets), len(self.rounds) if hi is None else hi
            for n in range(lo, hi):
                g, k = self.rounds[n]
                pe.wait_ge(x_ready, x_count(4 * g + 3))
                if n >= self.BANKS:
                    pe.wait_ge(self.full, nt * (n - self.BANKS + 1))
                for i in range(4):
                    mm = pe.transpose(ps[:, n % self.BANKS, i * P:(i + 1) * P],
                                      x_tok[:, 4 * g + i, k * P:(k + 1) * P], ident[:, :])
                mm.then_inc(self.turned, 1)
            n = len(self.rounds)
            if hi < n:
                return
            pe.wait_ge(x_ready, x_count(QB))
            pe.wait_ge(self.full, nt * (n - self.BANKS + 1))
            for k in range(KD):
                mm = pe.transpose(ps[:, n % self.BANKS, k * NS:(k + 1) * NS],
                                  x_tok[0:NS, QB, k * P:(k + 1) * P], ident[0:NS, 0:NS])
            mm.then_inc(self.turned, 1)

        def act(self, act):
            for m, k0, A, B, g, k, n in self.parts(0, len(self.rounds)):
                act.wait_ge(self.full, m + 1)
                act.copy(actH[:, k0 + k, g * BANK:(g + 1) * BANK], self.tmp[:, m % self.TMP, :]).then_inc(self.high, 1)

        def low_part(self, eng, m, k0, g, k):
            cols = slice(g * BANK, (g + 1) * BANK)
            eng.wait_ge(self.high, m + 1)
            eng.tensor_tensor(actL[:, k0 + k, cols], self.tmp[:, m % self.TMP, :],
                              actH[:, k0 + k, cols].bitcast(F32), ALU.subtract).then_inc(self.low[m % 2], 1)

        def pool(self, pool, lo=0, hi=None):
            for m, k0, A, B, g, k, n in self.parts(lo, len(self.rounds) if hi is None else hi):
                if m % 2:
                    self.low_part(pool, m, k0, g, k)

        def dve(self, dve, link, lo=0, hi=None):
            tmp, hi = self.tmp, len(self.rounds) if hi is None else hi
            every = [(k0, g, k) for _, k0, _, _, g, k, _ in self.parts(0, len(self.rounds))]
            for m, k0, A, B, g, k, n in self.parts(lo, hi):
                dve.wait_ge(self.turned, n + 1)
                src, t = ps[:, n % self.BANKS, :], tmp[:, m % self.TMP, :]
                if m >= self.TMP:
                    dve.wait_ge(self.low[m % 2], (m - self.TMP) // 2 + 1)
                if B is not None:
                    ins = dve.tensor_scalar(t, src, A[:, k, 0:1], B[:, k, 0:1], ALU.mult, ALU.add)
                else:
                    ins = dve.tensor_scalar(t, src, A[:, k:k + 1], None, ALU.mult)
                ins.then_inc(self.full, 1)
                if m % 2 == 0 and m >= 2:
                    self.low_part(dve, m - 2, *every[m - 2])
            if hi < len(self.rounds):
                return
            m = len(every)
            self.low_part(dve, m - 2, *every[m - 2])
            dve.wait_ge(self.low[0], m // 2)
            dve.wait_ge(self.low[1], m // 2)
            n = len(self.rounds)
            dve.wait_ge(self.turned, n + 1)
            src = ps[:, n % self.BANKS, 0:KD * NS]
            t = tmp[:, 0, 0:KD * NS]
            for k0, A, B in self.targets:
                hi, lo = (x[:, k0:k0 + KD, SEQ:T] for x in (actH, actL))
                v = t.rearrange("p (k b t) -> p k b t", k=KD, b=NB)
                s4 = src.rearrange("p (k b t) -> p k b t", k=KD, b=NB)
                for k in range(KD):
                    if B is not None:
                        bc = A[:, k, 1:NCOND].unsqueeze(2).broadcast_to([P, NB, NT])
                        ins = dve.tensor_tensor(v[:, k], s4[:, k], bc, ALU.mult)
                    else:
                        ins = dve.tensor_scalar(v[:, k], s4[:, k], A[:, k:k + 1], None, ALU.mult)
                link(dve, ins)
                if B is not None:
                    for k in range(KD):
                        bc = B[:, k, 1:NCOND].unsqueeze(2).broadcast_to([P, NB, NT])
                        ins = dve.tensor_tensor(v[:, k], v[:, k], bc, ALU.add)
                    link(dve, ins)
                t3 = t.rearrange("p (k n) -> p k n", k=KD)
                link(dve, dve.tensor_copy(hi, t3))
                link(dve, dve.tensor_tensor(lo, t3, hi.bitcast(F32), ALU.subtract))

    def stage_conditioning():
        a = Arena(free)
        crow = a.take("crow", [NCOND, D])
        srow = a.take("srow", [NCOND, D])
        scT = a.take("scT", [P, KD, NCOND])
        adab = a.take("adab", [NCOND, 2, BANK])
        mrow = a.take("mrow", [NCOND, 2, BANK])
        preg = a.take("preg", [P, 2, KD])
        x_tok = a.take("x_tok1", [P, TT, D])
        junk = a.take("junk1", [P, D])
        ss = a.take("ss1", [P, TT])
        rstd = a.take("rstd1", [P, TT])
        tmp = a.take("tmp1", [P, 4, BANK])
        adaw = Arena(actL_at + KD * T * 4).take("adaw", [P, 2, KD, BANK])

        chunks = [(l, n) for l in range(2) for n in range(3 * D // BANK)]
        s_c, s_small, s_x = sem("s_c"), sem("s_small"), sem("s_x")
        s_aw = [sem(f"s_aw{i}") for i in range(2)]
        s_ab = [sem(f"s_ab{i}") for i in range(2)]
        s_gate = [sem(f"s_gate{i}") for i in range(2)]
        s_const, s_id = sem("s_const"), sem("s_id")
        s_silu, s_cT, s_scT = sem("s_silu"), sem("s_cT"), sem("s_scT")
        s_m, s_mrow, s_mT, s_mod = sem("s_m"), sem("s_mrow"), sem("s_mT"), sem("s_mod")
        s_ss_init = sem("s_ss_init")
        s_ss, s_var, s_std, s_xn = sem("s_ss"), sem("s_var"), sem("s_std"), sem("s_xn")
        link = chainer("dve_chain1")
        alink = chainer("act_chain1")
        normed = NormedTranspose("l0", [(0, modA[:, 0], modB[:, 0])], tmp)
        GATE = 2 * D // BANK
        FIRST = GATE

        def rounds_after(j):
            each = len(normed.rounds) // (len(chunks) - FIRST)
            return (j - FIRST) * each, (j - FIRST + 1) * each

        with nc.Block() as block:
            @block.sync
            def _(sp):
                sp.dma_start(crow[0:1, :], c_prompt).then_inc(s_c, 16)
                sp.dma_start(crow[1:NCOND, :], c_sample).then_inc(s_c, 16)
                with nc.allow_non_contiguous_dma(reason="small per-channel vectors"):
                    sp.dma_start(preg[:, :, :], pre_g.rearrange("l (k p) -> p l k", p=P)).then_inc(s_small, 16)
                    sp.dma_start(kvg[:, :], kv_g.rearrange("(k p) -> p k", p=P)).then_inc(s_small, 16)
                    sp.dma_start(asc[:, :], a_scale.rearrange("a (k p) -> p (a k)", p=P)).then_inc(s_small, 16)
                for j, (l, n) in enumerate(chunks):
                    if j >= 2:
                        sp.wait_ge(s_m, j - 1)
                        sp.wait_ge(s_mrow, j - 1)
                    sp.dma_start(adaw[:, j % 2], w_tiles(ada_w[l], 0, KD, n * BANK, BANK)).then_inc(s_aw[j % 2], 16)
                    sp.dma_start(adab[:, j % 2], ada_b[l:l + 1, n * BANK:(n + 1) * BANK].broadcast_to(
                        [NCOND, BANK])).then_inc(s_ab[j % 2], 16)
                    if j == 1:
                        sp.dma_start(x_tok[:, 0:QB, :], x_p).then_inc(s_x, 16)
                        sp.dma_start(x_tok[0:NS, QB, :], x_s).then_inc(s_x, 16)

            @block.gpsimd
            def _(pool):
                pool.memset(ident[:, :], 0.0).then_inc(s_id, 1)
                pool.wait_ge(s_id, 1)
                pool.affine_select(out=ident[:, :], in_=ident[:, :], compare_op=ALU.not_equal, fill=1.0,
                                   base=0, pattern=[[-1, P]], channel_multiplier=1).then_inc(s_const, 1)
                for j, (l, n) in enumerate(chunks):
                    if n >= GATE:
                        pool.wait_ge(s_mrow, j + 1)
                        pool.dma_start(gate_d[l, :, (n - GATE) * BANK:(n - GATE + 1) * BANK],
                                       mrow[:, j % 2]).then_inc(s_gate[j % 2], 16)
                    if j >= FIRST:
                        normed.pool(pool, *rounds_after(j))
                pool.wait_ge(s_gate[0], 32)
                pool.wait_ge(s_gate[1], 32)

            @block.scalar
            def _(act):
                act.wait_ge(s_c, 32)
                act.activation(srow[:, :], crow[:, :], ACT.Silu).then_inc(s_silu, 1)
                act.wait_ge(s_x, 32)
                act.wait_ge(s_ss_init, 1)
                for i in range(TT):
                    r = rows_of(i)
                    if i:
                        act.wait_ge(s_ss, i)
                    act.activation(junk[0:r, :], x_tok[0:r, i, :], ACT.Square,
                                   accum_out=ss[0:r, i:i + 1]).then_inc(s_ss, 1)
                act.wait_ge(s_var, 1)
                act.activation(rstd[:, :], rstd[:, :], ACT.Sqrt).then_inc(s_std, 1)
                normed.act(act)

            @block.tensor
            def _(pe):
                pe.wait_ge(s_silu, 1)
                pe.wait_ge(s_const, 1)
                for k in range(KD):
                    mm = pe.transpose(ps[:, 4, k * NCOND:(k + 1) * NCOND], srow[:, k * P:(k + 1) * P],
                                      ident[0:NCOND, 0:NCOND])
                mm.then_inc(s_cT, 1)
                pe.wait_ge(s_scT, 1)

                turned = 0
                for j, (l, n) in enumerate(chunks):
                    pe.wait_ge(s_aw[j % 2], 16 * (j // 2 + 1))
                    if j >= 2:
                        pe.wait_ge(s_mrow, j - 1)
                    for k in range(KD):
                        mm = pe.matmul(ps[0:NCOND, 6 + j % 2, :], scT[:, k, :], adaw[:, j % 2, k, :],
                                       start=(k == 0), stop=(k == KD - 1))
                    mm.then_inc(s_m, 1)
                    if n < GATE:
                        pe.wait_ge(s_mrow, j + 1)
                        if turned:
                            pe.wait_ge(s_mod, turned)
                        for i in range(BANK // P):
                            mm = pe.transpose(ps[:, 5, i * NCOND:(i + 1) * NCOND],
                                              mrow[:, j % 2, i * P:(i + 1) * P], ident[0:NCOND, 0:NCOND])
                        mm.then_inc(s_mT, 1)
                        turned += 1
                    if j >= FIRST:
                        normed.pe(pe, x_tok, s_xn, lambda i: i + 1, *rounds_after(j))

            @block.vector
            def _(dve):
                dve.memset(ss[:, :], 1.0).then_inc(s_ss_init, 1)
                dve.wait_ge(s_cT, 1)
                dve.tensor_copy(scT[:, :, :], ps[:, 4, 0:KD * NCOND].rearrange("p (k c) -> p k c", k=KD)).then_inc(s_scT, 1)
                turned = 0
                gates = [0, 0]
                for j, (l, n) in enumerate(chunks):
                    dve.wait_ge(s_m, j + 1)
                    dve.wait_ge(s_ab[j % 2], 16 * (j // 2 + 1))
                    if gates[j % 2]:
                        dve.wait_ge(s_gate[j % 2], 16 * gates[j % 2])
                    if turned:
                        dve.wait_ge(s_mT, turned)
                    dve.tensor_tensor(mrow[:, j % 2], ps[0:NCOND, 6 + j % 2, :], adab[:, j % 2], ALU.add).then_inc(s_mrow, 1)
                    if n >= GATE:
                        gates[j % 2] += 1
                    else:
                        turned += 1
                        dve.wait_ge(s_mT, turned)
                        for i in range(BANK // P):
                            k = (n % 2) * (BANK // P) + i
                            src = ps[:, 5, i * NCOND:(i + 1) * NCOND]
                            if n < D // BANK:
                                ins = dve.tensor_copy(modB[:, l, k, :], src)
                            else:
                                if turned == 3 and i == 0:
                                    dve.wait_ge(s_small, 48)
                                ins = dve.tensor_scalar(modA[:, l, k, :], src, 1.0, preg[:, l, k:k + 1], ALU.add, ALU.mult)
                        ins.then_inc(s_mod, 1)
                    if j == FIRST - 1:
                        dve.wait_ge(s_ss, TT)
                        dve.tensor_scalar(rstd[:, :], ss[:, :], 1.0 / D, EPS, ALU.mult, ALU.add).then_inc(s_var, 1)
                        dve.wait_ge(s_std, 1)
                        link(dve, dve.reciprocal(rstd[:, :], rstd[:, :]))
                        for i in range(TT):
                            r = rows_of(i)
                            dve.tensor_scalar(x_tok[0:r, i, :], x_tok[0:r, i, :], rstd[0:r, i:i + 1], None,
                                              ALU.mult).then_inc(s_xn, 1)
                        dve.wait_ge(s_mod, turned)
                    if j >= FIRST:
                        normed.dve(dve, link, *rounds_after(j))

    def stage_pooling():
        a = Arena(free)
        w = weight_ring("a", a)
        U = a.take("U", [P, 2, UW])
        win = a.take("win", [P, 2, UW])
        pooled = a.take("pooled", [P, T])
        sz = a.take("sz", [P, 2, T])
        g = a.take("g", [P, 2, T])
        hist = Arena(actL_at + (KD + GT) * T * 4).take("hist", [NB * HIST, W_A])
        pk = a.take("pk", [P, 2, HIST + NB * HIST])
        po_p = a.take("po_p", [HIST, 2, P])
        po_s = a.take("po_s", [NB * HIST, 2, P])
        inv = a.take("inv", [P, HIST])

        PH = KD
        jobs, kinds = [], []
        for gr in range(NG):
            c0 = gr * GT * P
            for i in range(GT):
                jobs.append(w_tiles(a_in_w[0], 0, KD, c0 + i * P, P))
                kinds.append(("u", gr, i))
            for i0 in range(0, GT, 2):
                for i in (i0, i0 + 1):
                    jobs.append(w_tiles(a_in_w[0], 0, KD, W_A + c0 + i * P, P))
                    kinds.append(("z", gr, i))
                for i in (i0, i0 + 1):
                    jobs.append(w_tiles(a_grp_w[0, gr], 0, GT, i * P, P))
                    kinds.append(("m", gr, i))

        s_hist, s_inv, s_pad = sem("s_hist"), sem("s_inv"), sem("s_pad")
        s_hT, s_hU = sem("s_hT"), sem("s_hU")
        s_U = sem("s_U")
        s_pooled, s_ph, s_pl = sem("s_pooled"), sem("s_ph"), sem("s_pl")
        s_pk, s_pkT, s_pkfree = sem("s_pk"), sem("s_pkT"), sem("s_po")
        s_sz, s_g = sem("s_sz"), sem("s_g")
        s_gout = [sem(f"s_gout{i}") for i in range(2)]
        link = chainer("dve_chain2")
        U_s = [U[:, i, HIST + SEQ:UW].rearrange("p (b s) -> p b s", s=SEG) for i in range(2)]
        W_s = [win[:, i, HIST + SEQ:UW].rearrange("p (b s) -> p b s", s=SEG) for i in range(2)]

        with nc.Block() as block:
            @block.sync
            def _(sp):
                sp.dma_start(hist[:, :], state_pool[0].rearrange("b r c -> (b r) c")).then_inc(s_hist, 16)
                stream_weights(sp, w, jobs)

            @block.gpsimd
            def _(pool):
                for t in range(HIST):
                    pool.memset(inv[:, t:t + 1], 1.0 / (t + 1)).then_inc(s_inv, 1)
                for i in range(2):
                    pool.memset(U[:, i, 0:HIST], 0.0).then_inc(s_pad, 1)
                    pool.memset(win[:, i, :], 0.0).then_inc(s_pad, 1)
                split_weights(pool, w, jobs)

            @block.tensor
            def _(pe):
                def finish_tile(j):
                    pe.wait_ge(s_pk, j + 1)
                    if j:
                        pe.wait_ge(s_pkfree, 2 * j)
                    pe.transpose(ps[0:HIST, 7, 0:P], pk[:, j % 2, 0:HIST], ident[:, :])
                    pe.transpose(ps[0:NB * HIST, 7, P:2 * P], pk[:, j % 2, HIST:], ident[:, :]).then_inc(s_pkT, 1)

                pe.wait_ge(s_hist, 16)
                late = None
                for n, (kind, gr, i) in enumerate(kinds):
                    j = gr * GT + i
                    if kind == "u":
                        if j:
                            pe.wait_ge(s_hU, j)
                        pe.transpose(ps[:, 6, 0:NB * HIST], hist[:, j * P:(j + 1) * P],
                                     ident[0:NB * HIST, 0:NB * HIST]).then_inc(s_hT, 1)
                    if n >= 2:
                        was, gw, iw = kinds[n - 2]
                        pe.wait_ge({"u": s_U, "z": s_sz, "m": s_g}[was], gw * GT + iw + 1)
                    if kind == "m":
                        pe.wait_ge(s_pl, (gr + 1) * GT)
                        product(pe, w, n, GT, acc[n % 2], actH, actL, PH)
                    else:
                        product(pe, w, n, KD, acc[n % 2], actH, actL, 0)
                    if late is not None:
                        finish_tile(late)
                    late = j if kind == "u" else None

            @block.scalar
            def _(act):
                split_first_high(act, w, jobs[0])
                late_u, late_g = [], []

                def finish_tile(j):
                    act.wait_ge(s_pkT, j + 1)
                    if j >= 2:
                        act.wait_ge(s_pout[j % 2], 32 * (j // 2))
                    act.copy(po_p[:, j % 2], ps[0:HIST, 7, 0:P]).then_inc(s_pkfree, 1)
                    act.copy(po_s[:, j % 2], ps[0:NB * HIST, 7, P:2 * P]).then_inc(s_pkfree, 1)
                    act.wait_ge(s_pkfree, 2 * (j + 1))
                    c = slice(j * P, (j + 1) * P)
                    act.dma_start(pool_prompt[0, 0, :, c], po_p[:, j % 2]).then_inc(s_pout[j % 2], 16)
                    act.dma_start(pool_sample[0].rearrange("b r c -> (b r) c")[:, c],
                                  po_s[:, j % 2]).then_inc(s_pout[j % 2], 16)

                def store_g(j):
                    act.wait_ge(s_g, j + 1)
                    act.dma_start(g_d[j], g[:, j % 2]).then_inc(s_gout[j % 2], 16)

                for n, (kind, gr, i) in enumerate(kinds):
                    j = gr * GT + i
                    A = acc[n % 2]
                    if kind == "m":
                        late_g.append(j)
                        continue
                    act.wait_ge(w["used"], n + 1)
                    if kind == "u":
                        if j < 2:
                            act.wait_ge(s_pad, 4)
                        else:
                            act.wait_ge(s_pk, j - 1)
                        act.copy(U[:, j % 2, HIST:HIST + 2 * CH].rearrange("p (c t) -> p c t", c=2),
                                 A[:, 0:2, 0:CH])
                        act.copy(U[:, j % 2, HIST + 2 * CH:HIST + SEQ], A[:, 2, 0:SEQ - 2 * CH])
                        act.copy(U_s[j % 2][:, :, HIST:SEG],
                                 A[:, 2, SEQ - 2 * CH:CH].rearrange("p (b t) -> p b t", b=NB)).then_inc(s_U, 1)
                        act.wait_ge(s_pooled, j + 1)
                        act.copy(actH[:, PH + i, :], pooled[:, :]).then_inc(s_ph, 1)
                        late_u.append(j)
                    else:
                        if j >= 2:
                            act.wait_ge(s_g, j - 1)
                        act.activation(as_thirds(sz[:, j % 2]), thirds(A), ACT.Silu).then_inc(s_sz, 1)
                    while late_u and (late_u[0] < j or kind != "u"):
                        finish_tile(late_u.pop(0))
                    while late_g and late_g[0] < j - 1:
                        store_g(late_g.pop(0))
                for j in late_g:
                    store_g(j)
                for i in range(2):
                    act.wait_ge(s_gout[i], 16 * KA // 2)
                    act.wait_ge(s_pout[i], 32 * KA // 2)

            @block.vector
            def _(dve):
                split_first_low(dve, w, jobs[0])
                dve.wait_ge(s_inv, HIST)
                dve.wait_ge(s_pad, 4)
                for n, (kind, gr, i) in enumerate(kinds):
                    j = gr * GT + i
                    u = U[:, j % 2]
                    if kind == "u":
                        size_w = WINDOWS[gr]
                        dve.wait_ge(s_hT, j + 1)
                        dve.tensor_copy(U_s[j % 2][:, :, 0:HIST],
                                        ps[:, 6, 0:NB * HIST].rearrange("p (b r) -> p b r", b=NB)).then_inc(s_hU, 1)
                        dve.wait_ge(s_hU, j + 1)
                        dve.wait_ge(s_U, j + 1)
                        src, step, at = u, 1, 0
                        while step < size_w:
                            lo = 2 * step - 1
                            link(dve, dve.tensor_tensor(win[:, at, lo:UW], src[:, lo:UW], src[:, lo - step:UW - step], ALU.add))
                            src, ws, at, step = win[:, at], W_s[at], 1 - at, 2 * step
                        if j:
                            dve.wait_ge(s_ph, j)
                            dve.wait_ge(s_pl, j)
                        link(dve, dve.scalar_tensor_tensor(
                            out=pooled[:, 0:SEQ], in0=src[:, HIST:HIST + SEQ], scalar=1.0 / size_w,
                            in1=u[:, HIST:HIST + SEQ], op0=ALU.mult, op1=ALU.subtract))
                        cut = size_w - 1
                        link(dve, dve.tensor_tensor(pooled[:, 0:cut], src[:, HIST:HIST + cut], inv[:, 0:cut], ALU.mult))
                        link(dve, dve.tensor_tensor(pooled[:, 0:cut], pooled[:, 0:cut], u[:, HIST:HIST + cut], ALU.subtract))
                        dve.scalar_tensor_tensor(
                            out=pooled[:, SEQ:T].rearrange("p (b t) -> p b t", b=NB), in0=ws[:, :, HIST:SEG],
                            scalar=1.0 / size_w, in1=U_s[j % 2][:, :, HIST:SEG], op0=ALU.mult,
                            op1=ALU.subtract).then_inc(s_pooled, 1)
                        if j >= 2:
                            dve.wait_ge(s_pkT, j - 1)
                        dve.tensor_copy(pk[:, j % 2, 0:HIST], u[:, SEQ:SEQ + HIST])
                        dve.tensor_copy(pk[:, j % 2, HIST:].rearrange("p (b r) -> p b r", b=NB),
                                        U_s[j % 2][:, :, NT:SEG]).then_inc(s_pk, 1)
                        dve.wait_ge(s_ph, j + 1)
                        dve.tensor_tensor(actL[:, PH + i, :], pooled[:, :], actH[:, PH + i, :].bitcast(F32),
                                          ALU.subtract).then_inc(s_pl, 1)
                    elif kind == "m":
                        dve.wait_ge(w["used"], n + 1)
                        dve.wait_ge(s_sz, j + 1)
                        if j >= 2:
                            dve.wait_ge(s_gout[j % 2], 16 * (j // 2))
                        dve.scalar_tensor_tensor(out=as_thirds(g[:, j % 2]), in0=thirds(acc[n % 2]),
                                                 scalar=asc[:, j:j + 1], in1=as_thirds(sz[:, j % 2]),
                                                 op0=ALU.mult, op1=ALU.mult).then_inc(s_g, 1)

    class TokenRows:

        PARTS = (range(0, 4), range(4, 8), range(8, 9))

        def __init__(self, tag):
            self.turned = sem(f"rows_turned_{tag}")
            self.read = sem(f"rows_read_{tag}")

        def pe(self, pe, m, src):
            for q, tiles in enumerate(self.PARTS):
                c = 3 * m + q
                bank = 6 + c % 2
                if c >= 2:
                    pe.wait_ge(self.read, c - 1)
                for i in tiles:
                    r = rows_of(i)
                    mm = pe.transpose(ps[0:r, bank, (i % 4) * P:(i % 4 + 1) * P],
                                      src[:, i * P:i * P + r], ident[:, :])
                mm.then_inc(self.turned, 1)

        def dve(self, dve, m, dst):
            for q, tiles in enumerate(self.PARTS):
                bank = 6 + (3 * m + q) % 2
                dve.wait_ge(self.turned, 3 * m + q + 1)
                r = rows_of(tiles[0])
                dve.tensor_copy(dst[0:r, tiles[0]:tiles[-1] + 1, :],
                                ps[0:r, bank, 0:len(tiles) * P].rearrange("p (i n) -> p i n", n=P)).then_inc(self.read, 1)

    def stage_out(tag, mat, halves, y_tok, a, mov_hi, mov_lo, load):
        w = weight_ring(tag, a)
        yT = a.take(f"yT_{tag}", [P, 2, T])
        squares = a.take(f"squares_{tag}", [P, P])
        nk = halves * KD
        src = Arena(y_at).take(f"mov_{tag}", [P, 4, T])
        s_in = [sem(f"s_in_{tag}{i}") for i in range(4)]
        jobs = [w_tiles(mat, h * KD, KD, n * P, P) for n in range(KD) for h in range(halves)]
        s_high, s_low = sem(f"s_high_{tag}"), sem(f"s_low_{tag}")
        s_yT = sem(f"s_yT_{tag}")
        s_ssq, s_sq = sem(f"s_ssq_{tag}"), sem(f"s_sq_{tag}")
        rows = TokenRows(tag)

        def moving(k):
            return src[:, k % 4]

        with nc.Block() as block:
            @block.sync
            def _(sp):
                def load_moving(k):
                    if k >= 4:
                        sp.wait_ge(s_low, k - 3)
                    sp.dma_start(src[:, k % 4], load[k]).then_inc(s_in[k % 4], 16)

                for j, src_w in enumerate(jobs):
                    stream_weight(sp, w, j, src_w)
                    if j < halves:
                        for k in range(j * KD, (j + 1) * KD):
                            load_moving(k)

            @block.gpsimd
            def _(pool):
                split_weights(pool, w, jobs)

            @block.tensor
            def _(pe):
                for n in range(KD):
                    if n >= 2:
                        pe.wait_ge(s_yT, n - 1)
                    for h in range(halves):
                        product(pe, w, n * halves + h, KD, acc[n % 2], mov_hi, mov_lo, h * KD,
                                first=h == 0, last=h == halves - 1, moving_ready=s_low if n == 0 else None)
                    if n:
                        pe.wait_ge(s_yT, n)
                        rows.pe(pe, n - 1, yT[:, (n - 1) % 2])
                pe.wait_ge(s_yT, KD)
                rows.pe(pe, KD - 1, yT[:, (KD - 1) % 2])

            @block.scalar
            def _(act):
                split_first_high(act, w, jobs[0])
                for k in range(nk):
                    act.wait_ge(s_in[k % 4], 16 * (k // 4 + 1))
                    act.copy(mov_hi[:, k, :], moving(k)).then_inc(s_high, 1)
                def square_rows(n):
                    act.wait_ge(rows.read, 3 * (n + 1))
                    for i in range(TT):
                        r = rows_of(i)
                        if n or i:
                            act.wait_ge(s_sq, n * TT + i)
                        act.activation(squares[0:r, :], y_tok[0:r, i, n * P:(n + 1) * P], ACT.Square,
                                       accum_out=ssq[0:r, i, n:n + 1]).then_inc(s_sq, 1)

                act.wait_ge(s_ssq, 1)
                for n in range(KD):
                    act.wait_ge(w["used"], (n + 1) * halves)
                    if n >= 2:
                        act.wait_ge(rows.turned, 3 * (n - 1))
                    act.copy(as_thirds(yT[:, n % 2]), thirds(acc[n % 2])).then_inc(s_yT, 1)
                    if n:
                        square_rows(n - 1)
                square_rows(KD - 1)

            @block.vector
            def _(dve):
                split_first_low(dve, w, jobs[0])
                dve.memset(ssq[:, :, :], 1.0).then_inc(s_ssq, 1)
                for k in range(nk):
                    dve.wait_ge(s_high, k + 1)
                    dve.tensor_tensor(mov_lo[:, k, :], moving(k), mov_hi[:, k, :].bitcast(F32),
                                      ALU.subtract).then_inc(s_low, 1)
                for n in range(KD):
                    rows.dve(dve, n, y_tok[:, :, n * P:(n + 1) * P])

    y_at = free

    def stage_residual(layer, y_tok, a, x_src, targets):
        tag = f"res{layer}"
        tmp = a.take(f"tmpr{layer}", [P, 4, BANK])
        postg = a.take(f"postg{layer}", [P, D])
        G = a.take(f"G{layer}", [P, 2, D])
        x_in = a.take(f"x_in{layer}", [P, XR, D])
        junk = ps[:, 6:8, :].rearrange("p b n -> p (b n)")
        ss = a.take(f"ssr{layer}", [P, 2, TT])
        rstd = a.take(f"rstdr{layer}", [P, 2, TT])
        s_g, s_gs = sem(f"s_gin_{tag}"), sem(f"s_gsin_{tag}")
        s_in = [sem(f"s_xin_{tag}{i}") for i in range(XR)]
        s_init, s_ss, s_var, s_std = (sem(f"{n}_{tag}") for n in ("s_init", "s_ss", "s_var", "s_std"))
        s_new, s_scaled = [sem(f"s_new{i}_{tag}") for i in range(2)], sem(f"s_scaled_{tag}")
        s_xn, s_out = sem(f"s_xn_{tag}"), s_xout[layer]
        link = chainer(f"dve_chain_{tag}")
        normed = None
        if targets:
            normed = NormedTranspose(f"l{layer + 1}", targets, tmp)

        def add(eng, i):
            r = rows_of(i)
            eng.wait_ge(s_scaled, i + 1)
            eng.wait_ge(s_in[i % XR], 16 * (i // XR + 1))
            eng.tensor_tensor(y_tok[0:r, i, :], y_tok[0:r, i, :], x_in[0:r, i % XR, :], ALU.add).then_inc(s_new[i % 2], 1)

        with nc.Block() as block:
            @block.sync
            def _(sp):
                sp.dma_start(G[:, 0, :], gate_d[layer, 0:1, :].broadcast_to([P, D])).then_inc(s_g, 16)
                sp.dma_start(postg[:, :], post_g[layer:layer + 1, :].broadcast_to([P, D])).then_inc(s_g, 16)
                for b in range(NB):
                    sp.dma_start(G[b * NT:(b + 1) * NT, 1, :], gate_d[layer, 1 + b:2 + b, :].broadcast_to([NT, D])).then_inc(
                        s_gs, 16)
                for i in range(TT):
                    if i >= XR:
                        sp.wait_ge(s_new[(i - XR) % 2], (i - XR) // 2 + 1)
                    sp.dma_start(x_in[0:rows_of(i), i % XR, :], x_src(i)).then_inc(s_in[i % XR], 16)

            @block.gpsimd
            def _(pool):
                for i in range(1, TT, 2):
                    add(pool, i)
                if normed:
                    normed.pool(pool)

            @block.tensor
            def _(pe):
                if normed:
                    normed.pe(pe, y_tok, s_xn, lambda i: i + 1)

            @block.scalar
            def _(act):
                act.wait_ge(s_var, 1)
                act.activation(rstd[:, 0], rstd[:, 0], ACT.Sqrt).then_inc(s_std, 1)
                for i in range(TT):
                    r = rows_of(i)
                    act.wait_ge(s_new[i % 2], i // 2 + 1)
                    if normed:
                        act.dma_start(x1_d[i, 0:r], y_tok[0:r, i, :]).then_inc(s_out, 16)
                        if i:
                            act.wait_ge(s_ss, i)
                        else:
                            act.wait_ge(s_init, 1)
                        act.activation(junk[0:r, :], y_tok[0:r, i, :], ACT.Square,
                                       accum_out=ss[0:r, 1, i:i + 1]).then_inc(s_ss, 1)
                    else:
                        act.dma_start(yp[:, i, :] if i < QB else ys, y_tok[0:r, i, :]).then_inc(s_out, 16)
                if normed:
                    act.wait_ge(s_var, 2)
                    act.activation(rstd[:, 1], rstd[:, 1], ACT.Sqrt).then_inc(s_std, 1)
                    normed.act(act)
                act.wait_ge(s_out, 16 * TT)

            @block.vector
            def _(dve):
                dve.memset(ss[:, 1, :], 1.0).then_inc(s_init, 1)
                link(dve, dve.tensor_reduce(ss[:, 0, :], ssq[:, :, :], AX_X, ALU.add))
                dve.tensor_scalar(rstd[:, 0], ss[:, 0], 1.0 / D, EPS, ALU.mult, ALU.add).then_inc(s_var, 1)
                dve.wait_ge(s_g, 32)
                link(dve, dve.tensor_tensor(G[:, 0], G[:, 0], postg[:, :], ALU.mult))
                dve.wait_ge(s_std, 1)
                link(dve, dve.reciprocal(rstd[:, 0], rstd[:, 0]))
                for i in range(TT):
                    r, q = rows_of(i), i // QB
                    if q:
                        dve.wait_ge(s_gs, 16 * NB)
                        link(dve, dve.tensor_tensor(G[0:NS, 1], G[0:NS, 1], postg[0:NS, :], ALU.mult))
                    dve.scalar_tensor_tensor(out=y_tok[0:r, i, :], in0=y_tok[0:r, i, :],
                                             scalar=rstd[0:r, 0, i:i + 1], in1=G[0:r, q, :],
                                             op0=ALU.mult, op1=ALU.mult).then_inc(s_scaled, 1)
                    if i % 2 == 1:
                        add(dve, i - 1)
                add(dve, TT - 1)
                if normed:
                    dve.wait_ge(s_ss, TT)
                    dve.tensor_scalar(rstd[:, 1], ss[:, 1], 1.0 / D, EPS, ALU.mult, ALU.add).then_inc(s_var, 1)
                    dve.wait_ge(s_std, 2)
                    link(dve, dve.reciprocal(rstd[:, 1], rstd[:, 1]))
                    dve.wait_ge(s_out, 16 * TT)
                    for i in range(TT):
                        r = rows_of(i)
                        dve.tensor_scalar(y_tok[0:r, i, :], y_tok[0:r, i, :], rstd[0:r, 1, i:i + 1], None,
                                          ALU.mult).then_inc(s_xn, 1)
                    normed.dve(dve, link)

    def stage_projections():
        a = Arena(free)
        w = weight_ring("c", a)
        o = a.take("o", [P, 2, T])
        tk = a.take("tk", [P, 2, TT, P])
        fx = a.take("fx", [NH, T])
        fe = a.take("fe", [NH, T])
        lfT = a.take("lfT", [NH, T])
        F = a.take("F", [NH, SEQ])
        fb = a.take("fb", [NH, 1])
        lrow = a.take("lrow", [P, TT, NH])
        kinds = [("k", p) for p in range(NP)] + [(x, p) for x in "vqz" for p in range(NP)]
        kinds.insert(2, ("f", 0))
        W = NH * HD
        col = {"k": (kv_w, 0), "v": (kv_w, W), "f": (kv_w, 2 * W), "q": (b_in_w[0], 0), "z": (b_in_w[0], W)}
        jobs = [w_tiles(col[x][0], 0, KD, col[x][1] + p * P, NH if x == "f" else P) for x, p in kinds]
        tiles = [x for x in kinds if x[0] != "f"]
        order = {x: m for m, x in enumerate(tiles)}
        turn = {x: m for m, x in enumerate(t for t in tiles if t[0] in "kv")}
        store = {"k": kT_d, "q": qT_d, "z": zT_d}

        assert a.at <= LF_at
        s_pt, s_lfc = sem("s_pt"), sem("s_lfc")
        s_o = sem("s_o")
        s_oout = [sem(f"s_oout{i}") for i in range(2)]
        s_fb, s_fx, s_fe, s_lf, s_F, s_ones = (sem(n) for n in ("s_fb", "s_fx", "s_fe", "s_lf", "s_F", "s_ones"))
        s_lT, s_lrow = sem("s_lT"), sem("s_lrow")
        link, alink = chainer("dve_chain4"), chainer("act_chain4")
        rows = TokenRows("c")
        outs_before = {}
        count = [0, 0]
        for x, m in order.items():
            outs_before[x] = count[m % 2]
            count[m % 2] += x[0] in store

        def store_rows(act, x):
            t = turn[x]
            act.wait_ge(rows.read, 3 * (t + 1))
            big, small = (kp, ks) if x[0] == "k" else (vp, vs)
            c = slice(x[1] * P, (x[1] + 1) * P)
            act.dma_start(big[:, :, c], tk[:, t % 2, 0:QB, :]).then_inc(s_tout[t % 2], 16)
            act.dma_start(small[:, c], tk[0:NS, t % 2, QB, :]).then_inc(s_tout[t % 2], 16)

        with nc.Block() as block:
            @block.sync
            def _(sp):
                with nc.allow_non_contiguous_dma(reason="one value a head"):
                    sp.dma_start(fb[:, :], f_b.rearrange("(h a) -> h a", a=1)).then_inc(s_fb, 16)
                sp.dma_start(pt[:, :], page_table.rearrange("(a b) g -> a (b g)", a=1)).then_inc(s_pt, 16)
                sp.wait_ge(s_pt, 16)
                reg = sp.alloc_register("page4")
                for j, src in enumerate(jobs):
                    stream_weight(sp, w, j, src)
                    for t in range(4 * j, min(4 * j + 4, NB * NPG)):
                        sp.reg_load(reg, pt[0:1, t:t + 1])
                        page = bass.ds(sp.snap(reg, min_val=0, max_val=n_phys - 1), 1)
                        sp.dma_start(LF[:, t % NPG, t // NPG * NH:(t // NPG + 1) * NH],
                                     cache_logf[page].rearrange("a k h -> (a k) h")).then_inc(s_lfc, 16)
                sp.wait_ge(s_lfc, 16 * NB * NPG)

            @block.gpsimd
            def _(pool):
                split_weights(pool, w, jobs)

            @block.tensor
            def _(pe):
                late = None
                for n, x in enumerate(kinds):
                    if n >= 2:
                        was = kinds[n - 2]
                        if was[0] == "f":
                            pe.wait_ge(s_fx, 1)
                        else:
                            pe.wait_ge(s_o, order[was] + 1)
                    product(pe, w, n, KD, acc[n % 2], actH, actL, 0 if x[0] in "kvf" else KD)
                    if late:
                        pe.wait_ge(s_o, order[late] + 1)
                        rows.pe(pe, turn[late], o[:, order[late] % 2])
                    late = x if x[0] in "kv" else None
                pe.wait_ge(s_lf, 1)
                pe.wait_ge(s_F, 1)
                pe.wait_ge(s_o, len(tiles))
                for i in range(TT):
                    r = rows_of(i)
                    mm = pe.transpose(ps[0:r, 0, i * NH:(i + 1) * NH], lfT[:, i * P:i * P + r], ident[0:NH, 0:NH])
                for i in range(QB):
                    mm = pe.transpose(ps[:, 0, (TT + i) * NH:(TT + i + 1) * NH], F[:, i * P:(i + 1) * P],
                                      ident[0:NH, 0:NH])
                mm.then_inc(s_lT, 1)

            @block.scalar
            def _(act):
                split_first_high(act, w, jobs[0])
                late = None
                for n, x in enumerate(kinds):
                    if x[0] == "f":
                        act.wait_ge(s_fx, 1)
                        alink(act, act.activation(fe[:, :], fx[:, :], ACT.Abs))
                        alink(act, act.activation(fe[:, :], fe[:, :], ACT.Exp, scale=-1.0))
                        act.activation(fe[:, :], fe[:, :], ACT.Ln, bias=1.0).then_inc(s_fe, 1)
                        continue
                    m = order[x]
                    act.wait_ge(w["used"], n + 1)
                    if outs_before[x]:
                        act.wait_ge(s_oout[m % 2], 16 * outs_before[x])
                    if m >= 2 and tiles[m - 2][0] in "kv":
                        act.wait_ge(rows.turned, 3 * (turn[tiles[m - 2]] + 1))
                    dst, src = as_thirds(o[:, m % 2]), thirds(acc[n % 2])
                    if x[0] == "z":
                        act.activation(dst, src, ACT.Silu).then_inc(s_o, 1)
                    elif x[0] == "q":
                        act.activation(dst, src, ACT.Copy, scale=HD ** -0.5).then_inc(s_o, 1)
                    else:
                        act.copy(dst, src).then_inc(s_o, 1)
                    if late:
                        store_rows(act, late)
                    late = x if x[0] in "kv" else None
                    if x[0] in store:
                        act.wait_ge(s_o, m + 1)
                        act.dma_start(store[x[0]][x[1]], o[:, m % 2]).then_inc(s_oout[m % 2], 16)
                act.wait_ge(s_F, 1)
                act.wait_ge(s_lrow, 1)
                act.dma_start(negF_d, fe[:, 0:SEQ]).then_inc(s_lout, 16)
                act.dma_start(lfp, lrow[:, 0:QB, :]).then_inc(s_lout, 16)
                act.dma_start(lfs, lrow[0:NS, QB, :]).then_inc(s_lout, 16)
                act.wait_ge(s_lout, 48)
                for i in range(2):
                    act.wait_ge(s_oout[i], 16 * count[i])
                    act.wait_ge(s_tout[i], 32 * NP)

            @block.vector
            def _(dve):
                split_first_low(dve, w, jobs[0])
                dve.memset(F[:, :], 1.0).then_inc(s_ones, 1)
                for n, x in enumerate(kinds):
                    if x[0] == "f":
                        dve.wait_ge(w["used"], n + 1)
                        dve.wait_ge(s_fb, 16)
                        dve.tensor_scalar(as_thirds(fx[:, :]), acc[n % 2][0:NH, :, 0:CH], fb[:, 0:1], None,
                                          ALU.add).then_inc(s_fx, 1)
                        dve.wait_ge(s_fe, 1)
                        dve.wait_ge(s_fx, 1)
                        link(dve, dve.tensor_scalar(fx[:, :], fx[:, :], 0.0, None, ALU.min))
                        dve.tensor_tensor(lfT[:, :], fx[:, :], fe[:, :], ALU.subtract).then_inc(s_lf, 1)
                        dve.wait_ge(s_lf, 1)
                        dve.wait_ge(s_ones, 1)
                        link(dve, dve.tensor_tensor_scan(fx[:, 0:SEQ], F[:, :], lfT[:, 0:SEQ], 0.0,
                                                         op0=ALU.mult, op1=ALU.add))
                        link(dve, dve.tensor_scalar(fe[:, 0:SEQ], fx[:, 0:SEQ], -1.0, None, ALU.mult))
                        dve.tensor_copy(F[:, :], fx[:, 0:SEQ]).then_inc(s_F, 1)
                    elif x[0] in "kv":
                        t = turn[x]
                        if t >= 2:
                            dve.wait_ge(s_tout[t % 2], 32 * (t // 2))
                        rows.dve(dve, t, tk[:, t % 2])
                dve.wait_ge(s_lT, 1)
                link(dve, dve.tensor_copy(lrow[:, 0:QB, :], ps[:, 0, 0:QB * NH].rearrange("p (i h) -> p i h", h=NH)))
                link(dve, dve.tensor_copy(lf_s[:, :], ps[0:NS, 0, QB * NH:TT * NH]))
                link(dve, dve.tensor_copy(Ftok[:, :, :], ps[:, 0, TT * NH:(TT + QB) * NH].rearrange(
                    "p (i h) -> p i h", h=NH)))
                dve.tensor_copy(lrow[0:NS, QB, :], lf_s[:, :]).then_inc(s_lrow, 1)

    def stage_attention():
        a = Arena(act_at)
        KT_at = a.at
        KTh = a.take("KTh", [P, 2, NP, 2 * P], F32R)
        KTl = a.take("KTl", [P, 2, NP, 2 * P], F32R)
        KT_end = a.at
        Vh = a.take("Vh", [P, VR, D], F32R)
        Vl = a.take("Vl", [P, VR, D], F32R)
        qT = a.take("qT", [P, 2, SEQ])
        kT = a.take("kT", [P, 2, SEQ])
        zT = a.take("zT", [P, 2, SEQ])
        Vt = a.take("Vt", [P, 2, QB, P])
        nF = a.take("nF", [P, 2, SEQ])
        Sb = [a.take("S_short", [P, BANK]), a.take("S_long", [P, SEQ])]
        PT = [a.take("PT_short", [P, BANK]), a.take("PT_long0", [P, SEQ])]
        PT = [PT[0], PT[1], PT[0], a.take("PT_long1", [P, SEQ])]
        o_tok = a.take("o_tok", [P, 2, QB, P])
        nmax = a.take("nmax", [P, 4])
        rsum = a.take("rsum", [P, 4])
        rinv = a.take("rinv", [P, 4])
        q_s = a.take("q_s", [P, NP, NS])
        k_s = a.take("k_s", [P, NP, NS])
        z_s = a.take("z_s", [P, NP, NS])
        v_s = a.take("v_s", [NS, D])
        qblk = a.take("qblk", [P, NP, NB, 2 * NT])
        QW = P + 2 * NT
        qst = a.take("qst", [P, 2, NP * QW], F32R)
        newT = a.take("newT", [NS, NB, NP, 2 * NT])
        Sd = a.take("Sd", [NR, 2, PAST + NS])
        Slo = a.take("Slo", [NR, 2 * P])
        PTd = a.take("PTd", [P, NPG, 2 * NR], F32R)
        PTn = a.take("PTn", [NS, 2 * NR])
        O_sb = a.take("O_sb", [P, D])
        J = a.take("J", [P, 3 * NR])
        E_all = a.take("E_all", [P, NB, P])
        G = a.take("Gf", [P, PAST + NS])
        nmask = a.take("nmask", [NR, 2 * NS - NT])
        dstat = a.take("dstat", [NR, 2, 4])
        zero = a.take("zero", [P, 1])
        ogp = a.take("ogp", [P, 2, SEQ])
        ogs = a.take("ogs", [P, NP, NS])
        assert a.at <= K_at, a.at - K_at
        a = Arena(K_at)
        K = a.take("K", [P, KR, D])
        V = a.take("V", [P, VR, D])
        b = Arena(KT_at)
        LT = b.take("LT", [P, PAST + NT])
        Fs = b.take("Fs", [P, PAST + NT])
        X = b.take("X", [NS, NB, NH])
        bm = b.take("bm", [NS, NB, NH])
        tsel = b.take("tsel", [NS, NT])
        one = b.take("one", [P, 1])
        mpre = b.take("mpre", [NR, NH, 2 * NS - NT])
        assert b.at <= KT_end

        ORDER = (0, 7, 1, 6, 2, 5, 3, 4)
        UN = 2 * QB
        NU = NP * UN
        PAGES = NB * NPG
        V0 = UN + 6
        STEPS = PAGES + V0 + 1
        G_OUT, G_PTD, G_PTN, G_PTD2, G_OS = (2, 3), 4, 5, 7, 6

        def unit(u):
            return u // UN, u % UN // QB, ORDER[u % QB]

        def s_bank(u):
            return ps[:, 2, :] if u % 2 == 0 else ps[:, 0:2, :].rearrange("p b n -> p (b n)")

        def side_work(s):
            g, r = s % UN, s // UN - 1
            if r < 0:
                return None
            if g in G_OUT and r < NP:
                return "out", r, G_OUT.index(g)
            if g in (G_PTD, G_PTN, G_PTD2) and r < NB:
                return "probs", r, (G_PTD, G_PTN, G_PTD2).index(g)
            if g == G_OS and 1 <= r <= NB:
                return "sample", r - 1, 0
            return None

        s_set = sem("s_set")
        s_pair = [sem(f"s_pair{i}") for i in range(2)]
        s_nF = [sem(f"s_nF{i}") for i in range(2)]
        s_K = [sem(f"s_K{i}") for i in range(KR)]
        s_V = [sem(f"s_V{i}") for i in range(VR)]
        s_VK = [sem(f"s_VK{i}") for i in range(KR)]
        s_c, s_ones = sem("s_cst5"), sem("s_ones5")
        s_lT5, s_LT, s_X, s_newf, s_G5 = (sem(n) for n in ("s_lT5", "s_LT", "s_X", "s_newf", "s_G5"))
        s_qst, s_nT, s_newT = sem("s_qst"), sem("s_nT"), sem("s_newT")
        s_S, s_bias, s_mask, s_max, s_exp = (sem(n) for n in ("s_S", "s_bias", "s_mask", "s_max", "s_exp"))
        s_PT, s_PTe, s_O, s_On = (sem(n) for n in ("s_PT", "s_PTe", "s_O", "s_On"))
        s_Kt, s_Kh, s_Kl, s_sc, s_Slo, s_rowe = (sem(n) for n in ("s_Kt", "s_Kh", "s_Kl", "s_sc", "s_Slo", "s_rowe"))
        s_Vh, s_Vl = sem("s_Vh"), [sem(f"s_Vl{i}") for i in range(VR)]
        s_qs, s_side_hi, s_ogd = sem("s_qs"), sem("s_side_hi"), [sem(f"s_ogd{i}") for i in range(2)]
        s_dmax, s_dexp, s_dn = sem("s_dmax"), sem("s_dexp"), sem("s_dn")
        s_pv, s_osb = sem("s_pv"), sem("s_osb")
        s_side, s_side_read = sem("s_side"), sem("s_side_read")
        link, plink = chainer("dve_chain5"), chainer("pool_chain5")
        k_rows, v_rows = cache_k.rearrange("g k h d -> g k (h d)"), cache_v.rearrange("g k h d -> g k (h d)")
        NPAIR = 4

        sides_before = [sum(side_work(x) is not None for x in range(s)) for s in range(STEPS + 1)]

        loads = []
        for t in range(PAGES):
            loads.append((t - KR + 0.3, "K", t))
            loads.append((t + V0 - VR - 0.4, "V", t))
        for p in range(1, NP):
            loads.append((UN * (p - 1) + 5.7, "pair", p))
            loads.append((UN * p - QB + 3.8, "nF", 2 * p))
        for p in range(NP):
            loads.append((UN * p + 3.8 if p else -9.0, "nF", 2 * p + 1))
        loads.sort()

        TAIL = PAGES - V0
        rest = [(K, x % KR) for x in range(PAGES - KR, PAGES)] + [(V, (TAIL + x) % VR) for x in range(VR)]
        places, last, landed = [], {("K", x % KR): ("K", x) for x in range(PAGES - KR, PAGES)}, {}
        for t in range(PAGES):
            buf, i = (V, t % VR) if t < TAIL else rest[(t - TAIL) % len(rest)]
            key = ("K" if buf is K else "V", i)
            landed[key] = landed.get(key, 0) + 16
            places.append((buf[:, i], s_V[i] if buf is V else s_VK[i], landed[key], last.get(key)))
            last[key] = ("V", t)

        def dve_splits(t):
            return t + V0 - 1 >= NU

        def V_low(eng, t):
            eng.wait_ge(s_Vh, t + 1)
            eng.tensor_tensor(Vl[:, t % VR], places[t][0], Vh[:, t % VR].bitcast(F32), ALU.subtract).then_inc(
                s_Vl[t % VR], 1)

        with nc.Block() as block:
            @block.sync
            def _(sp):
                def pair_loads(p):
                    i = p % 2
                    if p >= 2:
                        sp.wait_ge(s_S, UN * (p - 1))
                        sp.wait_ge(s_O, UN * (p - 1))
                        sp.wait_ge(s_side_read, sides_before[UN * (p - 1) + G_OUT[1]] + 1)
                    sp.dma_start(qT[:, i], qT_d[p, :, 0:SEQ]).then_inc(s_pair[i], 16)
                    sp.dma_start(kT[:, i], kT_d[p, :, 0:SEQ]).then_inc(s_pair[i], 16)
                    sp.dma_start(zT[:, i], zT_d[p, :, 0:SEQ]).then_inc(s_pair[i], 16)
                    sp.dma_start(Vt[:, i], vp[:, :, p * P:(p + 1) * P]).then_inc(s_pair[i], 16)

                def head_load(h):
                    if h >= 2:
                        sp.wait_ge(s_bias, QB * (h - 1))
                    sp.dma_start(nF[:, h % 2], negF_d[h:h + 1, :].broadcast_to([P, SEQ])).then_inc(s_nF[h % 2], 16)

                sp.dma_start(q_s[:, :, :], qT_d[:, :, SEQ:T].rearrange("k p n -> p k n")).then_inc(s_set, 16)
                sp.dma_start(k_s[:, :, :], kT_d[:, :, SEQ:T].rearrange("k p n -> p k n")).then_inc(s_set, 16)
                sp.dma_start(z_s[:, :, :], zT_d[:, :, SEQ:T].rearrange("k p n -> p k n")).then_inc(s_set, 16)
                sp.dma_start(v_s[:, :], vs).then_inc(s_set, 16)
                reg = sp.alloc_register("page5")

                def page(t):
                    sp.reg_load(reg, pt[0:1, t:t + 1])
                    return bass.ds(sp.snap(reg, min_val=0, max_val=n_phys - 1), 1)

                pair_loads(0)
                head_load(0)
                for _, what, t in loads:
                    if what == "pair":
                        pair_loads(t)
                    elif what == "nF":
                        head_load(t)
                    elif what == "K":
                        if t >= KR:
                            sp.wait_ge(s_Kt, t - KR + 1)
                        sp.dma_start(K[:, t % KR], k_rows[page(t)].rearrange("a k n -> (a k) n")).then_inc(
                            s_K[t % KR], 16)
                    else:
                        if t == 0:
                            sp.wait_ge(s_lT5, 1)
                        dst, signal, _, before = places[t]
                        if before:
                            x = before[1]
                            if before[0] == "V":
                                sp.wait_ge(s_Vl[x % VR], x // VR + 1)
                            else:
                                sp.wait_ge(s_Kt, x + 1)
                        sp.dma_start(dst, v_rows[page(t)].rearrange("a k n -> (a k) n")).then_inc(signal, 16)

            @block.gpsimd
            def _(pool):
                pool.memset(qblk[:, :, :, :], 0.0).then_inc(s_ones, 1)
                pool.memset(zero[:, :], 0.0).then_inc(s_ones, 1)
                pool.memset(PTn[:, :], 0.0).then_inc(s_ones, 1)
                pool.memset(bm[:, :, :], 1.0).then_inc(s_ones, 1)
                pool.memset(one[:, :], 1.0).then_inc(s_ones, 1)
                pool.memset(E_all[:, :, :], 0.0).then_inc(s_ones, 1)
                pool.memset(mpre[:, :, :], 1.0).then_inc(s_ones, 1)
                pool.wait_ge(s_ones, 7)
                v = bm[:, :, :]
                plink(pool, pool.affine_select(out=v, in_=v, compare_op=ALU.is_ge, fill=0.0, base=0,
                                               pattern=[[-NT, NB], [0, NH]], channel_multiplier=1))
                pool.affine_select(out=v, in_=v, compare_op=ALU.is_ge, fill=0.0, base=NT - 1,
                                   pattern=[[NT, NB], [0, NH]], channel_multiplier=-1).then_inc(s_c, 1)
                v = E_all[:, :, 0:NR].rearrange("p b (h q) -> p b h q", q=NT)
                plink(pool, pool.affine_select(out=v, in_=v, compare_op=ALU.not_equal, fill=1.0, base=0,
                                               pattern=[[-NH, NB], [-1, NH], [0, NT]], channel_multiplier=1))
                pool.tensor_copy(qst[:, :, :].rearrange("p s w -> p (s w)"),
                                 zero[:, 0:1].broadcast_to([P, 2 * NP * QW])).then_inc(s_qs, 1)
                v, n = mpre[:, :, :], 2 * NS - NT
                plink(pool, pool.affine_select(out=v, in_=v, compare_op=ALU.is_ge, fill=0.0, base=NS - NT,
                                               pattern=[[-NT, NH], [-1, n]], channel_multiplier=1))
                plink(pool, pool.affine_select(out=v, in_=v, compare_op=ALU.is_ge, fill=0.0, base=NT - 1,
                                               pattern=[[NT, NH], [0, n]], channel_multiplier=-1))
                pool.affine_select(out=v, in_=v, compare_op=ALU.is_ge, fill=0.0, base=-(NS - NT),
                                   pattern=[[0, NH], [1, n]], channel_multiplier=0).then_inc(s_c, 1)

                def mask(u):
                    i = unit(u)[2]
                    pool.wait_ge(s_bias, u + 1)
                    blk = Sb[u % 2][:, i * P:(i + 1) * P]
                    pool.affine_select(out=blk, in_=blk, compare_op=ALU.is_ge, fill=NEG, base=0,
                                       pattern=[[-1, P]], channel_multiplier=1).then_inc(s_mask, 1)

                mask(0)
                for s in range(STEPS):
                    if s + 1 < NU:
                        mask(s + 1)
                    if 0 <= s + 1 - V0 < PAGES and not dve_splits(s + 1 - V0):
                        V_low(pool, s + 1 - V0)

            @block.tensor
            def _(pe):
                for g in range(NPG):
                    mm = pe.transpose(ps[:, g // 4, g % 4 * P:(g % 4 + 1) * P], LF[:, g, :], ident[:, :])
                mm.then_inc(s_lT5, 1)
                pe.wait_ge(s_X, 2)
                pe.matmul(ps[:, 4, 0:NT], X[:, :, :].rearrange("p b h -> p (b h)"), tsel[:, :],
                          start=True, stop=True).then_inc(s_newf, 1)
                pe.wait_ge(s_qst, 2)
                pe.wait_ge(s_set, 64)
                for p in range(NP):
                    mm = pe.matmul(ps[0:NS, 5, p * NR:(p + 1) * NR], k_s[:, p, :],
                                   qblk[:, p].rearrange("p b c -> p (b c)"), start=True, stop=True)
                mm.then_inc(s_nT, 1)

                def scores(u):
                    p, h, i = unit(u)
                    if u % UN == 0:
                        pe.wait_ge(s_pair[p % 2], 16 * NPAIR * (p // 2 + 1))
                    if u >= 2:
                        pe.wait_ge(s_PTe, u - 1)
                    n, bank, hs = (i + 1) * P, s_bank(u), slice(h * HD, (h + 1) * HD)
                    for c in range(0, n, BANK):
                        e = min(c + BANK, n)
                        mm = pe.matmul(bank[:, c:e], qT[hs, p % 2, i * P:(i + 1) * P], kT[hs, p % 2, c:e],
                                       start=True, stop=True)
                    mm.then_inc(s_S, 1)

                def turn_probs(u):
                    i, bank = unit(u)[2], s_bank(u)
                    pe.wait_ge(s_exp, u + 1)
                    for j in range(i + 1):
                        mm = pe.transpose(bank[:, j * P:(j + 1) * P], Sb[u % 2][:, j * P:(j + 1) * P], ident[:, :])
                    mm.then_inc(s_PT, 1)

                def values(u):
                    p, h, i = unit(u)
                    pe.wait_ge(s_PTe, u + 1)
                    for j in range(i + 1):
                        mm = pe.matmul(ps[:, 3, 0:P], PT[u % 4][:, j * P:(j + 1) * P],
                                       Vt[:, p % 2, j, :], start=(j == 0), stop=(j == i))
                    mm.then_inc(s_O, 1)

                def turn_K(t):
                    pe.wait_ge(s_K[t % KR], 16 * (t // KR + 1))
                    if t:
                        pe.wait_ge(s_Kl, 2 * t)
                    for c in range(NP):
                        mm = pe.transpose(ps[:, 6 + c // 4, c % 4 * P:(c % 4 + 1) * P],
                                          K[:, t % KR, c * P:(c + 1) * P], ident[:, :])
                    mm.then_inc(s_Kt, 1)

                def page_scores(j):
                    bq, g = j // (NPG // 2), j % (NPG // 2)
                    pe.wait_ge(s_Kl, 4 * (j + 1))
                    if g == 0:
                        pe.wait_ge(s_qs, 2 + bq)
                    out = ps[:, 3, P:3 * P]
                    pe.matmul(out, E_all[:, bq, :], G[:, 2 * g * P:2 * (g + 1) * P], start=True, stop=False)
                    for c in range(NP):
                        for kt in (KTh, KTl):
                            mm = pe.matmul(out, qst[:, bq % 2, c * P:(c + 1) * P], kt[:, j % 2, c, :],
                                           start=False, stop=(c == NP - 1 and kt is KTl))
                    if g == NPG // 2 - 1:
                        out = ps[0:NR, 3, 3 * P:3 * P + NS]
                        pe.matmul(out, E_all[:, bq, 0:NR], G[:, PAST:PAST + NS], start=True, stop=False)
                        mm = pe.matmul(out, newT[:, bq].rearrange("n k c -> n (k c)"), ident[0:NS, 0:NS],
                                       start=False, stop=True)
                    mm.then_inc(s_sc, 1)

                def page_values(t):
                    bq, g = t // NPG, t % NPG
                    pe.wait_ge(s_Vl[t % VR], t // VR + 1)
                    if g == 0:
                        pe.wait_ge(s_side_read, sides_before[UN * (bq + 1) + G_PTN] + 1)
                        if bq:
                            pe.wait_ge(s_osb, bq)
                        for c in range(2):
                            pe.matmul(ps[:, 4 + c, :], PTn[:, :], v_s[:, c * BANK:(c + 1) * BANK],
                                      start=True, stop=False)
                    if g == NPG // 2:
                        pe.wait_ge(s_side_read, sides_before[UN * (bq + 1) + G_PTD2] + 1)
                    for v in (Vh, Vl):
                        for c in range(2):
                            mm = pe.matmul(ps[:, 4 + c, :], PTd[:, g, :], v[:, t % VR, c * BANK:(c + 1) * BANK],
                                           start=False, stop=(g == NPG - 1 and v is Vl))
                    mm.then_inc(s_pv, 1)

                def side(s, what, r, part):
                    if s < PAGES:
                        pe.wait_ge(s_Kl, 2 * s + 1)
                    else:
                        pe.wait_ge(s_side_read, sides_before[s])
                    if what == "out":
                        pe.wait_ge(s_On, UN * (r + 1))
                        for i in range(4):
                            mm = pe.transpose(ps[:, 6, i * P:(i + 1) * P], o_tok[:, r % 2, 4 * part + i, :],
                                              ident[:, :])
                    elif what == "sample":
                        pe.wait_ge(s_osb, r + 1)
                        for c in range(NP):
                            mm = pe.matmul(ps[:, 6, 8 * c:8 * c + P], O_sb[:, c * P:(c + 1) * P],
                                           J[:, 8 * c:8 * c + P], start=True, stop=True)
                    elif part == 1:
                        mm = pe.transpose(ps[0:NS, 6, 0:NR], Sd[:, r % 2, PAST:PAST + NS], ident[0:NR, 0:NR])
                    else:
                        pe.wait_ge(s_dn, r + 1)
                        for g in range(8):
                            at = (4 * part + g) * P
                            mm = pe.transpose(ps[:, 6, g * NR:(g + 1) * NR], Sd[:, r % 2, at:at + P],
                                              ident[0:NR, 0:NR])
                    mm.then_inc(s_side, 1)

                pe.wait_ge(s_LT, 1)
                scores(0)
                scores(1)
                pe.wait_ge(s_newT, 1)
                pe.wait_ge(s_G5, 1)
                for s in range(STEPS):
                    if s < PAGES:
                        if sides_before[s]:
                            pe.wait_ge(s_side_read, sides_before[s])
                        turn_K(s)
                    if s < NU and s % 2 == 1:
                        turn_probs(s)
                    if 2 <= s < NU + 2:
                        if s >= 3:
                            pe.wait_ge(s_On, s - 2)
                            pe.wait_ge(s_rowe, (s - 1) // 2)
                        values(s - 2)
                    if s < NU and s % 2 == 0:
                        turn_probs(s)
                    if V0 <= s < V0 + PAGES:
                        page_values(s - V0)
                    if side_work(s):
                        side(s, *side_work(s))
                    if 2 <= s <= PAGES and s % 2 == 0:
                        pe.wait_ge(s_On, s - 1)
                        page_scores(s // 2 - 1)
                    if s + 2 < NU:
                        scores(s + 2)

            @block.scalar
            def _(act):
                act.wait_ge(s_lT5, 1)
                act.copy(LT[:, 0:PAST].rearrange("p (b n) -> p b n", b=4), ps[:, 0:4, :]).then_inc(s_LT, 1)
                act.wait_ge(s_newf, 1)
                act.copy(LT[:, PAST:PAST + NT], ps[:, 4, 0:NT]).then_inc(s_LT, 1)

                def exps(u):
                    n, t = (unit(u)[2] + 1) * P, Sb[u % 2]
                    act.wait_ge(s_max, u + 1)
                    act.activation(t[:, 0:n], t[:, 0:n], ACT.Exp, bias=nmax[:, u % 4:u % 4 + 1],
                                   accum_out=rsum[:, u % 4:u % 4 + 1]).then_inc(s_exp, 1)

                exps(0)
                for s in range(STEPS):
                    r, work = s // UN - 1, side_work(s)
                    if s >= 3 and s % 2 == 1 and s <= PAGES + 1:
                        j = (s - 3) // 2
                        act.wait_ge(s_sc, j + 1)
                        if j:
                            act.wait_ge(s_rowe, j)
                        act.copy(Slo[:, :], ps[NR:P, 3, P:3 * P]).then_inc(s_Slo, 1)
                    t = s + 1 - V0
                    if 0 <= t < PAGES:
                        src, signal, count, _ = places[t]
                        act.wait_ge(signal, count)
                        if t >= VR:
                            act.wait_ge(s_pv, t - VR + 1)
                        act.copy(Vh[:, t % VR], src).then_inc(s_Vh, 1)
                    if s < PAGES:
                        act.wait_ge(s_Kt, s + 1)
                        if s >= 4:
                            act.wait_ge(s_sc, s // 2 - 1)
                        for h in range(2):
                            act.copy(KTh[:, s // 2 % 2, 4 * h:4 * h + 4, s % 2 * P:(s % 2 + 1) * P],
                                     ps[:, 6 + h, :].rearrange("p (c n) -> p c n", c=4)).then_inc(s_Kh, 1)
                    if s < NU:
                        n = (unit(s)[2] + 1) * P
                        act.wait_ge(s_PT, s + 1)
                        if s >= 2:
                            act.wait_ge(s_O, s - 1 if s % 2 == 0 else max(s - 3, 1))
                        act.copy(PT[s % 4][:, 0:n], s_bank(s)[:, 0:n]).then_inc(s_PTe, 1)
                    if work and work[0] == "probs":
                        act.wait_ge(s_side, sides_before[s] + 1)
                        if work[2] == 1:
                            act.copy(PTn[:, 0:NR], ps[0:NS, 6, 0:NR]).then_inc(s_side_read, 1)
                        else:
                            h = 4 * work[2]
                            act.copy(PTd[:, h:h + 8, 0:NR],
                                     ps[:, 6, :].rearrange("p (g r) -> p g r", g=8)).then_inc(s_side_hi, 1)
                    if s + 1 < NU:
                        exps(s + 1)
                    if s >= V0 and (s - V0) % NPG == NPG - 1:
                        bv = (s - V0) // NPG
                        if bv < NB:
                            act.wait_ge(s_pv, NPG * (bv + 1))
                            if bv:
                                act.wait_ge(s_side, sides_before[UN * (bv + 1) + G_OS] + 1)
                            act.copy(O_sb[:, :].rearrange("p (b n) -> p b n", b=2), ps[:, 4:6, :]).then_inc(s_osb, 1)
                    if 0 <= r < NB and s % UN == 2:
                        st = dstat[:, r % 2]
                        act.wait_ge(s_dmax, r + 1)
                        act.activation(Sd[:, r % 2, :], Sd[:, r % 2, :], ACT.Exp, bias=st[:, 0:1],
                                       accum_out=st[:, 1:2]).then_inc(s_dexp, 1)
                    if 0 <= r < NP and s % UN == 4:
                        act.wait_ge(s_side_read, sides_before[s])
                        act.dma_start(og_d[r, :, 0:SEQ], ogp[:, r % 2]).then_inc(s_ogd[r % 2], 16)
                act.wait_ge(s_side_read, sides_before[STEPS])
                act.dma_start(og_d[:, :, SEQ:T].rearrange("k p n -> p k n"), ogs[:, :, :]).then_inc(s_ogd[0], 16)
                act.wait_ge(s_ogd[0], 16 * (NP // 2 + 1))
                act.wait_ge(s_ogd[1], 16 * (NP // 2))

            @block.vector
            def _(dve):
                dve.wait_ge(s_c, 1)
                dve.tensor_tensor(X[:, :, :], bm[:, :, :], lf_s[:, :].unsqueeze(1).broadcast_to([NS, NB, NH]),
                                  ALU.mult).then_inc(s_X, 1)
                dve.tensor_reduce(tsel[:, :], ident[0:NS, 0:NS].rearrange("p (b t) -> p t b", t=NT), AX_X,
                                  ALU.add).then_inc(s_X, 1)
                dve.wait_ge(s_set, 64)
                for h in range(2):
                    r = slice(h * HD, (h + 1) * HD)
                    dve.tensor_copy(qblk[r, :, :, h * NT:(h + 1) * NT],
                                    q_s[r, :, :].rearrange("p k (b t) -> p k b t", t=NT)).then_inc(s_qst, 1)
                for i in range(3):
                    dve.tensor_tensor(J[:, i * NR:(i + 1) * NR], ident[:, 0:NR], ident[:, NR:P], ALU.add)

                def queries(bq):
                    if bq >= 2:
                        dve.wait_ge(s_sc, NPG // 2 * (bq - 1))
                    q4 = qst[:, bq % 2].rearrange("p (c w) -> p c w", w=QW)
                    hi = q4[:, :, 0:2 * NT]
                    link(dve, dve.tensor_copy(hi, qblk[:, :, bq, :]))
                    dve.tensor_tensor(q4[:, :, NR:NR + 2 * NT], qblk[:, :, bq, :], hi.bitcast(F32),
                                      ALU.subtract).then_inc(s_qs, 1)

                dve.wait_ge(s_LT, 2)
                n = PAST + NT
                link(dve, dve.tensor_tensor_scan(Fs[:, :], one[:, 0:1].broadcast_to([P, n]), LT[:, :], 0.0,
                                                 op0=ALU.mult, op1=ALU.add))
                link(dve, dve.tensor_scalar(Fs[:, :], Fs[:, :], Fs[:, n - 1:n], -1.0, ALU.subtract, ALU.mult))
                dve.tensor_copy(G[:, 0:PAST], Fs[:, 0:PAST])
                link(dve, dve.tensor_copy(G[:, PAST:PAST + NS].rearrange("p (b t) -> p b t", b=NB),
                                          Fs[:, PAST:n].unsqueeze(1).broadcast_to([P, NB, NT])))
                dve.wait_ge(s_qs, 1)
                dve.wait_ge(s_qst, 2)
                queries(0)
                dve.wait_ge(s_c, 2)
                link(dve, dve.tensor_reduce(nmask[:, :], mpre[:, :, :].rearrange("p h c -> p c h"), AX_X, ALU.add))
                dve.tensor_scalar(nmask[:, :], nmask[:, :], 1.0, -NEG, ALU.subtract, ALU.mult).then_inc(s_G5, 1)
                dve.wait_ge(s_nT, 1)
                dve.tensor_copy(newT[:, :, :, :].rearrange("n b k c -> n k b c"),
                                ps[0:NS, 5, :].rearrange("n (k b c) -> n k b c", k=NP, b=NB)).then_inc(s_newT, 1)

                def logits(u):
                    p, h, i = unit(u)
                    m, t = (i + 1) * P, Sb[u % 2]
                    dve.wait_ge(s_S, u + 1)
                    if u % QB == 0:
                        dve.wait_ge(s_nF[h], 16 * (p + 1))
                    dve.scalar_tensor_tensor(out=t[:, 0:m], in0=nF[:, h, 0:m],
                                             scalar=Ftok[:, i, 2 * p + h:2 * p + h + 1], in1=s_bank(u)[:, 0:m],
                                             op0=ALU.add, op1=ALU.add).then_inc(s_bias, 1)

                def row_max(u):
                    m = (unit(u)[2] + 1) * P
                    dve.wait_ge(s_mask, u + 1)
                    dve.tensor_reduce(nmax[:, u % 4:u % 4 + 1], Sb[u % 2][:, 0:m], AX_X, ALU.max,
                                      negate=True).then_inc(s_max, 1)

                def normalise(u):
                    p, h, i = unit(u)
                    dve.wait_ge(s_O, u + 1)
                    dve.tensor_scalar(o_tok[:, p % 2, i, h * HD:(h + 1) * HD], ps[:, 3, h * HD:(h + 1) * HD],
                                      rinv[:, u % 4:u % 4 + 1], None, ALU.mult).then_inc(s_On, 1)

                def page_rows(j):
                    bq, g = j // (NPG // 2), j % (NPG // 2)
                    dve.wait_ge(s_Slo, j + 1)
                    if g == 0 and bq >= 2:
                        dve.wait_ge(s_side, sides_before[UN * (bq - 1) + G_PTD2] + 1)
                    mm = dve.tensor_tensor(Sd[:, bq % 2, 2 * g * P:2 * (g + 1) * P], ps[0:NR, 3, P:3 * P], Slo[:, :],
                                           ALU.add)
                    if g == NPG // 2 - 1:
                        mk = nmask[:, NS - NT - NT * bq:2 * NS - NT - NT * bq]
                        mm = dve.tensor_tensor(Sd[:, bq % 2, PAST:PAST + NS], ps[0:NR, 3, 3 * P:3 * P + NS], mk, ALU.add)
                    mm.then_inc(s_rowe, 1)

                logits(0)
                row_max(0)
                for s in range(STEPS):
                    r, g, work = s // UN - 1, s % UN, side_work(s)
                    if s >= 3 and s % 2 == 1 and s <= PAGES + 1:
                        page_rows((s - 3) // 2)
                    if s + 1 < NU:
                        logits(s + 1)
                    if 2 <= s < NU + 2 and s % 2 == 0:
                        normalise(s - 2)
                    if s < PAGES:
                        for h in range(2):
                            dve.wait_ge(s_Kh, 2 * s + h + 1)
                            at = slice(4 * h, 4 * h + 4), slice(s % 2 * P, (s % 2 + 1) * P)
                            dve.tensor_tensor(KTl[:, s // 2 % 2, at[0], at[1]],
                                              ps[:, 6 + h, :].rearrange("p (c n) -> p c n", c=4),
                                              KTh[:, s // 2 % 2, at[0], at[1]].bitcast(F32), ALU.subtract).then_inc(s_Kl, 1)
                    if 2 <= s < NU + 2 and s % 2 == 1:
                        normalise(s - 2)
                    if s < NU:
                        dve.wait_ge(s_exp, s + 1)
                        dve.reciprocal(rinv[:, s % 4:s % 4 + 1], rsum[:, s % 4:s % 4 + 1])
                    if s + 1 < NU:
                        row_max(s + 1)
                    if 0 <= r < NB and g == 1:
                        dve.wait_ge(s_rowe, NPG // 2 * (r + 1))
                        dve.tensor_reduce(dstat[:, r % 2, 0:1], Sd[:, r % 2, :], AX_X, ALU.max,
                                          negate=True).then_inc(s_dmax, 1)
                    if 0 <= r < NB and g == 3:
                        dve.wait_ge(s_dexp, r + 1)
                        st = dstat[:, r % 2]
                        link(dve, dve.reciprocal(st[:, 2:3], st[:, 1:2]))
                        dve.tensor_scalar(Sd[:, r % 2, :], Sd[:, r % 2, :], st[:, 2:3], None, ALU.mult).then_inc(s_dn, 1)
                    if s % UN == 8 and s // UN + 1 < NB:
                        queries(s // UN + 1)
                    if 0 <= s + 1 - V0 < PAGES and dve_splits(s + 1 - V0):
                        V_low(dve, s + 1 - V0)
                    if work:
                        what, r, part = work
                        if what == "out":
                            dve.wait_ge(s_side, sides_before[s] + 1)
                            if r >= 2 and part == 0:
                                dve.wait_ge(s_ogd[r % 2], 16 * (r // 2))
                            c = slice(part * BANK, (part + 1) * BANK)
                            dve.tensor_tensor(ogp[:, r % 2, c], ps[:, 6, :], zT[:, r % 2, c], ALU.mult).then_inc(s_side_read, 1)
                        elif what == "probs" and part != 1:
                            dve.wait_ge(s_side_hi, 2 * r + part // 2 + 1)
                            h = 4 * part
                            dve.tensor_tensor(PTd[:, h:h + 8, NR:2 * NR], ps[:, 6, :].rearrange("p (g r) -> p g r", g=8),
                                              PTd[:, h:h + 8, 0:NR].bitcast(F32), ALU.subtract).then_inc(s_side_read, 1)
                        elif what == "sample":
                            dve.wait_ge(s_side, sides_before[s] + 1)
                            o4 = ps[:, 6, 0:NR].rearrange("p (k h t) -> p k h t", k=NP, h=2)
                            for h in range(2):
                                rows, c = slice(h * HD, (h + 1) * HD), slice(r * NT, (r + 1) * NT)
                                ins = dve.tensor_tensor(ogs[rows, :, c], o4[rows, :, h, :], z_s[rows, :, c], ALU.mult)
                            ins.then_inc(s_side_read, 1)

    stage_conditioning()
    end_stage()
    stage_pooling()
    end_stage()
    arena = Arena(y_at)
    y_tok = arena.take("y_tok", [P, TT, D])
    stage_out("b", a_out_w[0], 2, y_tok, arena, actH, actL, g_d)
    end_stage()
    arena = Arena(y_at)
    arena.at += TT * D * 4
    stage_residual(0, y_tok, arena, lambda i: x_p[:, i, :] if i < QB else x_s,
                   [(0, kvg, None), (KD, modA[:, 1], modB[:, 1])])
    end_stage()
    stage_projections()
    end_stage()
    stage_attention()
    end_stage()
    arena = Arena(y_at)
    y2 = arena.take("y2_tok", [P, TT, D])
    stage_out("d", b_out_w[0], 1, y2, arena, actH, actL, og_d)
    end_stage()
    arena = Arena(y_at)
    arena.at += TT * D * 4
    stage_residual(1, y2, arena, lambda i: x1_d[i, 0:rows_of(i)], None)
    ctx.close()


_INS = ["x_prompt", "x_sample", "state_pool", "cache_k", "cache_v", "cache_logf", "page_table", "c_prompt",
        "c_sample", "ada_w", "ada_b", "pre_g", "post_g", "a_in_w", "a_grp_w", "a_scale", "a_out_w", "kv_g",
        "kv_w", "f_b", "b_in_w", "b_out_w"]
_OUTS = [(1, SEQ, D), (NB, NT, D), (1, 1, HIST, W_A), (1, NB, HIST, W_A), (1, SEQ, NH, HD), (1, SEQ, NH, HD),
         (1, SEQ, NH), (NB, NT, NH, HD), (NB, NT, NH, HD), (NB, NT, NH)]


def kernel(**inputs):
    import numpy as _np
    import concourse.bacc as _bacc
    from concourse import mybir as _mybir
    from concourse.bass_utils import run_bass_kernel_spmd as _run

    nc = _bacc.Bacc("TRN2", target_bir_lowering=False, num_devices=1)
    arrays, args = {}, []
    for name in _INS:
        a = _np.ascontiguousarray(inputs[name])
        arrays[f"in_{name}_dram"] = a
        args.append(nc.dram_tensor(f"in_{name}_dram", a.shape, _mybir.dt.from_np(a.dtype), kind="ExternalInput").ap())
    for i, shape in enumerate(_OUTS):
        args.append(nc.dram_tensor(f"out_{i}_dram", shape, _mybir.dt.float32, kind="ExternalOutput").ap())
    build(nc, *args)
    r = _run(nc, [arrays], core_ids=[0])
    return tuple(r.results[0][f"out_{i}_dram"] for i in range(len(_OUTS)))
```
